# Optimizing a Trainium2 kernel written in Bass

```python
import math, functools
import jax, jax.numpy as jnp
from jax import lax
import numpy as np

D_MODEL = 2048
BATCH = 1
SEQ = 256
DEPTH = 1
DEC_BATCH = 8
DEC_SEQ = 4
PAST_LEN = 1024
PAGE_SIZE = 128

HEAD_DIM = 64
MIX_A = D_MODEL // 2
H_A = MIX_A // HEAD_DIM
DIL_GROUPS = ((128, 1), (512, 4), (2048, 16))
WIN_MAX = 2048
N_BUCKETS = 32
MAX_DISTANCE = 2048
MIX_B = D_MODEL - MIX_A
H_B = 4
DV_B = MIX_B // H_B
DK_B = DV_B // 2
KEY_B = H_B * DK_B
GATE_RANK = 16
GATE_TAU = 16.0
GLA_CHUNK = 16
D_FF = ((8 * D_MODEL // 3 + 255) // 256) * 256
CONV_W = 3
EPS = 1e-6
ATTN_SCALE = HEAD_DIM ** -0.5
SPLIT_SIZES = (MIX_A, MIX_A, MIX_A, KEY_B, KEY_B, MIX_B, MIX_B, GATE_RANK)
IN_COLS = sum(SPLIT_SIZES)

kernel_name = 'hybrid_dilated_gla_convffn_step'

def rmsnorm(x, g):
    xf = x.astype(jnp.float32)
    y = xf * lax.rsqrt(jnp.mean(xf * xf, axis=-1, keepdims=True) + EPS)
    return (y * g.astype(jnp.float32)).astype(x.dtype)

def t5_bucket(dist):
    exact = N_BUCKETS // 2
    df = jnp.maximum(dist, 1).astype(jnp.float32)
    large = exact + (jnp.log(df / exact) / math.log(MAX_DISTANCE / exact) * (N_BUCKETS - exact)).astype(jnp.int32)
    return jnp.where(dist < exact, dist, jnp.minimum(large, N_BUCKETS - 1))

def masked_softmax_stats(s, valid):
    s = jnp.where(valid, s, -jnp.inf)
    m = jnp.max(s, axis=-1, keepdims=True)
    p = jnp.exp(s - m)
    l = jnp.sum(p, axis=-1, keepdims=True)
    return p / l, (m + jnp.log(l))[..., 0]

def dilated_prompt(q, k, v, rel_bias, window, dil):
    B, S, H, Dh = q.shape
    n = window // dil
    L = S // dil
    NB = -(-L // n)
    Lp = NB * n
    sub = lambda t: t.reshape(B, L, dil, H, Dh)
    qb = jnp.pad(sub(q), ((0, 0), (0, Lp - L), (0, 0), (0, 0), (0, 0))).reshape(B, NB, n, dil, H, Dh)
    pad_kv = lambda t: jnp.pad(sub(t), ((0, 0), (n, Lp - L), (0, 0), (0, 0), (0, 0))).reshape(B, NB + 1, n, dil, H, Dh)
    kb, vb = pad_kv(k), pad_kv(v)
    kcat = jnp.concatenate([kb[:, :-1], kb[:, 1:]], axis=2)
    vcat = jnp.concatenate([vb[:, :-1], vb[:, 1:]], axis=2)
    iq = jnp.arange(n)[:, None]
    ik = jnp.arange(2 * n)[None, :]
    dist = n + iq - ik
    blk = jnp.arange(NB)[:, None, None]
    valid = (dist >= 0) & (dist <= n) & (blk * n + ik - n >= 0)
    bias = jnp.transpose(rel_bias[t5_bucket(jnp.clip(dist, 0, n) * dil)], (2, 0, 1)).astype(jnp.float32)
    s = jnp.einsum('bnqrhd,bnkrhd->bnrhqk', qb, kcat) * ATTN_SCALE + bias
    p, lse = masked_softmax_stats(s, valid[None, :, None, None])
    o = jnp.einsum('bnrhqk,bnkrhd->bnqrhd', p, vcat)
    o = o.reshape(B, Lp, dil, H, Dh)[:, :L].reshape(B, S, H, Dh)
    lse = jnp.transpose(lse, (0, 1, 4, 2, 3)).reshape(B, Lp, dil, H)[:, :L].reshape(B, S, H)
    return o, lse

def dilated_sample(q, k_all, v_all, rel_bias, window, dil, wbuf):
    T = q.shape[1]
    n = window // dil
    steps = jnp.arange(n + 1)
    idx = wbuf + jnp.arange(T)[:, None] - steps[None, :] * dil
    valid = idx >= 0
    idx = jnp.maximum(idx, 0)
    kg, vg = k_all[:, idx], v_all[:, idx]
    bias = rel_bias[t5_bucket(steps * dil)].T.astype(jnp.float32)
    s = jnp.einsum('bthd,btmhd->bhtm', q, kg) * ATTN_SCALE + bias[:, None, :]
    p, lse = masked_softmax_stats(s, valid[None, None])
    o = jnp.einsum('bhtm,btmhd->bthd', p, vg)
    return o, jnp.transpose(lse, (0, 2, 1))

def combine_dilations(results):
    os = jnp.stack([o for o, _ in results], axis=0)
    alpha = jax.nn.softmax(jnp.stack([l for _, l in results], axis=0), axis=0)
    return jnp.sum(alpha[..., None] * os, axis=0)

def mix_a_prompt(q, k, v, rel_bias):
    q, k, v = (t.astype(jnp.float32) for t in (q, k, v))
    return combine_dilations([dilated_prompt(q, k, v, rel_bias, w, d) for (w, d) in DIL_GROUPS])

def mix_a_sample(q, k, v, k_past, v_past, rel_bias):
    wbuf = k_past.shape[1]
    k_all = jnp.concatenate([k_past.astype(jnp.float32), k.astype(jnp.float32)], axis=1)
    v_all = jnp.concatenate([v_past.astype(jnp.float32), v.astype(jnp.float32)], axis=1)
    qf = q.astype(jnp.float32)
    return combine_dilations([dilated_sample(qf, k_all, v_all, rel_bias, w, d, wbuf) for (w, d) in DIL_GROUPS])

def gla_prompt(q, k, v, log_a, s0):
    B, S, H, K = q.shape
    C = GLA_CHUNK
    NC = S // C
    chunks = lambda t: t.astype(jnp.float32).reshape(B, NC, C, H, -1).transpose(1, 0, 3, 2, 4)
    qc, kc, vc, ac = chunks(q), chunks(k), chunks(v), chunks(log_a)
    b = jnp.cumsum(ac, axis=3)
    b_last = b[:, :, :, -1:, :]
    qe = qc * jnp.exp(b)
    ke = kc * jnp.exp(-b)
    kd = kc * jnp.exp(b_last - b)
    causal = jnp.tril(jnp.ones((C, C), dtype=bool))
    att = jnp.where(causal, jnp.einsum('nbhck,nbhsk->nbhcs', qe, ke), 0.0)
    o_intra = jnp.einsum('nbhcs,nbhsv->nbhcv', att, vc)

    def step(state, inp):
        qe_c, kd_c, v_c, dec_c = inp
        o_c = jnp.einsum('bhck,bhkv->bhcv', qe_c, state)
        state = dec_c[:, :, 0, :, None] * state + jnp.einsum('bhck,bhcv->bhkv', kd_c, v_c)
        return state, o_c

    s_fin, o_inter = lax.scan(step, s0.astype(jnp.float32), (qe, kd, vc, jnp.exp(b_last)))
    o = (o_intra + o_inter).transpose(1, 0, 3, 2, 4).reshape(B, S, H, -1)
    return o, s_fin

def gla_sample(q, k, v, log_a, s0):
    xs = tuple(t.astype(jnp.float32).transpose(1, 0, 2, 3) for t in (q, k, v, log_a))

    def step(state, inp):
        q_t, k_t, v_t, a_t = inp
        state = jnp.exp(a_t)[..., None] * state + k_t[..., :, None] * v_t[..., None, :]
        return state, jnp.einsum('bhk,bhkv->bhv', q_t, state)

    s_fin, o = lax.scan(step, s0.astype(jnp.float32), xs)
    return o.transpose(1, 0, 2, 3), s_fin

def mix_b_prompt(q, k, v, log_a):
    B = q.shape[0]
    return gla_prompt(q, k, v, log_a, jnp.zeros((B, H_B, DK_B, DV_B), jnp.float32))

def mix_b_sample(q, k, v, log_a, s0):
    return gla_sample(q, k, v, log_a, s0)

def project(h, w_in, q_norm_g, k_norm_g, w_gate2, b_gate2):
    B, T, _ = h.shape
    offs = [int(o) for o in np.cumsum(SPLIT_SIZES)[:-1]]
    qa, ka, va, qb, kb, vb, r, glr = jnp.split(h @ w_in, offs, axis=-1)
    heads_a = lambda t: t.reshape(B, T, H_A, HEAD_DIM)
    qa = rmsnorm(heads_a(qa), q_norm_g)
    ka = rmsnorm(heads_a(ka), k_norm_g)
    va = heads_a(va)
    qb = qb.reshape(B, T, H_B, DK_B) * (DK_B ** -0.5)
    kb = kb.reshape(B, T, H_B, DK_B)
    vb = vb.reshape(B, T, H_B, DV_B)
    log_a = (jax.nn.log_sigmoid((glr @ w_gate2 + b_gate2).astype(jnp.float32)) / GATE_TAU).reshape(B, T, H_B, DK_B)
    return qa, ka, va, qb, kb, vb, r, log_a

def merge_out(oa, ob, r, a_out_g, gla_out_g, w_out, dtype):
    B, T = oa.shape[:2]
    oa = rmsnorm(oa, a_out_g).reshape(B, T, MIX_A)
    ob = rmsnorm(ob, gla_out_g).reshape(B, T, MIX_B) * jax.nn.silu(r.astype(jnp.float32))
    return jnp.concatenate([oa, ob], axis=-1).astype(dtype) @ w_out

def conv_ffn(h, hist, w_up, conv_w, conv_b, w_down):
    T = h.shape[1]
    g_pre, u = jnp.split(h @ w_up, 2, axis=-1)
    gp = jnp.concatenate([hist.astype(g_pre.dtype), g_pre], axis=1)
    conv = conv_b + conv_w[0] * gp[:, 0:T]
    for i in range(1, CONV_W):
        conv = conv + conv_w[i] * gp[:, i:i + T]
    y = (jax.nn.silu(conv) * u) @ w_down
    return y, gp[:, T:]

def layer(x, c, conv_hist, mix_a, mix_b, lw):
    (norm1_g, norm2_g, w_ada, b_ada, w_in, q_norm_g, k_norm_g, w_gate2, b_gate2,
     a_out_g, gla_out_g, w_out, w_up, conv_w, conv_b, w_down) = lw
    mod = jax.nn.silu(c) @ w_ada + b_ada
    shift1, scale1, gate1, shift2, scale2, gate2 = [t[:, None, :] for t in jnp.split(mod, 6, axis=-1)]
    h = rmsnorm(x, norm1_g) * (1 + scale1) + shift1
    qa, ka, va, qb, kb, vb, r, log_a = project(h, w_in, q_norm_g, k_norm_g, w_gate2, b_gate2)
    oa = mix_a(qa, ka, va)
    ob, gla_state = mix_b(qb, kb, vb, log_a)
    x = x + gate1 * merge_out(oa, ob, r, a_out_g, gla_out_g, w_out, x.dtype)
    h2 = rmsnorm(x, norm2_g) * (1 + scale2) + shift2
    y, new_hist = conv_ffn(h2, conv_hist, w_up, conv_w, conv_b, w_down)
    x = x + gate2 * y
    return x, ka, va, gla_state, new_hist

def setup_inputs(seed: int = 0) -> dict:
    key = jax.random.key(seed)
    ks = jax.random.split(key, 25)
    nrm = lambda i, shape, scale: scale * jax.random.normal(ks[i], shape, jnp.float32)
    gain = lambda i, shape: 1.0 + nrm(i, shape, 0.05)
    wbuf = min(WIN_MAX, PAST_LEN)
    return {
        'x_prompt': nrm(0, (BATCH, SEQ, D_MODEL), 1.0),
        'x_sample': nrm(1, (DEC_BATCH, DEC_SEQ, D_MODEL), 1.0),
        'cache_k_win': nrm(2, (DEPTH, DEC_BATCH, wbuf, H_A, HEAD_DIM), 1.0),
        'cache_v_win': nrm(3, (DEPTH, DEC_BATCH, wbuf, H_A, HEAD_DIM), 1.0),
        'state_gla': nrm(4, (DEPTH, DEC_BATCH, H_B, DK_B, DV_B), 1.0),
        'state_conv': nrm(5, (DEPTH, DEC_BATCH, CONV_W - 1, D_FF), 1.0),
        'c_prompt': nrm(6, (BATCH, D_MODEL), 1.0),
        'c_sample': nrm(7, (DEC_BATCH, D_MODEL), 1.0),
        'rel_bias': nrm(8, (N_BUCKETS, H_A), 0.5),
        'norm1_g': gain(9, (DEPTH, D_MODEL)),
        'norm2_g': gain(10, (DEPTH, D_MODEL)),
        'w_ada': nrm(11, (DEPTH, D_MODEL, 6 * D_MODEL), 0.5 * D_MODEL ** -0.5),
        'b_ada': nrm(12, (DEPTH, 6 * D_MODEL), 0.02),
        'w_in': nrm(13, (DEPTH, D_MODEL, IN_COLS), D_MODEL ** -0.5),
        'q_norm_g': gain(14, (DEPTH, HEAD_DIM)),
        'k_norm_g': gain(15, (DEPTH, HEAD_DIM)),
        'w_gate2': nrm(16, (DEPTH, GATE_RANK, KEY_B), GATE_RANK ** -0.5),
        'b_gate2': nrm(17, (DEPTH, KEY_B), 0.1),
        'a_out_g': gain(18, (DEPTH, HEAD_DIM)),
        'gla_out_g': gain(19, (DEPTH, DV_B)),
        'w_out': nrm(20, (DEPTH, D_MODEL, D_MODEL), D_MODEL ** -0.5),
        'w_up': nrm(21, (DEPTH, D_MODEL, 2 * D_FF), D_MODEL ** -0.5),
        'conv_w': nrm(22, (DEPTH, CONV_W, D_FF), CONV_W ** -0.5),
        'conv_b': nrm(23, (DEPTH, D_FF), 0.02),
        'w_down': nrm(24, (DEPTH, D_FF, D_MODEL), D_FF ** -0.5),
    }

def reference(x_prompt, x_sample, cache_k_win, cache_v_win, state_gla, state_conv, c_prompt, c_sample,
              rel_bias, norm1_g, norm2_g, w_ada, b_ada, w_in, q_norm_g, k_norm_g, w_gate2, b_gate2,
              a_out_g, gla_out_g, w_out, w_up, conv_w, conv_b, w_down):
    S = x_prompt.shape[1]
    keep_p = min(WIN_MAX, S)
    xp, xs = x_prompt, x_sample
    kp_l, vp_l, gp_l, cp_l, ks_l, vs_l, gs_l, cs_l = [], [], [], [], [], [], [], []
    for l in range(DEPTH):
        lw = (norm1_g[l], norm2_g[l], w_ada[l], b_ada[l], w_in[l], q_norm_g[l], k_norm_g[l], w_gate2[l],
              b_gate2[l], a_out_g[l], gla_out_g[l], w_out[l], w_up[l], conv_w[l], conv_b[l], w_down[l])
        hist0 = jnp.zeros((xp.shape[0], CONV_W - 1, D_FF), xp.dtype)
        xp, ka, va, g_st, c_st = layer(xp, c_prompt, hist0,
                                       functools.partial(mix_a_prompt, rel_bias=rel_bias),
                                       mix_b_prompt, lw)
        kp_l.append(ka[:, S - keep_p:])
        vp_l.append(va[:, S - keep_p:])
        gp_l.append(g_st)
        cp_l.append(c_st)
        xs, ka, va, g_st, c_st = layer(xs, c_sample, state_conv[l],
                                       functools.partial(mix_a_sample, k_past=cache_k_win[l],
                                                         v_past=cache_v_win[l], rel_bias=rel_bias),
                                       functools.partial(mix_b_sample, s0=state_gla[l]), lw)
        ks_l.append(ka)
        vs_l.append(va)
        gs_l.append(g_st)
        cs_l.append(c_st)
    return (xp, xs, jnp.stack(kp_l), jnp.stack(vp_l), jnp.stack(gp_l), jnp.stack(cp_l),
            jnp.stack(ks_l), jnp.stack(vs_l), jnp.stack(gs_l), jnp.stack(cs_l))


_drawn_inputs = setup_inputs


def setup_inputs(seed=0):
    import zlib

    import numpy as np

    out = dict(_drawn_inputs(seed))
    spreads = {}
    factors = {'q_norm_g': 5.875, 'a_out_g': 5.344, 'gla_out_g': 8.0, 'conv_b': 27.297}
    for name, (base, spread) in spreads.items():
        noise = np.random.default_rng([zlib.crc32(name.encode()), seed]).standard_normal(out[name].shape)
        drawn = base * np.exp(spread * noise) if base else spread * noise
        out[name] = __import__('jax').numpy.asarray(drawn.astype(out[name].dtype))
    for name, factor in factors.items():
        out[name] = (out[name] * factor).astype(out[name].dtype)
    return out
```

```python
import math
from contextlib import ExitStack

import concourse.bass as bass
import numpy as np
from concourse import mybir

F32 = mybir.dt.float32
ACT = mybir.ActivationFunctionType
ALU = mybir.AluOpType
AX_X = mybir.AxisListType.X

P = 128
D = 2048
SEQ = 256
NB, TS = 8, 4
NS = NB * TS
TOK = SEQ + NS
PAST = 1024
H_A, HD = 16, 64
PAIRS = H_A // 2
H_B, DK, DV = 4, 128, 256
RANK = 16
D_FF = 5632
EPS = 1e-6
TAU = 16.0
KD = D // P
KF = D_FF // P
NC9 = 1 + NB
DIL = ((128, 1), (512, 4), (2048, 16))
NBUCK, MAXD = 32, 2048
NEG = -1e30

SLOTS, SLOT = 8, 11 * 256

N1, N2, BA = 0, KD, 2 * KD
CW, CB = 128, 128 + 3 * KF
QG, KG, AO, GO, BG = 304, 305, 306, 307, 309

FAR = PAST // 2 // 16 * TS
CK = FAR + PAST // 2
KT = CK // P


def bucket(dist):
    dist = np.asarray(dist)
    exact = NBUCK // 2
    df = np.maximum(dist, 1).astype(np.float32)
    large = exact + (np.log(df / exact) / math.log(MAXD / exact) * (NBUCK - exact)).astype(np.int32)
    return np.where(dist < exact, dist, np.minimum(large, NBUCK - 1))


def multiplicity(dist):
    dist = np.asarray(dist)
    n = sum(((dist >= 0) & (dist <= w) & (dist % d == 0)).astype(np.int32) for w, d in DIL)
    return np.where(n > 0, np.log(np.maximum(n, 1)), NEG).astype(np.float32)


def one_hot(dist):
    d = np.asarray(dist)
    return ((bucket(np.maximum(d, 0))[None] == np.arange(NBUCK)[:, None]) & (d[None] >= 0)).astype(np.float32)


CONST_LAYOUT = {}


def constants():
    parts = []

    def add(name, a):
        full = np.zeros((P, a.shape[1]), np.float32)
        full[:a.shape[0]] = a
        CONST_LAYOUT[name] = (sum(p.shape[1] for p in parts), a.shape[1])
        parts.append(full)

    i = np.arange(P)
    add("ident", np.eye(P, dtype=np.float32))
    add("halves", (i[:, None] // HD == i[None] // HD).astype(np.float32))
    add("ones", np.ones((P, P), np.float32))
    s, c = np.arange(P)[:, None], np.arange(SEQ)[None]
    add("causal", np.concatenate([s <= c, s + P <= c[:, P:]], 1).astype(np.float32))
    a = np.arange(NS)
    same = a[:, None] // TS == a[None] // TS
    add("causal_s", (same & (a[:, None] <= a[None])).astype(np.float32))
    add("own_batch", (a[:, None] // TS == np.arange(NB)[None]).astype(np.float32))
    dist = 2 * P - 1 - np.arange(512)
    add("hot_p", one_hot(dist))
    add("mult_p", np.tile(multiplicity(dist), (H_A, 1)))
    r = np.arange(P)
    far = 16 * (r % 32) + r // 32
    pos = np.concatenate([far, PAST // 2 + np.arange(PAST // 2)])
    t = np.arange(TS)
    add("hot_s", np.concatenate(
        [np.concatenate([one_hot(PAST + k - pos), one_hot(k - a % TS)], 1) for k in t], 0))
    old = multiplicity(PAST + t[:, None] - pos[None])[r % TS]
    new = []
    for g in range(NB // 2):
        b = 2 * g + r // 64
        m = multiplicity((r % TS)[:, None] - (a % TS)[None])
        new.append(np.where(b[:, None] == a[None] // TS, m, NEG))
    add("mult_s", np.concatenate([old] + new, 1).astype(np.float32))
    return np.concatenate(parts, 1)


class Steps:

    def __init__(self, sem, *names):
        self.sem, self.names, self.at = sem, names, 0

    def step(self, name):
        assert self.names[self.at] == name, (self.names[self.at], name)
        self.at = (self.at + 1) % len(self.names)
        return self.sem, 1

    def upto(self, name, turn=0):
        return self.sem, (turn + 1) * len(self.names) + self.names.index(name) + 1


def build(nc, a, o, bias_rows, bias_full):
    ctx = ExitStack()
    with ctx:
        def sb(name, shape):
            return ctx.enter_context(nc.sbuf_tensor(name, shape, F32))

        def sem(name):
            return ctx.enter_context(nc.semaphore(name))

        ring = sb("ring", [P, SLOTS, SLOT])
        xT = sb("xT", [P, KD, TOK])
        hT = sb("hT", [P, KD, TOK])
        proj = sb("proj", [P, 48, TOK])
        work = sb("work", [P, 2304])
        keep = CONST_LAYOUT["own_batch"][0] + NB
        con = sb("con", [P, keep])
        small = sb("small", [P, 313])
        cT = sb("cT", [P, KD, NC9])
        modT = sb("modT", [P, 6 * KD, NC9])
        glrT = sb("glrT", [RANK, TOK])
        bias_s = sb("bias_s", [P, CK + 4 * NS])
        qS = sb("qS", [P, PAIRS, NS])
        kS = sb("kS", [P, PAIRS, NS])
        vrow_s = sb("vrow_s", [NS, H_A * HD])
        mrow = sb("mrow", [NC9, 512])
        ps = ctx.enter_context(nc.psum_tensor("ps", [P, 8, 512], F32))

        def cview(name, rows=P):
            at, n = CONST_LAYOUT[name]
            return con[0:rows, at:at + n]

        ident, halves, ones = cview("ident"), cview("halves"), cview("ones")
        causal, causal_s, own_batch = cview("causal"), cview("causal_s", NS), cview("own_batch", NS)
        projf = proj[:, :, :].rearrange("p n c -> p (n c)")
        hf = hT[:, :, :].rearrange("p n c -> p (n c)")

        xr = projf[:, 0:3 * D].rearrange("p (t d) -> p t d", t=3)
        crow = projf[0:NC9, 6144:6144 + D]
        vrow = projf[:, 8192:8704].rearrange("p (t d) -> p t d", t=4)
        c0, cn = CONST_LAYOUT["hot_p"][0], CONST_LAYOUT["mult_s"]
        temp = projf[:, 8704:8704 + cn[0] + cn[1] - c0]

        def tview(name, rows):
            at, n = CONST_LAYOUT[name]
            return temp[0:rows, at - c0:at - c0 + n]

        relb = projf[:, 11300:11316]
        rel_rows = projf[:, 11328:11456]
        btab = work[0:H_A, 1024:1536]
        sq = projf[:, 11520:13824].rearrange("p (j n c) -> p j n c", j=2, n=4)
        wglr = work[:, 0:256].rearrange("p (k c) -> p k c", k=KD)
        rs = work[:, 256:544]

        sqqk = work[:, 0:576].rearrange("p (g c) -> p g c", g=2)
        rsqk = work[:, 576:1152].rearrange("p (g c) -> p g c", g=2)
        vst = work[:, 0:288]
        prob = work[:, 0:768].rearrange("p (e c) -> p e c", e=2)
        bias_p = work[:, 1152:2176].rearrange("p (j e c) -> p j e c", j=2, e=2)
        stat = work[:, 2176:2192]
        hhi = hf[:, 8 * TOK:16 * TOK]
        krows = hhi[:, 0:384].rearrange("p (t c) -> p t c", t=3)
        vrows = hhi[:, 384:768].rearrange("p (t c) -> p t c", t=3)
        probT = hhi[:, 768:1536].rearrange("p (e c) -> p e c", e=2)
        qkst = hhi[:, 1536:2112].rearrange("p (g c) -> p g c", g=2)

        qd = projf[:, 0:2048]
        kcT = projf[:, 2048:3328].rearrange("p (j c) -> p j c", j=2)
        sc = projf[:, 3328:4000]
        sT = projf[:, 4000:4768].rearrange("p (t c) -> p t c", t=6)

        s0 = projf[:, 0:4096].rearrange("p (j b v) -> p j b v", j=2, b=NB)
        zb, ex = projf[:, 4096:4384], projf[:, 4384:4672]
        cumz = projf[:, 4672:4961]
        qp = projf[:, 4962:5218]
        ki = projf[:, 5218:5730].rearrange("p (j c) -> p j c", j=2)
        attT = projf[:, 5730:6114]
        attS = projf[0:NS, 6114:6146]
        kd = projf[:, 6146:6434]
        qe, ke = projf[:, 6434:6466], projf[:, 6466:6498]
        rb = projf[:, 6498:6506]
        stp = projf[:, 6506:6762]
        dec = projf[:, 6762:6770]
        keep_g = work[:, 0:288]
        vbst = work[:, 288:864].rearrange("p (j c) -> p j c", j=2)
        vbr = work[:, 864:1632].rearrange("p (t c) -> p t c", t=3)
        kdr = work[:, 1632:2016].rearrange("p (t c) -> p t c", t=3)
        rso = work[:, 2016:2304]
        kdm = vrow_s[:, :]
        wg2 = bias_s[0:RANK, 0:512]
        wgs = bias_s[0:RANK, 512:640]
        sqo = projf[:, 5218:5794].rearrange("p (j c) -> p j c", j=2)

        actT = projf[:, 0:KF * TOK].rearrange("p (n c) -> p n c", n=KF)
        tail = projf[:, KF * TOK:48 * TOK]
        GW = 2 + SEQ + NB * 6
        gpad = work[:, 0:4 * GW].rearrange("p (n c) -> p n c", n=4)
        cv = work[:, 1224:1832].rearrange("p (n c) -> p n c", n=2)
        glast = work[:, 1832:1904].rearrange("p (n c) -> p n c", n=4)
        hrow = tail[0:16, 0:512]
        crows = tail[0:18, 512:1024]
        tmp_s = work[:, 1904:1968]

        yst = work[:, 0:1152].rearrange("p (j n c) -> p j n c", j=2, n=2)
        yrow = hf[:, 0:1536].rearrange("p (j t c) -> p j t c", j=2, t=3)

        full = [sem(f"slot_full{s}") for s in range(SLOTS)]
        used = sem("slabs_used")
        con_in, x_in, c_in, vec_in, rel_in, temp_in, wglr_in, wg2_in = (
            sem(n) for n in ("con_in", "x_in", "c_in", "vec_in", "rel_in", "temp_in", "wglr_in", "wg2_in"))
        btab_out, slant_out = sem("bias_table_out"), sem("bias_slant_out")
        biasp_in = [sem(f"bias_pair_in{j}") for j in range(2)]
        s0_in = [sem(f"state_in{j}") for j in range(2)]
        pool_turns, row_turns = sem("pool_turns"), sem("row_turns")
        k_out, v_out = sem("k_rows_out"), sem("v_rows_out")
        stp_out = sem("prompt_state_out")
        s0_out = [sem(f"state_out{j}") for j in range(2)]
        hist_in, conv_out = sem("history_in"), sem("conv_rows_out")
        y_out = [sem(f"y_rows_out{j}") for j in range(2)]

        st = lambda name, *names: Steps(sem(name), *names)
        PT_ = st("prep_tensor", "bias_p", "bias_s", "vectors", "c", *(f"x{k}" for k in range(KD)))
        PV_ = st("prep_vector", "zero_rel", "rel_rows", "bias_p", "bias_s0", "bias_s", "vectors", "c",
                 *(f"x{k}" for k in range(KD)))
        PA_ = st("prep_scalar", "silu_c")
        NT = [st(f"norm{n}_tensor", "s0", "s1", "s2", "s3") for n in (1, 2)]
        NA = [st(f"norm{n}_scalar", "q0", "q1", "q2", "q3", "ln", "rs") for n in (1, 2)]
        NV = [st(f"norm{n}_vector", "ms", "scale", "times_r", "prompt", "s_scaled", "done") for n in (1, 2)]
        AT = st("ada_tensor", "a", "b", "turn_a", "turn_b")
        AA = st("ada_scalar", "rows_a", "rows_b")
        AV = st("ada_vector", "mod")
        WT = st("in_tensor", "u0", "u1", "u2", "u3")
        WV = st("in_evac", "u0", "u1", "u2", "u3")
        GT = st("glr_tensor", "done")
        GA = st("glr_scalar", "rows", "silu_r")
        TT = st("pair_tensor", "sums", "ada_a", "kv_rows", "scores", "ada_b", "turn_a", "probT", "out", "turn_b")
        TV = st("pair_vector", "squares", "ms", "q", "k", "samples", "krows", "vrows", "vrow_s", "biased",
                "max", "recip", "norm", "mod", "out")
        TA = st("pair_scalar", "ln", "rs", "vstage", "rows_a", "exp", "rows_b", "probT")
        SU = [f"k{n}" for n in range(16)]
        ST = st("sample_tensor", *(x for n in range(16) for x in (f"k{n}", f"s{n}")), "probT", "out")
        SV = st("sample_vector", "zero", "qd", "biased", "max", "recip", "norm", "out")
        SK = st("sample_key_copies", *SU)
        SA = st("sample_scalar", "exp", "probT")
        RT = st("gla_tensor", "z", "vrows", *(f"att{i}" for i in range(8)), "kdrows", "att_s", "o", "state",
                "states", "sum")
        RV = st("gla_vector", "wgs", "z", "la", "keep", "cum", "rb", "dq", "dd", "qp", "qe", "ke", "kd", "zero_att",
                *(f"ki{i}" for i in range(8)), "att", "att_s", "kdr", "kdm", "new_state",
                "ms", "g0", "o0", "g1", "o1")
        RA = st("gla_scalar", "vstage", "abs", "exp", "ln", "vrows", "eq", "eqs", "eks", "ekd", "ekds", "dec",
                *(f"ki{i}" for i in range(8)), "sq", "stp", "lnr", "rs")
        OT = st("onorm_tensor", "sums")
        OA = st("onorm_scalar", "sq", "ln", "rs")
        OV = st("onorm_vector", "ms", "done")
        UT = st("out_tensor", "u0", "u1", "u2", "u3")
        UV = st("out_vector", *(x for n in range(4) for x in (f"s{n}", f"u{n}")))
        FT = st("up_tensor", "hist", "g0", "u0", "g1", "u1", "rows")
        FV = st("up_vector", "hist", *(x for n in range(2) for x in (f"a{n}", f"b{n}", f"conv{n}", f"act{n}")),
                "last")
        FA = st("up_scalar", "g0", "silu0", "g1", "silu1", "rows")
        FZ = st("up_first", "zero")
        DT = st("down_tensor", "u0", "u1", "t0", "t1")
        DV_ = st("down_vector", "s0", "u0", "s1", "u1")
        DA = st("down_scalar", "r0", "r1")

        N_ADA1, N_IN, N_ADA2, N_SAMP, N_OUT, N_UP, N_DOWN = 32, 48, 64, 32, 16, 88, 32
        at_in = N_ADA1
        at_ada2 = at_in + N_IN
        at_samp = at_ada2 + N_ADA2
        at_out = at_samp + N_SAMP
        at_up = at_out + N_OUT
        at_down = at_up + N_UP

        def landed(first, turns_in, per_pass=1):
            extra = 16 * 4 if first > at_samp else 0
            return first // SLOTS * 16 + extra + 16 * per_pass * (turns_in + 1)

        w_ada = a["w_ada"][0].rearrange("(k p) c -> p k c", p=P)
        w_in = a["w_in"][0].rearrange("(k p) c -> p k c", p=P)
        w_out = a["w_out"][0].rearrange("(k p) c -> p k c", p=P)
        w_up = a["w_up"][0].rearrange("(k p) c -> p k c", p=P)
        w_down = a["w_down"][0].rearrange("(k p) c -> p k c", p=P)

        def slab(s, k, c):
            return ring[:, s, 0:k * c].rearrange("p (k c) -> p k c", k=k)

        block = ctx.enter_context(nc.Block())

        @block.sync
        def _(sp):
            def ada_loads(i, wait):
                for s in range(SLOTS):
                    if wait is not None:
                        sp.wait_ge(used, wait + s + 1 - SLOTS)
                    sp.dma_start(slab(s, 4, 512), w_ada[:, 4 * (s % 4):4 * (s % 4) + 4,
                                                        bass.ds(i * 1024 + 512 * (s // 4), 512)]).then_inc(full[s], 16)

            def half_loads(w, columns, wait):
                for s in range(SLOTS):
                    sp.wait_ge(used, wait + s + 1 - SLOTS)
                    sp.dma_start(slab(s, 8, 256), w[:, 8 * (s % 2):8 * (s % 2) + 8,
                                                    bass.ds(columns[s // 2], 256)]).then_inc(full[s], 16)

            sp.dma_start(con[:, :], a["tables"][:, 0:keep]).then_inc(con_in, 16)
            sp.dma_start(crow[0:1, :], a["c_prompt"]).then_inc(c_in, 16)
            sp.dma_start(crow[1:NC9, :], a["c_sample"]).then_inc(c_in, 16)
            sp.dma_start(vrow[0:16, 0, :], a["norm1_g"].rearrange("a (n p) -> (a n) p", p=P)).then_inc(vec_in, 16)
            sp.dma_start(vrow[16:32, 0, :], a["norm2_g"].rearrange("a (n p) -> (a n) p", p=P)).then_inc(vec_in, 16)
            sp.dma_start(vrow[32:128, 0, :], a["b_ada"].rearrange("a (n p) -> (a n) p", p=P)).then_inc(vec_in, 16)
            ada_loads(0, None)
            with sp.Fori(1, N_ADA1 // SLOTS) as i:
                ada_loads(i, i * SLOTS)
            with sp.Fori(0, N_IN // SLOTS) as i:
                half_loads(w_in, [i * 1024 + 256 * u for u in range(4)], i * SLOTS + at_in)
            with sp.Fori(0, N_ADA2 // SLOTS) as i:
                ada_loads(i + 4, i * SLOTS + at_ada2)
            with sp.Fori(0, N_SAMP // SLOTS) as g:
                for s in range(SLOTS):
                    cache = a["cache_k_win" if s < 4 else "cache_v_win"][0]
                    u = s % 4
                    rows = cache[bass.ds(g * 2 + u // 2, 1), :, :, :].rearrange("a s h d -> (a s) (h d)")
                    cols = slice(512 * (u % 2), 512 * (u % 2) + 512)
                    view = slab(s, KT, 512)
                    sp.wait_ge(used, g * SLOTS + (at_samp + s + 1 - SLOTS))
                    far = rows[0:PAST // 2, cols].rearrange("(a r) c -> r a c", r=16)[0:TS]
                    sp.dma_start(view[:, 0, :], far).then_inc(full[s], 16)
                    sp.dma_start(view[:, 1:KT, :],
                                 rows[PAST // 2:PAST, cols].rearrange("(n p) c -> p n c", p=P)).then_inc(full[s], 16)
            with sp.Fori(0, N_OUT // SLOTS) as i:
                half_loads(w_out, [i * 1024 + 256 * u for u in range(4)], i * SLOTS + at_out)
            with sp.Fori(0, N_UP // SLOTS) as i:
                half_loads(w_up, [i * 512, i * 512 + D_FF, i * 512 + 256, i * 512 + D_FF + 256], i * SLOTS + at_up)
            with sp.Fori(0, N_DOWN // SLOTS) as i:
                for s in range(SLOTS):
                    sp.wait_ge(used, i * SLOTS + (at_down + s + 1 - SLOTS))
                    sp.dma_start(slab(s, 11, 256), w_down[:, 11 * (s % 4):11 * (s % 4) + 11,
                                                          bass.ds(i * 512 + 256 * (s // 4), 256)]).then_inc(full[s], 16)

        @block.gpsimd
        def _(pool):
            pool.wait_ge(*PV_.upto("bias_p"))
            pool.dma_start(bias_rows[:, :], btab).then_inc(btab_out, 16)
            pool.wait_ge(btab_out, 16)
            slant = bass.AP(bias_rows[:, :].tensor, P - 1, [[512, H_A], [-1, P], [1, SEQ]])
            pool.dma_start(bias_full[:, :, :], slant).then_inc(slant_out, 16)
            pool.wait_ge(slant_out, 16)
            by_head = bias_full[:, :, :].rearrange("h p c -> p h c")
            pool.wait_ge(*GT.upto("done"))
            with pool.Fori(0, PAIRS // 2) as i:
                for j in range(2):
                    p = i * 2 + j
                    pool.wait_ge(*TV.upto("biased", p - 1))
                    pool.sem_inc(pool_turns, 1)
                    pool.dma_start(bias_p[:, j], by_head[:, bass.ds(p * 2, 2), :]).then_inc(biasp_in[j], 16)
                    pool.wait_ge(*TV.upto("krows", p))
                    pool.sem_inc(pool_turns, 1)
                    cols = bass.ds(p * P, P)
                    ko = o["new_k_p"].rearrange("(t s) c -> s t c", s=P)
                    vo = o["new_v_p"].rearrange("(t s) c -> s t c", s=P)
                    pool.dma_start(ko[:, :, cols], krows[:, 0:2, :]).then_inc(k_out, 16)
                    pool.dma_start(o["new_k_s"][:, cols], krows[0:NS, 2, :]).then_inc(k_out, 16)
                    pool.wait_ge(*TV.upto("vrows", p))
                    pool.sem_inc(pool_turns, 1)
                    pool.dma_start(vo[:, :, cols], vrows[:, 0:2, :]).then_inc(v_out, 16)
                    pool.dma_start(o["new_v_s"][:, cols], vrows[0:NS, 2, :]).then_inc(v_out, 16)
            pool.wait_ge(*ST.upto("out", 3))
            pool.wait_ge(*SV.upto("out", 3))
            pool.dma_start(wg2, a["w_gate2"][0]).then_inc(wg2_in, 16)
            s_in = a["state_gla"][0].rearrange("b h k v -> k h b v")
            s_out = o["new_gla_s"].rearrange("b h k v -> k h b v")
            pool.dma_start(s0[:, 0], s_in[:, 0]).then_inc(s0_in[0], 16)
            pool.dma_start(s0[:, 1], s_in[:, 1]).then_inc(s0_in[1], 16)
            with pool.Fori(0, 2) as i:
                for j in range(2):
                    h = i * 2 + j
                    pool.wait_ge(*RA.upto("stp", h))
                    pool.sem_inc(pool_turns, 1)
                    pool.dma_start(o["new_gla_p"][bass.ds(h, 1)].rearrange("a k v -> (a k) v"),
                                   stp).then_inc(stp_out, 16)
                    pool.wait_ge(*RV.upto("new_state", h))
                    pool.sem_inc(pool_turns, 1)
                    pool.dma_start(s_out[:, bass.ds(h, 1)].rearrange("k a b v -> k (a b) v"),
                                   s0[:, j]).then_inc(s0_out[j], 16)
                    with pool.If(i < 1):
                        pool.wait_ge(s0_out[j], 16)
                        pool.sem_inc(pool_turns, 1)
                        pool.dma_start(s0[:, j], s_in[:, 2 + j]).then_inc(s0_in[j], 16)
                    with pool.Else():
                        pool.wait_ge(s0_out[j], 16)
            pool.wait_ge(*NV[1].upto("done"))
            pool.wait_ge(s0_out[0], 32)
            pool.wait_ge(s0_out[1], 32)
            pool.wait_ge(stp_out, 64)
            hist = a["state_conv"][0].rearrange("b r c -> (b r) c")
            with pool.Fori(0, 11) as i:
                pool.wait_ge(*FT.upto("hist", i - 1))
                pool.sem_inc(pool_turns, 1)
                pool.dma_start(hrow, hist[:, bass.ds(i * 512, 512)]).then_inc(hist_in, 16)
                pool.wait_ge(*FA.upto("rows", i))
                pool.sem_inc(pool_turns, 1)
                pool.dma_start(o["new_conv_p"][:, bass.ds(i * 512, 512)], crows[0:2]).then_inc(conv_out, 16)
                pool.dma_start(o["new_conv_s"][:, bass.ds(i * 512, 512)], crows[2:18]).then_inc(conv_out, 16)
            yp = o["y_p"].rearrange("(t s) c -> s t c", s=P)
            with pool.Fori(0, 4) as i:
                for j in range(2):
                    pool.wait_ge(*DA.upto(f"r{j}", i))
                    pool.sem_inc(pool_turns, 1)
                    cols = bass.ds(i * 512 + 256 * j, 256)
                    pool.dma_start(yp[:, :, cols], yrow[:, j, 0:2, :]).then_inc(y_out[j], 16)
                    pool.dma_start(o["y_s"][:, cols], yrow[0:NS, j, 2, :]).then_inc(y_out[j], 16)
            for s, n in ((y_out[0], 128), (y_out[1], 128), (conv_out, 352), (k_out, 256), (v_out, 256), (stp_out, 64),
                         (s0_out[0], 32), (s0_out[1], 32)):
                pool.wait_ge(s, n)

        @block.tensor
        def _(pe):
            mm, turn = nc.tensor.matmul, nc.tensor.transpose
            for s_ in (PT_, *NT, AT, WT, GT, TT, ST, RT, OT, UT, FT, DT):
                pe.sem_inc(s_.sem, len(s_.names))

            pe.wait_ge(con_in, 16)
            pe.wait_ge(temp_in, 16)
            pe.wait_ge(rel_in, 64)
            mm(ps[0:H_A, 0, :], relb[0:NBUCK, :], tview("hot_p", NBUCK), start=True,
               stop=True).then_inc(*PT_.step("bias_p"))
            pe.wait_ge(*PV_.upto("rel_rows"))
            mm(ps[:, 1, :], rel_rows, tview("hot_s", P)[:, 0:512], start=True, stop=True)
            mm(ps[:, 2, 0:160], rel_rows, tview("hot_s", P)[:, 512:672], start=True,
               stop=True).then_inc(*PT_.step("bias_s"))
            pe.wait_ge(vec_in, 16 * 15)
            for t, (n, c) in enumerate(((128, 0), (88, 128), (88, 216), (9, 304))):
                last = turn(ps[:, 3, c:c + n], vrow[0:n, t, :], ident[0:n, 0:n])
            last.then_inc(*PT_.step("vectors"))
            pe.wait_ge(*PA_.upto("silu_c"))
            for k in range(KD):
                last = turn(ps[:, 4, NC9 * k:NC9 * k + NC9], crow[:, P * k:P * k + P], ident[0:NC9, 0:NC9])
            last.then_inc(*PT_.step("c"))
            pe.wait_ge(x_in, 32)
            for k in range(KD):
                if k >= 3:
                    pe.wait_ge(*PV_.upto(f"x{k - 3}"))
                for t in range(3):
                    n = P if t < 2 else NS
                    last = turn(ps[:, 5 + k % 3, P * t:P * t + n], xr[0:n, t, P * k:P * k + P], ident[0:n, 0:n])
                last.then_inc(*PT_.step(f"x{k}"))

            def norm_sums(n, bank):
                for j in range(4):
                    pe.wait_ge(*NA[n].upto(f"q{j}"))
                    for k in range(4):
                        last = mm(ps[:, bank, 0:TOK], ones, sq[:, j % 2, k, :], start=(j + k == 0),
                                  stop=(j == 3 and k == 3))
                    last.then_inc(*NT[n].step(f"s{j}"))

            def ada_slabs(bank, slots, pass_of):
                for s in slots:
                    pe.wait_ge(full[s], pass_of)
                    for k in range(4):
                        kk = 4 * (s % 4) + k
                        last = mm(ps[0:NC9, bank, :], cT[:, kk, :], slab(s, 4, 512)[:, k, :], start=(kk == 0),
                                  stop=(kk == KD - 1))
                    if s != slots[-1]:
                        last.then_inc(used, 1)
                return last

            def ada_turn(bank):
                pe.sem_inc(row_turns, 1)
                for n in range(4):
                    last = turn(ps[:, bank, NC9 * n:NC9 * n + NC9], mrow[:, P * n:P * n + P], ident[0:NC9, 0:NC9])
                return last

            norm_sums(0, 4)
            pe.wait_ge(*PV_.upto("c"))
            with pe.Fori(0, N_ADA1 // SLOTS) as i:
                for n, name in enumerate("ab"):
                    pe.wait_ge(*AA.upto(f"rows_{name}", i - 1))
                    ada_slabs(n, range(4 * n, 4 * n + 4), i * 16 + 16).then_inc(*AT.step(name))
                    pe.wait_ge(*AT.upto(name, i))
                    pe.sem_inc(used, 1)
                pe.wait_ge(*AA.upto("rows_a", i))
                pe.wait_ge(*AV.upto("mod", i - 1))
                ada_turn(2).then_inc(*AT.step("turn_a"))
                pe.wait_ge(*AA.upto("rows_b", i))
                ada_turn(3).then_inc(*AT.step("turn_b"))

            def unit(bank, s, kk, nk, width, rhs, pass_of, first, last_of):
                pe.wait_ge(full[s], pass_of)
                w = slab(s, nk, width)
                for k in range(nk):
                    for n in range(2):
                        last = mm(ps[:, bank + n, 0:TOK], w[:, k, P * n:P * n + P], rhs[:, kk + k, :],
                                  start=(first and k == 0), stop=(last_of and k == nk - 1))
                return last

            def two_slabs(bank, u, rhs, pass_of, step):
                unit(bank, 2 * u, 0, 8, 256, rhs, pass_of, True, False).then_inc(used, 1)
                unit(bank, 2 * u + 1, 8, 8, 256, rhs, pass_of, False, True).then_inc(used, 1)

            pe.wait_ge(*NV[0].upto("done"))
            with pe.Fori(0, N_IN // SLOTS) as i:
                for u in range(4):
                    b = 2 * (u % 2)
                    if u >= 2:
                        pe.wait_ge(*WV.upto(f"u{u - 2}", i))
                    else:
                        pe.wait_ge(*WV.upto(f"u{u + 2}", i - 1))
                    unit(b, 2 * u, 0, 8, 256, hT, landed(at_in, i), True, False).then_inc(used, 1)
                    unit(b, 2 * u + 1, 8, 8, 256, hT, landed(at_in, i), False, True).then_inc(*WT.step(f"u{u}"))
                    pe.wait_ge(*WT.upto(f"u{u}", i))
                    pe.sem_inc(used, 1)
            pe.wait_ge(wglr_in, 16)
            for k in range(KD):
                last = mm(ps[0:RANK, 4, 0:TOK], wglr[:, k, :], hT[:, k, :], start=(k == 0), stop=(k == KD - 1))
            last.then_inc(*GT.step("done"))

            pe.wait_ge(*WV.upto("u3", 5))
            pe.wait_ge(*GA.upto("rows"))
            with pe.Fori(0, PAIRS) as p:
                pe.wait_ge(*TV.upto("squares", p))
                pe.wait_ge(*TV.upto("out", p - 1))
                for g in range(2):
                    last = mm(ps[:, 4 + g, 0:TOK], halves, sqqk[:, g, :], start=True, stop=True)
                last.then_inc(*TT.step("sums"))
                pe.wait_ge(*TA.upto("rows_a", p - 1))
                ada_slabs(0, range(0, 4), landed(at_ada2, p)).then_inc(*TT.step("ada_a"))
                pe.wait_ge(*TT.upto("ada_a", p))
                pe.sem_inc(used, 1)
                pe.wait_ge(*TV.upto("k", p))
                pe.wait_ge(*TA.upto("vstage", p))
                pe.wait_ge(*TA.upto("probT", p - 1))
                for g, src in enumerate((qkst[:, 1, :], vst)):
                    for t in range(3):
                        n = P if t < 2 else NS
                        last = turn(ps[0:n, 6 + g, P * t:P * t + P], src[:, P * t:P * t + n], ident)
                last.then_inc(*TT.step("kv_rows"))
                for e in range(2):
                    h = slice(HD * e, HD * e + HD)
                    for qt in range(2):
                        last = mm(ps[:, 4 + e, P * qt:P * qt + P * (qt + 1)], qkst[h, 0, P * qt:P * qt + P],
                                  qkst[h, 1, 0:P * (qt + 1)], start=True, stop=True)
                last.then_inc(*TT.step("scores"))
                pe.wait_ge(*TA.upto("rows_b", p - 1))
                ada_slabs(1, range(4, 8), landed(at_ada2, p)).then_inc(*TT.step("ada_b"))
                pe.wait_ge(*TT.upto("ada_b", p))
                pe.sem_inc(used, 1)
                pe.wait_ge(*TA.upto("rows_a", p))
                pe.wait_ge(*TV.upto("mod", p - 1))
                ada_turn(2).then_inc(*TT.step("turn_a"))
                pe.wait_ge(*TV.upto("norm", p))
                for e in range(2):
                    for n in range(3):
                        last = turn(ps[:, 6 + e, P * n:P * n + P], prob[:, e, P * n:P * n + P], ident)
                last.then_inc(*TT.step("probT"))
                pe.wait_ge(*TA.upto("probT", p))
                for e in range(2):
                    mm(ps[:, 4 + e, 0:SEQ], vrows[:, 0, :], probT[:, e, 0:SEQ], start=True, stop=False)
                    last = mm(ps[:, 4 + e, P:SEQ], vrows[:, 1, :], probT[:, e, SEQ:3 * P], start=False, stop=True)
                last.then_inc(*TT.step("out"))
                pe.wait_ge(*TA.upto("rows_b", p))
                ada_turn(3).then_inc(*TT.step("turn_b"))

            pe.wait_ge(*TV.upto("mod", PAIRS - 1))
            pe.wait_ge(*TV.upto("out", PAIRS - 1))
            with pe.Fori(0, NB // 2) as g:
                pe.wait_ge(*SV.upto("qd", g))
                def key_turns(n):
                    u, j = n // 4, n % 4
                    if j == 0:
                        pe.wait_ge(full[u], g * 32 + (at_samp // SLOTS * 16 + 32))
                    if n >= 2:
                        pe.wait_ge(*SK.upto(f"k{n - 2}", g))
                    elif n == 0:
                        pe.wait_ge(*SA.upto("probT", g - 1))
                    for t in range(KT):
                        last = turn(ps[:, 2 * (n % 2) + t // 4, P * (t % 4):P * (t % 4) + P],
                                    slab(u, KT, 512)[:, t, P * j:P * j + P], ident)
                    last.then_inc(*ST.step(f"k{n}"))
                    if j == 3:
                        pe.wait_ge(*ST.upto(f"k{n}", g))
                        pe.sem_inc(used, 1)

                def scores(n):
                    u, j = n // 4, n % 4
                    if n == 0:
                        pe.wait_ge(*SV.upto("biased", g - 1))
                    pe.wait_ge(*SK.upto(f"k{n}", g))
                    q = qd[:, P * n:P * n + P]
                    f, l = n == 0, n == 15
                    mm(ps[:, 4, :], q, kcT[:, n % 2, 0:512], start=f, stop=l)
                    mm(ps[:, 5, 0:P], q, kcT[:, n % 2, 512:CK], start=f, stop=l)
                    mm(ps[:, 6, 0:NS], q, kS[:, 4 * (u % 2) + j, :], start=f, stop=l).then_inc(*ST.step(f"s{n}"))

                for n in range(16):
                    key_turns(n)
                    scores(n)
                pe.wait_ge(*SV.upto("norm", g))
                for t in range(KT):
                    turn(ps[:, t // 4, P * (t % 4):P * (t % 4) + P], sc[:, P * t:P * t + P], ident)
                turn(ps[0:NS, 2, 0:P], sc[:, CK:CK + NS], ident).then_inc(*ST.step("probT"))
                pe.wait_ge(*SA.upto("probT", g))
                pe.wait_ge(*SV.upto("out", g - 1))
                for n in range(16):
                    u, j = n // 4, n % 4
                    if j == 0:
                        pe.wait_ge(full[4 + u], g * 32 + (at_samp // SLOTS * 16 + 32))
                    out = ps[:, 7, 8 * n:8 * n + 8]
                    rows = slice(8 * n, 8 * n + 8)
                    for t in range(KT):
                        last = mm(out, slab(4 + u, KT, 512)[:, t, P * j:P * j + P], sT[:, t, rows], start=(t == 0),
                                  stop=False)
                    pair = 4 * (u % 2) + j
                    if j == 3 and n < 15:
                        mm(out, vrow_s[:, P * pair:P * pair + P], sT[0:NS, KT, rows], start=False,
                           stop=True).then_inc(used, 1)
                    else:
                        last = mm(out, vrow_s[:, P * pair:P * pair + P], sT[0:NS, KT, rows], start=False, stop=True)
                last.then_inc(*ST.step("out"))
                pe.wait_ge(*ST.upto("out", g))
                pe.sem_inc(used, 1)

            with pe.Fori(0, 2) as i:
                for half in range(2):
                    h = i * 2 + half
                    pe.wait_ge(*RV.upto("wgs", h))
                    pe.wait_ge(*RV.upto("o1", h - 1))
                    mm(ps[:, 0, 0:TOK], wgs, glrT[:, :], start=True, stop=True).then_inc(*RT.step("z"))
                    pe.wait_ge(*RA.upto("vstage", h))
                    for t in range(3):
                        n = P if t < 2 else NS
                        for v in range(2):
                            last = turn(ps[0:n, 1 + t // 2, 256 * (t % 2) + P * v:256 * (t % 2) + P * v + P],
                                        vbst[:, v, P * t:P * t + n], ident)
                    last.then_inc(*RT.step("vrows"))
                    for c in range(8):
                        pe.wait_ge(*RV.upto(f"ki{c}", h))
                        q = qp[:, 32 * c:32 * c + 32]
                        n = min(P, 32 * (c + 1))
                        last = mm(ps[0:n, 3, 32 * c:32 * c + 32], ki[:, c % 2, 0:n], q, start=True, stop=True)
                        if c >= 4:
                            n = 32 * (c - 3)
                            last = mm(ps[0:n, 3, P + 32 * c:P + 32 * c + 32], ki[:, c % 2, P:P + n], q, start=True,
                                      stop=True)
                        last.then_inc(*RT.step(f"att{c}"))
                    pe.wait_ge(*RV.upto("kd", h))
                    for t in range(3):
                        n = P if t < 2 else NS
                        last = turn(ps[0:n, 6, P * t:P * t + P], kd[:, P * t:P * t + n], ident)
                    last.then_inc(*RT.step("kdrows"))
                    mm(ps[0:NS, 7, 0:NS], ke, qe, start=True, stop=True).then_inc(*RT.step("att_s"))
                    pe.wait_ge(*RV.upto("att_s", h))
                    pe.wait_ge(*RA.upto("vrows", h))
                    pe.wait_ge(s0_in[half], i * 16 + 16)
                    for v in range(2):
                        c = slice(P * v, P * v + P)
                        mm(ps[:, 4 + v, 0:SEQ], vbr[:, 0, c], attT[:, 0:SEQ], start=True, stop=False)
                        mm(ps[:, 4 + v, P:SEQ], vbr[:, 1, c], attT[:, SEQ:3 * P], start=False, stop=True)
                        for b in range(NB):
                            mm(ps[:, 4 + v, SEQ + TS * b:SEQ + TS * b + TS], s0[:, half, b, c],
                               qe[:, TS * b:TS * b + TS], start=(b == 0), stop=False)
                        last = mm(ps[:, 4 + v, SEQ:TOK], vbr[0:NS, 2, c], attS, start=False, stop=True)
                    last.then_inc(*RT.step("o"))
                    pe.wait_ge(*RV.upto("kdm", h))
                    mm(ps[:, 0, 0:DV], kdr[:, 0, :], vbr[:, 0, :], start=True, stop=False)
                    mm(ps[:, 0, 0:DV], kdr[:, 1, :], vbr[:, 1, :], start=False, stop=True).then_inc(*RT.step("state"))
                    for b in range(NB):
                        bank = (1, 2, 6, 7)[b // 2]
                        last = mm(ps[:, bank, DV * (b % 2):DV * (b % 2) + DV], kdm[:, P * b:P * b + P],
                                  vbr[0:NS, 2, :], start=True, stop=True)
                    last.then_inc(*RT.step("states"))
                    pe.wait_ge(*RA.upto("sq", h))
                    for v in range(2):
                        last = mm(ps[:, 3, 0:TOK], ones, sqo[:, v, :], start=(v == 0), stop=(v == 1))
                    last.then_inc(*RT.step("sum"))

            pe.wait_ge(*OA.upto("sq"))
            pe.wait_ge(*RV.upto("o1", 3))
            for n in range(PAIRS):
                last = mm(ps[:, n, 0:TOK], halves, projf[:, TOK * n:TOK * n + TOK], start=True, stop=True)
            last.then_inc(*OT.step("sums"))

            pe.wait_ge(*OV.upto("done"))
            with pe.Fori(0, 2) as i:
                for u in range(4):
                    b = 2 * (u % 2)
                    if u >= 2:
                        pe.wait_ge(*UV.upto(f"u{u - 2}", i))
                    else:
                        pe.wait_ge(*UV.upto(f"u{u + 2}", i - 1))
                    unit(b, 2 * u, 0, 8, 256, hT, landed(at_out, i), True, False).then_inc(used, 1)
                    unit(b, 2 * u + 1, 8, 8, 256, hT, landed(at_out, i), False, True).then_inc(*UT.step(f"u{u}"))
                    pe.wait_ge(*UT.upto(f"u{u}", i))
                    pe.sem_inc(used, 1)
            norm_sums(1, 4)

            pe.wait_ge(*NV[1].upto("done"))
            with pe.Fori(0, 11) as i:
                pe.wait_ge(hist_in, i * 16 + 16)
                pe.wait_ge(*FV.upto("hist", i - 1))
                pe.sem_inc(row_turns, 1)
                for n in range(4):
                    last = turn(ps[:, 4, 16 * n:16 * n + 16], hrow[:, P * n:P * n + P], ident[0:16, 0:16])
                last.then_inc(*FT.step("hist"))
                for n in range(2):
                    for w, b in (("g", 0), ("u", 2)):
                        s = 4 * n + b
                        if w == "g":
                            pe.wait_ge(*FA.upto(f"g{1 - n}", i - 1 + n))
                        else:
                            pe.wait_ge(*FV.upto(f"act{1 - n}", i - 1 + n))
                        unit(b, s, 0, 8, 256, hT, landed(at_up, i), True, False).then_inc(used, 1)
                        unit(b, s + 1, 8, 8, 256, hT, landed(at_up, i), False, True).then_inc(*FT.step(f"{w}{n}"))
                        pe.wait_ge(*FT.upto(f"{w}{n}", i))
                        pe.sem_inc(used, 1)
                pe.wait_ge(*FV.upto("last", i))
                pe.wait_ge(*FA.upto("rows", i - 1))
                for n in range(4):
                    last = turn(ps[0:18, 5, P * n:P * n + P], glast[:, n, :], ident)
                last.then_inc(*FT.step("rows"))

            pe.wait_ge(*FV.upto("act1", 10))
            pe.wait_ge(*FA.upto("rows", 10))
            with pe.Fori(0, 4) as i:
                for n in range(2):
                    pe.wait_ge(*DV_.upto(f"u{n}", i - 1))
                    for s in range(4):
                        m = unit(2 * n, 4 * n + s, 11 * s, 11, 256, actT, landed(at_down, i), s == 0, s == 3)
                        if s < 3:
                            m.then_inc(used, 1)
                    m.then_inc(*DT.step(f"u{n}"))
                    pe.wait_ge(*DT.upto(f"u{n}", i))
                    pe.sem_inc(used, 1)
                for n in range(2):
                    pe.wait_ge(*DV_.upto(f"u{n}", i))
                    pe.wait_ge(*DA.upto(f"r{n}", i - 1))
                    for t in range(3):
                        m = P if t < 2 else NS
                        for b in range(2):
                            last = turn(ps[0:m, 4 + 2 * n + t // 2, 256 * (t % 2) + P * b:256 * (t % 2) + P * b + P],
                                        yst[:, n, b, P * t:P * t + m], ident)
                    last.then_inc(*DT.step(f"t{n}"))

        @block.scalar
        def _(act):
            f = nc.scalar.activation
            for s_ in (PA_, *NA, AA, GA, TA, SA, RA, OA, FA, DA):
                act.sem_inc(s_.sem, len(s_.names))
            act.dma_start(xr[:, 0:2, :], a["x_prompt"][0].rearrange("(t p) d -> p t d", p=P)).then_inc(x_in, 16)
            act.dma_start(xr[0:NS, 2, :], a["x_sample"].rearrange("b t d -> (b t) d")).then_inc(x_in, 16)
            act.dma_start(temp, a["tables"][:, c0:cn[0] + cn[1]]).then_inc(temp_in, 16)
            for t in range(4):
                act.dma_start(relb[32 * t:32 * t + 32, :], a["rel_bias"]).then_inc(rel_in, 16)
            for j, (dst, src) in enumerate([
                    (vrow[0:44, 1, :], a["conv_w"][0, 0:1, :]), (vrow[44:88, 1, :], a["conv_w"][0, 1:2, :]),
                    (vrow[0:44, 2, :], a["conv_w"][0, 2:3, :]), (vrow[44:88, 2, :], a["conv_b"]),
                    (vrow[3:5, 3, :], a["gla_out_g"]), (vrow[5:9, 3, :], a["b_gate2"])]):
                act.dma_start(dst, src.rearrange("a (n p) -> (a n) p", p=P)).then_inc(vec_in, 16)
            for j, name in enumerate(("q_norm_g", "k_norm_g", "a_out_g")):
                for e in range(2):
                    act.dma_start(vrow[j:j + 1, 3, HD * e:HD * e + HD], a[name]).then_inc(vec_in, 16)
            act.dma_start(wglr, w_in[:, :, 6144:6160]).then_inc(wglr_in, 16)
            act.wait_ge(c_in, 32)
            f(crow, crow, ACT.Silu).then_inc(*PA_.step("silu_c"))

            def norm_squares(n):
                for j in range(4):
                    if n == 0:
                        act.wait_ge(*PV_.upto(f"x{4 * j + 3}"))
                    if j >= 2:
                        act.wait_ge(*NT[n].upto(f"s{j - 2}"))
                    f(sq[:, j % 2], xT[:, 4 * j:4 * j + 4, :], ACT.Square).then_inc(*NA[n].step(f"q{j}"))
                act.wait_ge(*NV[n].upto("ms"))
                f(rs, rs, ACT.Ln).then_inc(*NA[n].step("ln"))
                act.wait_ge(*NA[n].upto("ln"))
                f(rs, rs, ACT.Exp, scale=-0.5).then_inc(*NA[n].step("rs"))

            norm_squares(0)
            with act.Fori(0, N_ADA1 // SLOTS) as i:
                for n, name in enumerate("ab"):
                    act.wait_ge(*AT.upto(name, i))
                    act.wait_ge(*AT.upto("turn_a" if n else "turn_b", i - 1 + n))
                    f(mrow[:, :], ps[0:NC9, n, :], ACT.Copy).then_inc(*AA.step(f"rows_{name}"))
            with act.Fori(0, N_IN // SLOTS) as i:
                for u in (0, 2):
                    act.wait_ge(*WT.upto(f"u{u}", i))
                    if u:
                        act.wait_ge(*WV.upto("u1", i))
                    else:
                        act.wait_ge(*WV.upto("u3", i - 1))
                    f(proj[:, bass.ds(i * 8 + 2 * u, 2), :], ps[:, 0:2, 0:TOK], ACT.Copy).then_inc(WV.sem, 1)
            act.wait_ge(*GT.upto("done"))
            f(glrT[:, :], ps[0:RANK, 4, 0:TOK], ACT.Copy).then_inc(*GA.step("rows"))
            act.wait_ge(*WV.upto("u3", 5))
            f(proj[:, 40:48, :], proj[:, 40:48, :], ACT.Silu).then_inc(*GA.step("silu_r"))

            with act.Fori(0, PAIRS) as p:
                act.wait_ge(*TV.upto("ms", p))
                f(rsqk, rsqk, ACT.Ln).then_inc(*TA.step("ln"))
                act.wait_ge(*TA.upto("ln", p))
                f(rsqk, rsqk, ACT.Exp, scale=-0.5).then_inc(*TA.step("rs"))
                f(vst, proj[:, bass.ds(p + 16, 1), :].rearrange("p a c -> p (a c)"),
                  ACT.Copy).then_inc(*TA.step("vstage"))
                act.wait_ge(*TT.upto("ada_a", p))
                act.wait_ge(*TT.upto("turn_b", p - 1))
                f(mrow[:, :], ps[0:NC9, 0, :], ACT.Copy).then_inc(*TA.step("rows_a"))
                act.wait_ge(*TV.upto("max", p))
                for e in range(2):
                    for q in range(2):
                        part = prob[:, e, P * q:P * q + P * (q + 1)]
                        c = 2 * e + q
                        last = f(part, part, ACT.Exp, bias=stat[:, c:c + 1], accum_out=stat[:, 4 + c:5 + c])
                last.then_inc(*TA.step("exp"))
                act.wait_ge(*TT.upto("ada_b", p))
                act.wait_ge(*TT.upto("turn_a", p))
                f(mrow[:, :], ps[0:NC9, 1, :], ACT.Copy).then_inc(*TA.step("rows_b"))
                act.wait_ge(*TT.upto("probT", p))
                act.wait_ge(*TT.upto("out", p - 1))
                f(probT, ps[:, 6:8, 0:384], ACT.Copy).then_inc(*TA.step("probT"))

            with act.Fori(0, NB // 2) as g:
                for n in range(0, 16, 2):
                    act.wait_ge(*ST.upto(f"k{n}", g))
                    if n >= 2:
                        act.wait_ge(*ST.upto(f"s{n - 2}", g))
                    act.wait_ge(*SK.upto(f"k{n - 1 if n else 15}", g if n else g - 1))
                    f(kcT[:, 0, 0:512], ps[:, 0, :], ACT.Copy)
                    f(kcT[:, 0, 512:CK], ps[:, 1, 0:P], ACT.Copy).then_inc(SK.sem, 1)
                act.wait_ge(*SV.upto("max", g))
                f(sc, sc, ACT.Exp, bias=stat[:, 0:1], accum_out=stat[:, 1:2]).then_inc(*SA.step("exp"))
                act.wait_ge(*ST.upto("probT", g))
                act.wait_ge(*ST.upto("out", g - 1))
                f(sT[:, 0:4, :].rearrange("p t c -> p (t c)"), ps[:, 0, :], ACT.Copy)
                f(sT[:, 4, :], ps[:, 1, 0:P], ACT.Copy)
                f(sT[0:NS, 5, :], ps[0:NS, 2, 0:P], ACT.Copy).then_inc(*SA.step("probT"))

            act.wait_ge(*ST.upto("out", 3))
            with act.Fori(0, 2) as i:
                for half in range(2):
                    h = i * 2 + half
                    cum, cums = cumz[:, 1:1 + SEQ], cumz[:, 1 + SEQ:1 + TOK]
                    act.wait_ge(*RT.upto("vrows", h - 1))
                    f(vbst, proj[:, bass.ds(h * 2 + 32, 2), :], ACT.Copy).then_inc(*RA.step("vstage"))
                    act.wait_ge(*RV.upto("z", h))
                    act.wait_ge(*RV.upto("o1", h - 1))
                    f(ex, zb, ACT.Abs).then_inc(*RA.step("abs"))
                    act.wait_ge(*RA.upto("abs", h))
                    f(ex, ex, ACT.Exp, scale=-1.0).then_inc(*RA.step("exp"))
                    act.wait_ge(*RA.upto("exp", h))
                    f(ex, ex, ACT.Ln, bias=1.0).then_inc(*RA.step("ln"))
                    act.wait_ge(*RT.upto("vrows", h))
                    act.wait_ge(*RT.upto("states", h - 1))
                    f(vbr[:, 0:2, :].rearrange("p t c -> p (t c)"), ps[:, 1, :], ACT.Copy)
                    f(vbr[0:NS, 2, :], ps[0:NS, 2, 0:256], ACT.Copy).then_inc(*RA.step("vrows"))
                    act.wait_ge(*RV.upto("dd", h))
                    f(qp, qp, ACT.Exp, scale=1 / TAU).then_inc(*RA.step("eq"))
                    f(qe, cums, ACT.Exp, scale=1 / TAU).then_inc(*RA.step("eqs"))
                    f(ke, cums, ACT.Exp, scale=-1 / TAU).then_inc(*RA.step("eks"))
                    f(kd[:, 0:SEQ], cum, ACT.Exp, scale=-1 / TAU, bias=rb[:, 0:1]).then_inc(*RA.step("ekd"))
                    f(kd[:, SEQ:TOK], kd[:, SEQ:TOK], ACT.Exp, scale=1 / TAU).then_inc(*RA.step("ekds"))
                    f(dec, cums.rearrange("p (b t) -> p b t", t=TS)[:, :, TS - 1], ACT.Exp,
                      scale=1 / TAU).then_inc(*RA.step("dec"))
                    for c in range(8):
                        if c >= 2:
                            act.wait_ge(*RT.upto(f"att{c - 2}", h))
                        n = 32 * (c + 1)
                        f(ki[:, c % 2, 0:n], cum[:, 0:n], ACT.Exp, scale=-1 / TAU,
                          bias=keep_g[:, c:c + 1]).then_inc(*RA.step(f"ki{c}"))
                    act.wait_ge(*RT.upto("o", h))
                    for v in range(2):
                        last = f(sqo[:, v, :], ps[:, 4 + v, 0:TOK], ACT.Square)
                    last.then_inc(*RA.step("sq"))
                    act.wait_ge(*RT.upto("state", h))
                    act.wait_ge(stp_out, h * 16)
                    f(stp, ps[:, 0, 0:DV], ACT.Copy).then_inc(*RA.step("stp"))
                    act.wait_ge(*RV.upto("ms", h))
                    f(rso, rso, ACT.Ln).then_inc(*RA.step("lnr"))
                    act.wait_ge(*RA.upto("lnr", h))
                    f(rso, rso, ACT.Exp, scale=-0.5).then_inc(*RA.step("rs"))

            act.wait_ge(s0_out[0], 32)
            act.wait_ge(s0_out[1], 32)
            act.wait_ge(stp_out, 64)
            act.wait_ge(*RV.upto("o1", 3))
            f(projf[:, 0:8 * TOK], hf[:, 0:8 * TOK], ACT.Square).then_inc(*OA.step("sq"))
            act.wait_ge(*OV.upto("ms"))
            f(projf[:, 0:8 * TOK], projf[:, 0:8 * TOK], ACT.Ln).then_inc(*OA.step("ln"))
            act.wait_ge(*OA.upto("ln"))
            f(projf[:, 0:8 * TOK], projf[:, 0:8 * TOK], ACT.Exp, scale=-0.5).then_inc(*OA.step("rs"))

            act.wait_ge(*UV.upto("u3", 1))
            norm_squares(1)

            with act.Fori(0, 11) as i:
                for n in range(2):
                    act.wait_ge(*FT.upto(f"g{n}", i))
                    act.wait_ge(*FV.upto("last", i - 1))
                    f(gpad[:, 2 * n:2 * n + 2, 2:2 + SEQ], ps[:, 0:2, 0:SEQ], ACT.Copy)
                    f(gpad[:, 2 * n:2 * n + 2, 2 + SEQ:GW].rearrange("p n (b t) -> p n b t", t=6)[:, :, :, 2:6],
                      ps[:, 0:2, SEQ:TOK].rearrange("p n (b t) -> p n b t", t=TS),
                      ACT.Copy).then_inc(*FA.step(f"g{n}"))
                    act.wait_ge(*FV.upto(f"conv{n}", i))
                    f(cv, cv, ACT.Silu).then_inc(*FA.step(f"silu{n}"))
                act.wait_ge(*FT.upto("rows", i))
                act.wait_ge(conv_out, i * 32)
                f(crows, ps[0:18, 5, :], ACT.Copy).then_inc(*FA.step("rows"))

            with act.Fori(0, 4) as i:
                for n in range(2):
                    act.wait_ge(*DT.upto(f"t{n}", i))
                    act.wait_ge(y_out[n], i * 32)
                    f(yrow[:, n, 0:2, :].rearrange("p t c -> p (t c)"), ps[:, 4 + 2 * n, :], ACT.Copy)
                    f(yrow[0:NS, n, 2, :], ps[0:NS, 5 + 2 * n, 0:256], ACT.Copy).then_inc(*DA.step(f"r{n}"))

        @block.vector
        def _(dve):
            v = nc.vector
            for s_ in (PV_, *NV, AV, WV, TV, SV, SK, RV, OV, UV, FV, FZ, DV_):
                dve.sem_inc(s_.sem, len(s_.names))
            v.memset(rel_rows, 0.0).then_inc(*PV_.step("zero_rel"))
            dve.wait_ge(*PV_.upto("zero_rel"))
            dve.wait_ge(rel_in, 64)
            for t in range(TS):
                b = slice(32 * t, 32 * t + 32)
                dst = rel_rows[b, :].rearrange("p (b h t) -> p b h t", b=2, h=H_A)[:, :, :, t]
                src = relb[b, :].rearrange("p (a h) -> p a h", a=1).to_broadcast([32, 2, H_A])
                last = v.tensor_copy(dst, src)
            last.then_inc(*PV_.step("rel_rows"))
            dve.wait_ge(*PT_.upto("bias_p"))
            v.tensor_tensor(btab, ps[0:H_A, 0, :], tview("mult_p", H_A), ALU.add).then_inc(*PV_.step("bias_p"))
            dve.wait_ge(*PT_.upto("bias_s"))
            ms = tview("mult_s", P)
            v.tensor_tensor(bias_s[:, 0:512], ps[:, 1, :], ms[:, 0:512], ALU.add)
            v.tensor_tensor(bias_s[:, 512:CK], ps[:, 2, 0:P], ms[:, 512:CK], ALU.add).then_inc(*PV_.step("bias_s0"))
            new = ps[:, 2, P:P + NS].rearrange("p (a c) -> p a c", a=1).to_broadcast([P, 4, NS])
            v.tensor_tensor(bias_s[:, CK:].rearrange("p (g c) -> p g c", g=4), new,
                            ms[:, CK:].rearrange("p (g c) -> p g c", g=4), ALU.add).then_inc(*PV_.step("bias_s"))
            dve.wait_ge(*PT_.upto("vectors"))
            v.tensor_copy(small[:, :], ps[:, 3, 0:313]).then_inc(*PV_.step("vectors"))
            dve.wait_ge(*PT_.upto("c"))
            v.tensor_copy(cT[:, :, :].rearrange("p k c -> p (k c)"), ps[:, 4, 0:KD * NC9]).then_inc(*PV_.step("c"))
            for k in range(KD):
                dve.wait_ge(*PT_.upto(f"x{k}"))
                v.tensor_copy(xT[:, k, :], ps[:, 5 + k % 3, 0:TOK]).then_inc(*PV_.step(f"x{k}"))

            def mod(turn_no, group, step):
                for n in range(2):
                    t = bass.ds(group * 8 + 4 * n, 4)
                    bias = small[:, bass.ds(group * 8 + (BA + 4 * n), 4)].rearrange("p (n a) -> p n a", a=1)
                    last = v.tensor_tensor(modT[:, t, :], ps[:, 2 + n, 0:4 * NC9].rearrange("p (n c) -> p n c", n=4),
                                           bias.to_broadcast([P, 4, NC9]), ALU.add)
                last.then_inc(*step)

            def norm_mean(n, bank):
                dve.wait_ge(*NT[n].upto("s3"))
                v.tensor_scalar(rs, ps[:, bank, 0:TOK], 1 / D, EPS, ALU.mult, ALU.add).then_inc(*NV[n].step("ms"))

            def norm(n):
                sh, scl, g = (0, KD, N1) if n == 0 else (3 * KD, 4 * KD, N2)
                N = NV[n]
                gain = small[:, g:g + KD].rearrange("p (k a) -> p k a", a=1).to_broadcast([P, KD, NC9])
                v.scalar_tensor_tensor(out=modT[:, scl:scl + KD, :], in0=modT[:, scl:scl + KD, :], scalar=1.0,
                                       in1=gain, op0=ALU.add, op1=ALU.mult).then_inc(*N.step("scale"))
                dve.wait_ge(*NA[n].upto("rs"))
                r = rs.rearrange("p (a c) -> p a c", a=1).to_broadcast([P, KD, TOK])
                v.tensor_tensor(hT[:, :, :], xT[:, :, :], r, ALU.mult).then_inc(*N.step("times_r"))
                dve.wait_ge(*N.upto("times_r"))
                for k in range(KD):
                    last = v.tensor_scalar(hT[:, k, 0:SEQ], hT[:, k, 0:SEQ], modT[:, scl + k, 0:1],
                                           modT[:, sh + k, 0:1], ALU.mult, ALU.add)
                last.then_inc(*N.step("prompt"))
                hs = hT[:, :, SEQ:TOK].rearrange("p k (b t) -> p k b t", t=TS)
                for k0, names in ((scl, "s_scaled"), (sh, "done")):
                    m = modT[:, k0:k0 + KD, 1:NC9].rearrange("p k (b a) -> p k b a", a=1).to_broadcast([P, KD, NB, TS])
                    v.tensor_tensor(hs, hs, m, ALU.mult if k0 == scl else ALU.add).then_inc(*N.step(names))
                    dve.wait_ge(*N.upto(names))

            norm_mean(0, 4)
            with dve.Fori(0, N_ADA1 // SLOTS) as i:
                dve.wait_ge(*AT.upto("turn_b", i))
                mod(i, i, AV.step("mod"))
            dve.wait_ge(*AV.upto("mod", 3))
            norm(0)
            with dve.Fori(0, N_IN // SLOTS) as i:
                for u in (1, 3):
                    dve.wait_ge(*WT.upto(f"u{u}", i))
                    dve.wait_ge(*WV.upto(f"u{u - 1}", i))
                    v.tensor_copy(proj[:, bass.ds(i * 8 + 2 * u, 2), :], ps[:, 2:4, 0:TOK]).then_inc(WV.sem, 1)

            pg = proj[:, :, :].rearrange("p (g n) c -> p g n c", n=8)
            dve.wait_ge(*WV.upto("u3", 5))
            dve.wait_ge(*GT.upto("done"))
            dve.wait_ge(btab_out, 16)
            with dve.Fori(0, PAIRS // 2) as i:
                for par in range(2):
                    p = i * 2 + par
                    qk = pg[:, 0:2, bass.ds(p, 1), :].rearrange("p g a c -> p g (a c)")
                    dve.wait_ge(*TT.upto("probT", p - 1))
                    v.tensor_tensor(sqqk, qk, qk, ALU.mult).then_inc(*TV.step("squares"))
                    dve.wait_ge(*TT.upto("sums", p))
                    v.tensor_scalar(rsqk, ps[:, 4:6, 0:TOK], 1 / HD, EPS, ALU.mult, ALU.add).then_inc(*TV.step("ms"))
                    dve.wait_ge(*TA.upto("rs", p))
                    for g, name in enumerate("qk"):
                        v.scalar_tensor_tensor(
                            out=qkst[:, g, :], in0=proj[:, bass.ds(p + 8 * g, 1), :].rearrange("p a c -> p (a c)"),
                            scalar=small[:, QG + g:QG + g + 1], in1=rsqk[:, g, :], op0=ALU.mult,
                            op1=ALU.mult).then_inc(*TV.step(name))
                    dve.wait_ge(*TV.upto("k", p))
                    for g, dst in enumerate((qS, kS)):
                        last = v.tensor_copy(dst[:, bass.ds(p, 1), :].rearrange("p a c -> p (a c)"),
                                             qkst[:, g, SEQ:TOK])
                    last.then_inc(*TV.step("samples"))
                    dve.wait_ge(*TT.upto("kv_rows", p))
                    for g, (dst, stored, name) in enumerate(((krows, k_out, "krows"), (vrows, v_out, "vrows"))):
                        dve.wait_ge(stored, p * 32)
                        if g:
                            dve.wait_ge(*TT.upto("out", p - 1))
                        v.tensor_copy(dst[:, 0:2, :], ps[:, 6 + g, 0:256].rearrange("p (t c) -> p t c", t=2))
                        v.tensor_copy(dst[0:NS, 2, :], ps[0:NS, 6 + g, 256:384]).then_inc(*TV.step(name))
                    dve.wait_ge(*TV.upto("vrows", p))
                    v.tensor_copy(vrow_s[:, bass.ds(p * P, P)], vrows[0:NS, 2, :]).then_inc(*TV.step("vrow_s"))
                    dve.wait_ge(*TT.upto("scores", p))
                    dve.wait_ge(biasp_in[par], i * 16 + 16)
                    for e in range(2):
                        v.scalar_tensor_tensor(out=prob[:, e, 0:P], in0=ps[:, 4 + e, 0:P], scalar=HD ** -0.5,
                                               in1=bias_p[:, par, e, P:SEQ], op0=ALU.mult, op1=ALU.add)
                        last = v.scalar_tensor_tensor(out=prob[:, e, P:3 * P], in0=ps[:, 4 + e, P:3 * P],
                                                      scalar=HD ** -0.5, in1=bias_p[:, par, e, :], op0=ALU.mult,
                                                      op1=ALU.add)
                    last.then_inc(*TV.step("biased"))
                    dve.wait_ge(*TV.upto("biased", p))
                    for e in range(2):
                        for q in range(2):
                            c = 2 * e + q
                            last = v.tensor_reduce(out=stat[:, c:c + 1], in_=prob[:, e, P * q:P * q + P * (q + 1)],
                                                   axis=AX_X, op=ALU.max, negate=True)
                    last.then_inc(*TV.step("max"))
                    dve.wait_ge(*TA.upto("exp", p))
                    v.reciprocal(stat[:, 8:12], stat[:, 4:8]).then_inc(*TV.step("recip"))
                    dve.wait_ge(*TV.upto("recip", p))
                    for e in range(2):
                        for q in range(2):
                            c = 2 * e + q
                            part = prob[:, e, P * q:P * q + P * (q + 1)]
                            last = v.tensor_scalar(part, part, stat[:, 8 + c:9 + c], None, ALU.mult)
                    last.then_inc(*TV.step("norm"))
                    dve.wait_ge(*TT.upto("turn_b", p))
                    mod(p, p + 4, TV.step("mod"))
                    for e in range(2):
                        h = slice(HD * e, HD * e + HD)
                        last = v.tensor_copy(hT[h, bass.ds(p, 1), 0:SEQ].rearrange("p a c -> p (a c)"),
                                             ps[h, 4 + e, 0:SEQ])
                    last.then_inc(*TV.step("out"))

            qdn = qd.rearrange("p (n c) -> p n c", c=P)
            with dve.Fori(0, NB // 2) as g:
                dve.wait_ge(*ST.upto("s15", g - 1))
                v.memset(qd, 0.0).then_inc(*SV.step("zero"))
                dve.wait_ge(*SV.upto("zero", g))
                for e in range(2):
                    h = slice(HD * e, HD * e + HD)
                    for b in range(2):
                        lo = 8 * b * 136 + TS * e
                        dst = qd_diag(qd, h, lo)
                        last = v.tensor_copy(dst, qS[h, :, bass.ds(g * 8 + TS * b, TS)])
                last.then_inc(*SV.step("qd"))
                for n in range(1, 16, 2):
                    dve.wait_ge(*ST.upto(f"k{n}", g))
                    if n >= 2:
                        dve.wait_ge(*ST.upto(f"s{n - 2}", g))
                    dve.wait_ge(*SK.upto(f"k{n - 1}", g))
                    v.tensor_copy(kcT[:, 1, 0:512], ps[:, 2, :])
                    v.tensor_copy(kcT[:, 1, 512:CK], ps[:, 3, 0:P]).then_inc(SK.sem, 1)
                dve.wait_ge(*ST.upto("s15", g))
                sd = HD ** -0.5
                for out, src, bias in ((sc[:, 0:512], ps[:, 4, :], bias_s[:, 0:512]),
                                       (sc[:, 512:CK], ps[:, 5, 0:P], bias_s[:, 512:CK]),
                                       (sc[:, CK:CK + NS], ps[:, 6, 0:NS], bias_s[:, bass.ds(g * NS + CK, NS)])):
                    last = v.scalar_tensor_tensor(out=out, in0=src, scalar=sd, in1=bias, op0=ALU.mult, op1=ALU.add)
                last.then_inc(*SV.step("biased"))
                dve.wait_ge(*SV.upto("biased", g))
                v.tensor_reduce(out=stat[:, 0:1], in_=sc, axis=AX_X, op=ALU.max,
                                negate=True).then_inc(*SV.step("max"))
                dve.wait_ge(*SA.upto("exp", g))
                v.reciprocal(stat[:, 2:3], stat[:, 1:2]).then_inc(*SV.step("recip"))
                dve.wait_ge(*SV.upto("recip", g))
                v.tensor_scalar(sc, sc, stat[:, 2:3], None, ALU.mult).then_inc(*SV.step("norm"))
                dve.wait_ge(*ST.upto("out", g))
                for e in range(2):
                    h = slice(HD * e, HD * e + HD)
                    src = ps[h, 7, 0:128].rearrange("p (b n e t) -> p b n e t", b=2, n=8, e=2)
                    for b in range(2):
                        last = v.tensor_copy(hT[h, 0:8, bass.ds(g * 8 + (SEQ + TS * b), TS)], src[:, b, :, e, :])
                last.then_inc(*SV.step("out"))

            v.memset(cumz[:, 0:1], 0.0)
            v.memset(rso, 1.0)
            dve.wait_ge(*ST.upto("out", 3))
            dve.wait_ge(wg2_in, 16)
            with dve.Fori(0, 2) as i:
                for half in range(2):
                    h = i * 2 + half
                    cum = cumz[:, 1:1 + TOK]
                    qb = proj[:, bass.ds(h + 24, 1), :].rearrange("p a c -> p (a c)")
                    kb = proj[:, bass.ds(h + 28, 1), :].rearrange("p a c -> p (a c)")
                    dve.wait_ge(*RT.upto("z", h - 1))
                    v.tensor_copy(wgs, wg2[:, bass.ds(h * P, P)]).then_inc(*RV.step("wgs"))
                    dve.wait_ge(*RT.upto("z", h))
                    v.tensor_scalar(zb, ps[:, 0, 0:TOK], small[:, bass.ds(h + BG, 1)], None,
                                    ALU.add).then_inc(*RV.step("z"))
                    dve.wait_ge(*RA.upto("ln", h))
                    v.scalar_tensor_tensor(out=ex, in0=zb, scalar=0.0, in1=ex, op0=ALU.min,
                                           op1=ALU.subtract).then_inc(*RV.step("la"))
                    kept = keep_g[:, SEQ:TOK].rearrange("p (b t) -> p b t", t=TS)
                    v.memset(keep_g[:, 0:SEQ], 1.0)
                    v.memset(kept[:, :, 1:TS], 1.0)
                    v.memset(kept[:, :, 0:1], 0.0).then_inc(*RV.step("keep"))
                    dve.wait_ge(*RV.upto("keep", h))
                    v.tensor_tensor_scan(cum, keep_g, ex, 0.0, ALU.mult, ALU.add).then_inc(*RV.step("cum"))
                    dve.wait_ge(*RV.upto("cum", h))
                    mid = cum[:, 15:SEQ:32]
                    v.tensor_scalar(keep_g[:, 0:8], mid, 1 / TAU, None, ALU.mult)
                    v.tensor_scalar(rb[:, 0:1], cum[:, SEQ - 1:SEQ], 1 / TAU, None, ALU.mult).then_inc(*RV.step("rb"))
                    v.tensor_tensor(qp.rearrange("p (n c) -> p n c", c=32),
                                    cum[:, 0:SEQ].rearrange("p (n c) -> p n c", c=32),
                                    mid.rearrange("p (n a) -> p n a", a=1).to_broadcast([P, 8, 32]),
                                    ALU.subtract).then_inc(*RV.step("dq"))
                    cs = cum[:, SEQ:TOK].rearrange("p (b t) -> p b t", t=TS)
                    v.tensor_tensor(kd[:, SEQ:TOK].rearrange("p (b t) -> p b t", t=TS),
                                    cs[:, :, TS - 1:TS].to_broadcast([P, NB, TS]), cs,
                                    ALU.subtract).then_inc(*RV.step("dd"))
                    sd = DK ** -0.5
                    dve.wait_ge(*RA.upto("dec", h))
                    v.scalar_tensor_tensor(out=qp, in0=qb[:, 0:SEQ], scalar=sd, in1=qp, op0=ALU.mult,
                                           op1=ALU.mult).then_inc(*RV.step("qp"))
                    v.scalar_tensor_tensor(out=qe, in0=qb[:, SEQ:TOK], scalar=sd, in1=qe, op0=ALU.mult,
                                           op1=ALU.mult).then_inc(*RV.step("qe"))
                    v.tensor_tensor(ke, kb[:, SEQ:TOK], ke, ALU.mult).then_inc(*RV.step("ke"))
                    v.tensor_tensor(kd, kb, kd, ALU.mult).then_inc(*RV.step("kd"))
                    v.memset(ps[:, 3, 0:384], 0.0).then_inc(*RV.step("zero_att"))
                    dve.wait_ge(*RV.upto("zero_att", h))
                    for c in range(8):
                        dve.wait_ge(*RA.upto(f"ki{c}", h))
                        n = 32 * (c + 1)
                        v.tensor_tensor(ki[:, c % 2, 0:n], kb[:, 0:n], ki[:, c % 2, 0:n],
                                        ALU.mult).then_inc(*RV.step(f"ki{c}"))
                    dve.wait_ge(*RT.upto("att7", h))
                    v.tensor_tensor(attT, ps[:, 3, 0:384], causal, ALU.mult).then_inc(*RV.step("att"))
                    dve.wait_ge(*RT.upto("att_s", h))
                    v.tensor_tensor(attS, ps[0:NS, 7, 0:NS], causal_s, ALU.mult).then_inc(*RV.step("att_s"))
                    v.tensor_copy(kdr[:, 0:2, :].rearrange("p t c -> p (t c)"), ps[:, 6, 0:256])
                    v.tensor_copy(kdr[0:NS, 2, :], ps[0:NS, 6, 256:384]).then_inc(*RV.step("kdr"))
                    dve.wait_ge(*RV.upto("kdr", h))
                    v.tensor_tensor(kdm.rearrange("p (b c) -> p b c", b=NB),
                                    kdr[0:NS, 2:3, :].to_broadcast([NS, NB, P]),
                                    own_batch.rearrange("p (b a) -> p b a", a=1).to_broadcast([NS, NB, P]),
                                    ALU.mult).then_inc(*RV.step("kdm"))
                    dve.wait_ge(*RT.upto("states", h))
                    for b in range(NB):
                        bank = (1, 2, 6, 7)[b // 2]
                        last = v.scalar_tensor_tensor(out=s0[:, half, b, :], in0=s0[:, half, b, :],
                                                      scalar=dec[:, b:b + 1],
                                                      in1=ps[:, bank, DV * (b % 2):DV * (b % 2) + DV],
                                                      op0=ALU.mult, op1=ALU.add)
                    last.then_inc(*RV.step("new_state"))
                    dve.wait_ge(*RT.upto("sum", h))
                    v.tensor_scalar(rso, ps[:, 3, 0:TOK], 1 / DV, EPS, ALU.mult, ALU.add).then_inc(*RV.step("ms"))
                    dve.wait_ge(*RA.upto("rs", h))
                    for j in range(2):
                        dve.wait_ge(*RV.upto("ms", h))
                        dst = hT[:, bass.ds(h * 2 + 8 + j, 1), :].rearrange("p a c -> p (a c)")
                        tmp = sqo[:, j, :]
                        v.scalar_tensor_tensor(out=tmp, in0=ps[:, 4 + j, 0:TOK], scalar=small[:, GO + j:GO + j + 1],
                                               in1=rso, op0=ALU.mult, op1=ALU.mult).then_inc(*RV.step(f"g{j}"))
                        dve.wait_ge(*RV.upto(f"g{j}", h))
                        v.tensor_tensor(dst, tmp, proj[:, bass.ds(h * 2 + 40 + j, 1), :].rearrange("p a c -> p (a c)"),
                                        ALU.mult).then_inc(*RV.step(f"o{j}"))

            dve.wait_ge(*OT.upto("sums"))
            q8 = projf[:, 0:8 * TOK].rearrange("p (n c) -> p n c", n=8)
            v.tensor_scalar(q8, ps[:, :, 0:TOK], 1 / HD, EPS, ALU.mult, ALU.add).then_inc(*OV.step("ms"))
            dve.wait_ge(*OA.upto("rs"))
            v.scalar_tensor_tensor(out=hf[:, 0:8 * TOK], in0=hf[:, 0:8 * TOK], scalar=small[:, AO:AO + 1],
                                   in1=projf[:, 0:8 * TOK], op0=ALU.mult, op1=ALU.mult).then_inc(*OV.step("done"))

            def gated(gate, tile, psum, out, steps, n, i):
                ts = tmp_s.rearrange("p (n b t) -> p n b t", n=2, b=NB)
                gs = modT[:, bass.ds(tile + gate, 2), 1:NC9].rearrange("p n (b a) -> p n b a", a=1)
                v.tensor_tensor(ts, psum[:, :, SEQ:TOK].rearrange("p n (b t) -> p n b t", t=TS),
                                gs.to_broadcast([P, 2, NB, TS]), ALU.mult).then_inc(*steps.step(f"s{n}"))
                for m in range(2):
                    v.scalar_tensor_tensor(
                        out=out(m)[:, 0:SEQ], in0=psum[:, m, 0:SEQ],
                        scalar=modT[:, bass.ds(tile + (gate + m), 1), 0:1].rearrange("p a b -> p (a b)"),
                        in1=xT[:, bass.ds(tile + m, 1), 0:SEQ].rearrange("p a c -> p (a c)"),
                        op0=ALU.mult, op1=ALU.add)
                dve.wait_ge(*steps.upto(f"s{n}", i))
                for m in range(2):
                    last = v.tensor_tensor(out(m)[:, SEQ:TOK], tmp_s[:, NS * m:NS * m + NS],
                                           xT[:, bass.ds(tile + m, 1), SEQ:TOK].rearrange("p a c -> p (a c)"), ALU.add)
                last.then_inc(*steps.step(f"u{n}"))

            with dve.Fori(0, 2) as i:
                for u in range(4):
                    dve.wait_ge(*UT.upto(f"u{u}", i))
                    t = i * 8 + 2 * u
                    if u:
                        dve.wait_ge(*UV.upto(f"u{u - 1}", i))
                    else:
                        dve.wait_ge(*UV.upto("u3", i - 1))
                    gated(2 * KD, t, ps[:, 2 * (u % 2):2 * (u % 2) + 2, :],
                          lambda m, t=t: xT[:, bass.ds(t + m, 1), :].rearrange("p a c -> p (a c)"), UV, u, i)
            norm_mean(1, 4)
            norm(1)

            v.memset(gpad[:, :, 0:2], 0.0).then_inc(*FZ.step("zero"))
            dve.wait_ge(*FZ.upto("zero"))
            with dve.Fori(0, 11) as i:
                dve.wait_ge(*FT.upto("hist", i))
                dve.wait_ge(*FV.upto("last", i - 1))
                v.tensor_copy(gpad[:, :, 2 + SEQ:GW].rearrange("p n (b t) -> p n b t", t=6)[:, :, :, 0:2],
                              ps[:, 4, 0:64].rearrange("p (n b r) -> p n b r", n=4, b=NB)).then_inc(*FV.step("hist"))
                dve.wait_ge(*FV.upto("hist", i))
                for n in range(2):
                    dve.wait_ge(*FA.upto(f"g{n}", i))
                    dve.wait_ge(*FV.upto(f"act{1 - n}", i - 1 + n))
                    w = lambda j, m: small[:, bass.ds(i * 4 + (CW + KF * j + 2 * n + m), 1)]
                    for j, name in ((0, "a"), (1, "b"), (2, "conv")):
                        for m in range(2):
                            g = gpad[:, 2 * n + m, j:j + GW - 2]
                            if j == 0:
                                last = v.tensor_scalar(cv[:, m, :], g, w(0, m), w(3, m), ALU.mult, ALU.add)
                            else:
                                last = v.scalar_tensor_tensor(out=cv[:, m, :], in0=g, scalar=w(j, m),
                                                              in1=cv[:, m, :], op0=ALU.mult, op1=ALU.add)
                        last.then_inc(*FV.step(f"{name}{n}"))
                        dve.wait_ge(*FV.upto(f"{name}{n}", i))
                    dve.wait_ge(*FT.upto(f"u{n}", i))
                    dve.wait_ge(*FA.upto(f"silu{n}", i))
                    dst = actT[:, bass.ds(i * 4 + 2 * n, 2), :]
                    v.tensor_tensor(dst[:, :, 0:SEQ], ps[:, 2:4, 0:SEQ], cv[:, :, 0:SEQ], ALU.mult)
                    v.tensor_tensor(dst[:, :, SEQ:TOK].rearrange("p n (b t) -> p n b t", t=TS),
                                    ps[:, 2:4, SEQ:TOK].rearrange("p n (b t) -> p n b t", t=TS),
                                    samples_of(cv, 2 + SEQ), ALU.mult).then_inc(*FV.step(f"act{n}"))
                dve.wait_ge(*FT.upto("rows", i - 1))
                v.tensor_copy(glast[:, :, 0:2], gpad[:, :, SEQ:SEQ + 2])
                v.tensor_copy(glast[:, :, 2:18].rearrange("p n (b r) -> p n b r", r=2),
                              gpad[:, :, 2 + SEQ:GW].rearrange("p n (b t) -> p n b t", t=6)[:, :, :, 4:6]
                              ).then_inc(*FV.step("last"))

            dve.wait_ge(*FT.upto("rows", 10))
            with dve.Fori(0, 4) as i:
                for n in range(2):
                    dve.wait_ge(*DT.upto(f"u{n}", i))
                    dve.wait_ge(*DT.upto(f"t{n}", i - 1))
                    dve.wait_ge(*DV_.upto("u0" if n else "u1", i - 1 + n))
                    gated(5 * KD, i * 4 + 2 * n, ps[:, 2 * n:2 * n + 2, :], lambda m, n=n: yst[:, n, m, :], DV_, n, i)


def qd_diag(qd, h, lo):
    v = qd[h, lo:lo + 8]
    part = list(v.ap[0])
    return bass.AP(v.tensor, v.offset, [part, [136, 8], [1, TS]])


def samples_of(cv, lo):
    v = cv[:, :, lo:lo + TS]
    part, blk = list(v.ap[0]), list(v.ap[1])
    return bass.AP(v.tensor, v.offset, [part, blk, [6, NB], [1, TS]])


_OUTS = [("y_p", (SEQ, D)), ("y_s", (NS, D)), ("new_k_p", (SEQ, 1024)), ("new_v_p", (SEQ, 1024)),
         ("new_gla_p", (H_B, DK, DV)), ("new_conv_p", (2, D_FF)), ("new_k_s", (NS, 1024)), ("new_v_s", (NS, 1024)),
         ("new_gla_s", (NB, H_B, DK, DV)), ("new_conv_s", (2 * NB, D_FF))]


def kernel(**inputs):
    import concourse.bacc as bacc
    from concourse.bass_utils import run_bass_kernel_spmd

    nc = bacc.Bacc("TRN2", target_bir_lowering=False, num_devices=1)
    tables = constants()
    arrays, a, o = {}, {}, {}
    for name, x in {**inputs, "tables": tables}.items():
        x = np.ascontiguousarray(x)
        arrays[f"in_{name}"] = x
        a[name] = nc.dram_tensor(f"in_{name}", x.shape, mybir.dt.from_np(x.dtype), kind="ExternalInput").ap()
    for name, shape in _OUTS:
        o[name] = nc.dram_tensor(f"out_{name}", shape, F32, kind="ExternalOutput").ap()
    bias_rows = nc.dram_tensor("bias_rows", [H_A, 512], F32)
    bias_full = nc.dram_tensor("bias_full", [H_A, P, SEQ], F32)
    build(nc, a, o, bias_rows, bias_full)
    r = run_bass_kernel_spmd(nc, [arrays], core_ids=[0]).results[0]
    g = {name: r[f"out_{name}"] for name, _ in _OUTS}
    return (g["y_p"].reshape(1, SEQ, D), g["y_s"].reshape(NB, TS, D),
            g["new_k_p"].reshape(1, 1, SEQ, H_A, HD), g["new_v_p"].reshape(1, 1, SEQ, H_A, HD),
            g["new_gla_p"].reshape(1, 1, H_B, DK, DV), g["new_conv_p"].reshape(1, 1, 2, D_FF),
            g["new_k_s"].reshape(1, NB, TS, H_A, HD), g["new_v_s"].reshape(1, NB, TS, H_A, HD),
            g["new_gla_s"].reshape(1, NB, H_B, DK, DV), g["new_conv_s"].reshape(1, NB, 2, D_FF))
```

```python
import math
from contextlib import ExitStack

import concourse.bass as bass
import numpy as np
from concourse import mybir

F32 = mybir.dt.float32
F32R = mybir.dt.float32r
ACT = mybir.ActivationFunctionType
ALU = mybir.AluOpType
AX_X = mybir.AxisListType.X

P = 128
D = 2048
SEQ = 256
NB, TS = 8, 4
NS = NB * TS
TOK = SEQ + NS
PAST = 1024
H_A, HD = 16, 64
PAIRS = H_A // 2
H_B, DK, DV = 4, 128, 256
RANK = 16
D_FF = 5632
EPS = 1e-6
TAU = 16.0
KD = D // P
KF = D_FF // P
NC9 = 1 + NB
DIL = ((128, 1), (512, 4), (2048, 16))
NBUCK, MAXD = 32, 2048
NEG = -1e30

SLOTS, SLOT = 4, 11 * 256
BUFS, CHUNK = 4, 1024

N1, N2, BA = 0, KD, 2 * KD
CW, CB = 128, 128 + 3 * KF
QG, KG, AO, GO, BG = 304, 305, 306, 307, 309

FAR = PAST // 2 // 16 * TS
CK = FAR + PAST // 2
KT = CK // P


def bucket(dist):
    dist = np.asarray(dist)
    exact = NBUCK // 2
    df = np.maximum(dist, 1).astype(np.float32)
    large = exact + (np.log(df / exact) / math.log(MAXD / exact) * (NBUCK - exact)).astype(np.int32)
    return np.where(dist < exact, dist, np.minimum(large, NBUCK - 1))


def multiplicity(dist):
    dist = np.asarray(dist)
    n = sum(((dist >= 0) & (dist <= w) & (dist % d == 0)).astype(np.int32) for w, d in DIL)
    return np.where(n > 0, np.log(np.maximum(n, 1)), NEG).astype(np.float32)


def one_hot(dist):
    d = np.asarray(dist)
    return ((bucket(np.maximum(d, 0))[None] == np.arange(NBUCK)[:, None]) & (d[None] >= 0)).astype(np.float32)


CONST_LAYOUT = {}


def constants():
    parts = []

    def add(name, a):
        full = np.zeros((P, a.shape[1]), np.float32)
        full[:a.shape[0]] = a
        CONST_LAYOUT[name] = (sum(p.shape[1] for p in parts), a.shape[1])
        parts.append(full)

    i = np.arange(P)
    add("ident", np.eye(P, dtype=np.float32))
    add("halves", (i[:, None] // HD == i[None] // HD).astype(np.float32))
    add("ones", np.ones((P, P), np.float32))
    s, c = np.arange(P)[:, None], np.arange(SEQ)[None]
    add("causal", np.concatenate([s <= c, s + P <= c[:, P:]], 1).astype(np.float32))
    a = np.arange(NS)
    same = a[:, None] // TS == a[None] // TS
    add("causal_s", (same & (a[:, None] <= a[None])).astype(np.float32))
    add("own_batch", (a[:, None] // TS == np.arange(NB)[None]).astype(np.float32))
    dist = 2 * P - 1 - np.arange(512)
    add("hot_p", one_hot(dist))
    add("mult_p", np.tile(multiplicity(dist), (H_A, 1)))
    r = np.arange(P)
    far = 16 * (r % 32) + r // 32
    pos = np.concatenate([far, PAST // 2 + np.arange(PAST // 2)])
    t = np.arange(TS)
    add("hot_s", np.concatenate(
        [np.concatenate([one_hot(PAST + k - pos), one_hot(k - a % TS)], 1) for k in t], 0))
    old = multiplicity(PAST + t[:, None] - pos[None])[r % TS]
    new = []
    for g in range(NB // 2):
        b = 2 * g + r // 64
        m = multiplicity((r % TS)[:, None] - (a % TS)[None])
        new.append(np.where(b[:, None] == a[None] // TS, m, NEG))
    add("mult_s", np.concatenate([old] + new, 1).astype(np.float32))
    return np.concatenate(parts, 1)


class Steps:

    def __init__(self, sem, *names):
        self.sem, self.names, self.at = sem, names, 0

    def step(self, name):
        assert self.names[self.at] == name, (self.names[self.at], name)
        self.at = (self.at + 1) % len(self.names)
        return self.sem, 1

    def upto(self, name, turn=0):
        return self.sem, (turn + 1) * len(self.names) + self.names.index(name) + 1


def build(nc, a, o, bias_rows, bias_full):
    ctx = ExitStack()
    with ctx:
        def sb(name, shape):
            return ctx.enter_context(nc.sbuf_tensor(name, shape, F32))

        def sem(name):
            return ctx.enter_context(nc.semaphore(name))

        def sbr(name, shape):
            return ctx.enter_context(nc.sbuf_tensor(name, shape, F32R))

        ring = sb("ring", [P, SLOTS, SLOT])
        whi = sbr("whi", [P, BUFS, CHUNK])
        wlo = sbr("wlo", [P, BUFS, CHUNK])
        xT = sb("xT", [P, KD, TOK])
        hhi = sbr("hhi", [P, KD, TOK])
        hlo = sbr("hlo", [P, KD, TOK])
        proj = sb("proj", [P, 48, TOK])
        work = sb("work", [P, 2048])
        keep = CONST_LAYOUT["own_batch"][0] + NB
        con = sb("con", [P, keep])
        small = sb("small", [P, 313])
        c18 = sbr("c18", [P, KD, 2 * NC9])
        modT = sb("modT", [P, 6 * KD, NC9])
        ghi = sbr("ghi", [P, KD, RANK])
        glo = sbr("glo", [P, KD, RANK])
        qkS = sb("qkS", [P, 512])
        qS = qkS[:, 0:256].rearrange("p (n c) -> p n c", n=PAIRS)
        kS = qkS[:, 256:512].rearrange("p (n c) -> p n c", n=PAIRS)
        mrow = sb("mrow", [2 * NC9, 512])
        ps = ctx.enter_context(nc.psum_tensor("ps", [P, 8, 512], F32))

        def cview(name, rows=P):
            at, n = CONST_LAYOUT[name]
            return con[0:rows, at:at + n]

        ident, halves, ones = cview("ident"), cview("halves"), cview("ones")
        causal, causal_s, own_batch = cview("causal"), cview("causal_s", NS), cview("own_batch", NS)
        projf = proj[:, :, :].rearrange("p n c -> p (n c)")

        xr = projf[:, 0:3 * D].rearrange("p (t d) -> p t d", t=3)
        crow = projf[0:NC9, 6144:6144 + D]
        vrow = projf[:, 8192:8704].rearrange("p (t d) -> p t d", t=4)
        c0, cn = CONST_LAYOUT["hot_p"][0], CONST_LAYOUT["mult_s"]
        temp = projf[:, 8704:8704 + cn[0] + cn[1] - c0]

        def tview(name, rows):
            at, n = CONST_LAYOUT[name]
            return temp[0:rows, at - c0:at - c0 + n]

        relb = projf[:, 11300:11316]
        rel_rows = projf[:, 11328:11456]
        sq = projf[:, 11520:13824].rearrange("p (j n c) -> p j n c", j=2, n=4)
        hraw = projf[:, 0:KD * TOK].rearrange("p (n c) -> p n c", n=KD)
        btab = work[0:H_A, 0:512]
        cT = work[:, 512:656].rearrange("p (k c) -> p k c", k=KD)
        rs = work[:, 656:944]
        bias_s = work[:, 1248:2016]
        wglr = qkS[:, 0:256].rearrange("p (k c) -> p k c", k=KD)
        stat = work[:, 2016:2032]

        def at(lo, n, **parts):
            v = projf[:, 24 * TOK + lo:24 * TOK + lo + n]
            return v.rearrange("p (g c) -> p g c", g=parts["g"]) if parts else v

        sqqk, rsqk = at(0, 576, g=2), at(576, 576, g=2)
        vst = at(1152, 288)
        prob = at(1440, 768, g=2)
        bias_p = at(2208, 1024).rearrange("p (j e c) -> p j e c", j=2, e=2)
        krows, vrows = at(3232, 384, g=3), at(3616, 384, g=3)
        probT = at(4000, 768, g=2)
        qkst = at(4768, 576, g=2)

        kv0 = 8 * TOK
        qd = projf[:, kv0:kv0 + 512]
        kcT = projf[:, kv0 + 512:kv0 + 1856].rearrange("p (j c) -> p j c", j=2)
        sc = projf[:, kv0 + 1856:kv0 + 2528]
        orow = projf[:, kv0 + 2528:kv0 + 3040]
        vrow_s = projf[0:NS, kv0 + 3296:kv0 + 4320]
        glrT = projf[0:RANK, kv0 + 4320:kv0 + 4608]
        sT = work[:, 0:768].rearrange("p (t c) -> p t c", t=6)

        s0 = projf[:, 0:2048].rearrange("p (b v) -> p b v", b=NB)
        zb, ex = projf[:, 2048:2336], projf[:, 2336:2624]
        cumz = projf[:, 2624:2913]
        qp = projf[:, 2914:3170]
        ki = projf[:, 3170:3682].rearrange("p (j c) -> p j c", j=2)
        sqo = projf[:, 3170:3746].rearrange("p (j c) -> p j c", j=2)
        attT = projf[:, 3746:4130]
        attS = projf[0:NS, 4130:4162]
        kd = projf[:, 4162:4450]
        qe, ke = projf[:, 4450:4482], projf[:, 4482:4514]
        rb = projf[:, 4514:4523]
        dec = projf[:, 4524:4532]
        stp = projf[:, 4532:4788]
        kdm = projf[0:NS, 4788:5812]
        wgs = projf[0:RANK, 5812:5940]
        keep_g = projf[:, 5940:6228]
        wg2 = mrow[0:RANK, :]
        vbst = work[:, 0:576].rearrange("p (j c) -> p j c", j=2)
        vbr = work[:, 576:1344].rearrange("p (t c) -> p t c", t=3)
        kdr = work[:, 1344:1728].rearrange("p (t c) -> p t c", t=3)
        rso = work[:, 1728:2016]

        actT = projf[:, 0:KF * TOK].rearrange("p (n c) -> p n c", n=KF)
        tail = projf[:, KF * TOK:48 * TOK]
        GW = 2 + SEQ + NB * 6
        gpad = work[:, 0:4 * GW].rearrange("p (n c) -> p n c", n=4)
        cv = work[:, 1224:1832].rearrange("p (n c) -> p n c", n=2)
        glast = work[:, 1832:1904].rearrange("p (n c) -> p n c", n=4)
        hrow = tail[0:16, 0:1024].rearrange("p (j c) -> p j c", j=2)
        crows = qkS[0:18, :]
        tmp_s = work[:, 1904:2032]

        yst = work[:, 0:1152].rearrange("p (n c) -> p n c", n=4)
        yrow = tail[:, 0:1024].rearrange("p (j c) -> p j c", j=2)
        ahi = hhi[:, 0:8, :].rearrange("p (j n) c -> p j n c", j=2)
        alo = hlo[:, 0:8, :].rearrange("p (j n) c -> p j n c", j=2)

        full = [sem(f"slot_full{s}") for s in range(SLOTS)]
        far_in = [sem(f"far_rows_in{s}") for s in range(SLOTS)]
        hi_done = sem("chunks_hi")
        lo_done = sem("chunks_lo")
        used = sem("chunks_used")
        act_hi, act_lo = sem("act_hi"), sem("act_lo")
        con_in, x_in, c_in, vec_in, rel_in, temp_in, wglr_in, wg2_in, vrow_in = (
            sem(n) for n in ("con_in", "x_in", "c_in", "vec_in", "rel_in", "temp_in", "wglr_in", "wg2_in",
                             "vrow_in"))
        btab_out, slant_out = sem("bias_table_out"), sem("bias_slant_out")
        biasp_in = [sem(f"bias_pair_in{j}") for j in range(2)]
        pool_turns, row_turns, copy_turns = sem("pool_turns"), sem("row_turns"), sem("copy_turns")
        k_out, v_out = sem("k_rows_out"), sem("v_rows_out")
        stp_out = sem("prompt_state_out")
        conv_out = sem("conv_rows_out")
        y_out = sem("y_rows_out")
        kv_stored, stp_stored, conv_stored, y_stored = (
            sem(f"{n}_stored") for n in ("kv_rows", "prompt_state", "conv_rows", "y_rows"))
        s0_in, s0_out = sem("state_in"), sem("state_out")
        hist_in = [sem(f"history_in{j}") for j in range(2)]

        st = lambda name, *names: Steps(sem(name), *names)
        PT_ = st("prep_tensor", "bias_p", "bias_s", "vectors", "c", *(f"x{k}" for k in range(KD)))
        PV_ = st("prep_vector", "zero_rel", "rel_rows", "bias_p", "bias_s0", "bias_s", "vectors", "c",
                 *(f"x{k}" for k in range(KD)))
        PA_ = st("prep_scalar", "silu_c")
        NT = [st(f"norm{n}_tensor", "s0", "s1", "s2", "s3") for n in (1, 2)]
        NA = [st(f"norm{n}_scalar", "q0", "q1", "q2", "q3", "ln", "rs", "h0", "h1", "h2", "h3") for n in (1, 2)]
        NV = [st(f"norm{n}_vector", "ms", "scale", *(f"{x}{j}" for j in range(4) for x in "tpsdl")) for n in (1, 2)]
        CV = st("prep_split_vector", "c_lo", "glr_lo")
        CA = st("prep_split_scalar", "c_hi", "glr_hi")
        AT = st("ada_tensor", "turn_a", "turn_b")
        AA = st("ada_scalar", "rows_a", "rows_b")
        AV = st("ada_vector", "base", "mod")
        WV = [st(f"in_evac{n}", "u0", "u1", "u2", "u3") for n in range(2)]
        GT = st("glr_tensor", "done")
        GA = st("glr_scalar", "rows", "silu_r")
        TT = st("pair_tensor", "sums", "kv_rows", "scores", "turn_a", "probT", "out", "turn_b")
        TV = st("pair_vector", "squares", "ms", "q", "k", "samples", "krows", "vrows", "biased",
                "max", "recip", "norm", "out", "base", "mod")
        TA = st("pair_scalar", "ln", "rs", "vstage", "rows_a", "exp", "probT", "rows_b")
        ST = st("sample_tensor", "k0", *(x for n in range(1, 16) for x in (f"k{n}", f"s{n - 1}")), "s15", "probT",
                "v0", "v1", "v2", "v3", "oT")
        SV = st("sample_vector", "qd", "biased", "max", "recip", "norm", "out")
        SK = st("sample_key_copies", *(f"k{n}" for n in range(16)))
        SA = st("sample_scalar", "exp", "probT", "orow")
        RT = st("gla_tensor", "z", "vrows", *(f"att{i}" for i in range(8)), "kdrows", "att_s", "o", "state",
                "states", "sum")
        RV = st("gla_vector", "wgs", "z", "la", "cum", "rb", "dq", "dd", "qp", "qe", "ke", "kd", "zero_att",
                *(f"ki{i}" for i in range(8)), "att", "att_s", "kdr", "kdm", "new_state",
                "ms", "g0", "o0", "g1", "o1")
        RA = st("gla_scalar", "vstage", "abs", "exp", "ln", "vrows", "eq", "eqs", "eks", "ekd", "ekds", "dec",
                *(f"ki{i}" for i in range(8)), "sq", "stp", "lnr", "rs")
        OT = st("onorm_tensor", "sums")
        OA = st("onorm_scalar", "sq", "ln", "rs", "hi", "gla_hi")
        OV = st("onorm_vector", "ms", "done", "lo", "gla_lo")
        UV = st("out_vector", *(x for n in range(4) for x in (f"s{n}", f"u{n}")))
        FT = st("up_tensor", "hist", "rows")
        FV = st("up_vector", "hist", "a0", "b0", "conv0", "act0", "a1", "b1", "conv1", "last", "act1")
        FA = st("up_scalar", "g0", "silu0", "g1", "silu1", "rows")
        FZ = st("first_fills", "zero_qd", "keep", "zero")
        DT = st("down_tensor", "t0", "t1", "t2")
        DV_ = st("down_vector", "s0", "u0", "s1", "u1")
        DA = st("down_scalar", "r0", "r1", "r2")

        SL_IN, SL_ADA2, SL_IN2, SL_SAMP, SL_OUT, SL_UP, SL_DOWN = 32, 56, 120, 144, 176, 192, 280
        CH_IN, CH_ADA2, CH_IN2, CH_OUT, CH_UP, CH_DOWN = 64, 112, 240, 288, 320, 496
        LEAD = 2

        w_ada = a["w_ada"][0].rearrange("(k p) c -> p k c", p=P)
        w_in = a["w_in"][0].rearrange("(k p) c -> p k c", p=P)
        w_out = a["w_out"][0].rearrange("(k p) c -> p k c", p=P)
        w_up = a["w_up"][0].rearrange("(k p) c -> p k c", p=P)
        w_down = a["w_down"][0].rearrange("(k p) c -> p k c", p=P)

        def slab(s, k, c):
            return ring[:, s, 0:k * c].rearrange("p (k c) -> p k c", k=k)

        def landed(first, i, s):
            return i * 32 + (first // SLOTS + s // SLOTS + 1) * 16

        def pieces(k0, n):
            at, out = k0 % KD, []
            while n:
                m = min(n, KD - at)
                out.append((k0, at, m))
                k0, at, n = k0 + m, (at + m) % KD, n - m
            return out

        KCH = [(11 * g + o, n) for g in range(4) for o, n in ((0, 4), (4, 4), (8, 3))]

        def last_use(c):
            k0, n = KCH[c]
            old = k0 + n - 1 - KD if k0 >= KD or k0 + n > KD else k0 + n - 1 + 2 * KD
            back = 24 if old >= k0 + n - 1 else 0
            old = min(old, KF - 1)
            j = next(j for j, (k, m) in enumerate(KCH) if k <= old < k + m)
            return 6 * (j // 3) + 3 + j % 3 + 1 - back

        block = ctx.enter_context(nc.Block())

        @block.sync
        def _(sp):
            def ada_loads(i, chunks, slabs=range(8)):
                for s in slabs:
                    if chunks is not None:
                        sp.wait_ge(lo_done, chunks + 2 * s - 6)
                    sp.dma_start(slab(s % SLOTS, 4, 512),
                                 w_ada[:, 4 * (s % 4):4 * (s % 4) + 4, bass.ds(i * 1024 + 512 * (s // 4), 512)]
                                 ).then_inc(full[s % SLOTS], 16)

            def half_loads(w, columns, chunks):
                for s in range(8):
                    sp.wait_ge(lo_done, chunks + 2 * s - 6)
                    sp.dma_start(slab(s % SLOTS, 8, 256),
                                 w[:, 8 * (s % 2):8 * (s % 2) + 8, bass.ds(columns[s // 2], 256)]
                                 ).then_inc(full[s % SLOTS], 16)

            sp.dma_start(con[:, :], a["tables"][:, 0:keep]).then_inc(con_in, 16)
            sp.dma_start(xr[:, 0:2, :], a["x_prompt"][0].rearrange("(t p) d -> p t d", p=P)).then_inc(x_in, 16)
            sp.dma_start(xr[0:NS, 2, :], a["x_sample"].rearrange("b t d -> (b t) d")).then_inc(x_in, 16)
            ada_loads(0, None, range(4))
            ada_loads(0, 0, range(4, 8))
            with sp.Fori(1, 4) as i:
                ada_loads(i, i * 16)
            with sp.Fori(0, 3) as i:
                half_loads(w_in, [i * 1024 + 256 * u for u in range(4)], i * 16 + CH_IN)
            with sp.Fori(0, 8) as i:
                ada_loads(i + 4, i * 16 + CH_ADA2)
            with sp.Fori(0, 3) as i:
                half_loads(w_in, [i * 1024 + (3072 + 256 * u) for u in range(4)], i * 16 + CH_IN2)
            sp.wait_ge(lo_done, CH_OUT)
            with sp.Fori(0, NB // 2) as g:
                for s in range(8):
                    cache = a["cache_k_win" if s < 4 else "cache_v_win"][0]
                    u = s % 4
                    rows = cache[bass.ds(g * 2 + u // 2, 1), :, :, :].rearrange("a s h d -> (a s) (h d)")
                    cols = slice(512 * (u % 2), 512 * (u % 2) + 512)
                    view = slab(u, KT, 512)
                    if s < 4:
                        sp.wait_ge(*ST.upto(f"v{u}", g - 1))
                    else:
                        sp.wait_ge(*ST.upto(f"k{4 * u + 3}", g))
                    far = rows[0:PAST // 2, cols].rearrange("(a r) c -> r a c", r=16)[0:TS]
                    sp.dma_start(view[:, 0, :], far).then_inc(far_in[u], 16)
                    sp.dma_start(view[:, 1:KT, :],
                                 rows[PAST // 2:PAST, cols].rearrange("(n p) c -> p n c", p=P)).then_inc(full[u], 16)
            sp.wait_ge(*ST.upto("v3", 3))
            with sp.Fori(0, 2) as i:
                half_loads(w_out, [i * 1024 + 256 * u for u in range(4)], i * 16 + CH_OUT)
            with sp.Fori(0, 11) as i:
                half_loads(w_up, [i * 512, i * 512 + D_FF, i * 512 + 256, i * 512 + D_FF + 256], i * 16 + CH_UP)
            with sp.Fori(0, 4) as i:
                for s in range(8):
                    kg, h = s // 2, s % 2
                    sp.wait_ge(lo_done, i * 24 + (CH_DOWN + 6 * kg + 3 * h - 6))
                    sp.dma_start(slab(s % SLOTS, 11, 256),
                                 w_down[:, 11 * kg:11 * kg + 11, bass.ds(i * 512 + 256 * h, 256)]
                                 ).then_inc(full[s % SLOTS], 16)

        @block.gpsimd
        def _(pool):
            for s_ in (kv_stored, stp_stored, conv_stored, y_stored):
                pool.sem_inc(s_, 1)
            pool.wait_ge(*PV_.upto("bias_p"))
            pool.dma_start(bias_rows[:, :], btab).then_inc(btab_out, 16)
            pool.wait_ge(btab_out, 16)
            slant = bass.AP(bias_rows[:, :].tensor, P - 1, [[512, H_A], [-1, P], [1, SEQ]])
            pool.dma_start(bias_full[:, :, :], slant).then_inc(slant_out, 16)
            pool.wait_ge(slant_out, 16)
            by_head = bias_full[:, :, :].rearrange("h p c -> p h c")
            with pool.Fori(0, PAIRS // 2) as i:
                for j in range(2):
                    p = i * 2 + j
                    if j == 0:
                        pool.wait_ge(*TV.upto("squares", i * 2))
                    else:
                        pool.wait_ge(*TV.upto("biased", i * 2))
                    pool.sem_inc(pool_turns, 1)
                    pool.dma_start(bias_p[:, j], by_head[:, bass.ds(p * 2, 2), :]).then_inc(biasp_in[j], 16)
                    pool.wait_ge(*TV.upto("krows", p))
                    pool.sem_inc(pool_turns, 1)
                    cols = bass.ds(p * P, P)
                    ko = o["new_k_p"].rearrange("(t s) c -> s t c", s=P)
                    vo = o["new_v_p"].rearrange("(t s) c -> s t c", s=P)
                    pool.dma_start(ko[:, :, cols], krows[:, 0:2, :]).then_inc(k_out, 16)
                    pool.dma_start(o["new_k_s"][:, cols], krows[0:NS, 2, :]).then_inc(k_out, 16)
                    pool.wait_ge(*TV.upto("vrows", p))
                    pool.sem_inc(pool_turns, 1)
                    pool.dma_start(vo[:, :, cols], vrows[:, 0:2, :]).then_inc(v_out, 16)
                    pool.dma_start(o["new_v_s"][:, cols], vrows[0:NS, 2, :]).then_inc(v_out, 16)
                    pool.wait_ge(k_out, i * 64 + (32 * j + 32))
                    pool.wait_ge(v_out, i * 64 + (32 * j + 32))
                    pool.sem_inc(kv_stored, 1)
            pool.wait_ge(v_out, 256)
            pool.wait_ge(*TV.upto("out", PAIRS - 1))
            pool.wait_ge(*TT.upto("kv_rows", PAIRS - 1))
            pool.dma_start(vrow_s, o["new_v_s"]).then_inc(vrow_in, 16)
            pool.wait_ge(*TT.upto("turn_b", PAIRS - 1))
            pool.dma_start(wg2, a["w_gate2"][0]).then_inc(wg2_in, 16)
            pool.wait_ge(*OV.upto("lo"))
            pool.wait_ge(*OA.upto("hi"))
            pool.wait_ge(*ST.upto("oT", 3))
            s_in = a["state_gla"][0].rearrange("b h k v -> k h b v")
            s_out = o["new_gla_s"].rearrange("b h k v -> k h b v")
            pool.dma_start(s0, s_in[:, 0]).then_inc(s0_in, 16)
            with pool.Fori(0, H_B - 1) as h:
                pool.wait_ge(*RA.upto("stp", h))
                pool.sem_inc(pool_turns, 1)
                pool.dma_start(o["new_gla_p"][bass.ds(h, 1)].rearrange("a k v -> (a k) v"), stp).then_inc(stp_out, 16)
                pool.wait_ge(*RV.upto("new_state", h))
                pool.sem_inc(pool_turns, 1)
                pool.dma_start(s_out[:, bass.ds(h, 1)].rearrange("k a b v -> k (a b) v"), s0).then_inc(s0_out, 16)
                pool.wait_ge(stp_out, h * 16 + 16)
                pool.sem_inc(stp_stored, 1)
                pool.wait_ge(s0_out, h * 16 + 16)
                pool.sem_inc(pool_turns, 1)
                pool.dma_start(s0, s_in[:, bass.ds(h + 1, 1)].rearrange("k a b v -> k (a b) v")).then_inc(s0_in, 16)
            pool.wait_ge(*RA.upto("stp", H_B - 1))
            pool.dma_start(o["new_gla_p"][H_B - 1], stp).then_inc(stp_out, 16)
            pool.wait_ge(*RV.upto("new_state", H_B - 1))
            pool.dma_start(s_out[:, H_B - 1], s0).then_inc(s0_out, 16)
            hist = a["state_conv"][0].rearrange("b r c -> (b r) c")
            pool.wait_ge(*NT[1].upto("s3"))
            pool.dma_start(hrow[:, 0], hist[:, 0:512]).then_inc(hist_in[0], 16)

            def history(j, i):
                pool.dma_start(hrow[:, j], hist[:, bass.ds(i * 512, 512)]).then_inc(hist_in[j], 16)

            def conv_rows(i):
                pool.wait_ge(*FA.upto("rows", i))
                pool.sem_inc(pool_turns, 1)
                pool.dma_start(o["new_conv_p"][:, bass.ds(i * 512, 512)], crows[0:2]).then_inc(conv_out, 16)
                pool.dma_start(o["new_conv_s"][:, bass.ds(i * 512, 512)], crows[2:18]).then_inc(conv_out, 16)
                pool.wait_ge(conv_out, i * 32 + 32)
                pool.sem_inc(conv_stored, 1)

            with pool.Fori(0, 5) as i:
                for j in range(2):
                    pool.wait_ge(*FT.upto("hist", i * 2 + (j - 1)))
                    pool.sem_inc(pool_turns, 1)
                    history(1 - j, i * 2 + (j + 1))
                    conv_rows(i * 2 + j)
            conv_rows(10)
            yp = o["y_p"].rearrange("(t s) c -> t s c", s=P)
            pool.sem_inc(pool_turns, 1)
            with pool.Fori(0, 4) as i:
                cols = bass.ds(i * 512, 512)
                for t in range(3):
                    pool.wait_ge(*DA.upto(f"r{t}", i))
                    pool.sem_inc(pool_turns, 1)
                    if t < 2:
                        pool.dma_start(yp[t][:, cols], yrow[:, t, :]).then_inc(y_out, 16)
                        pool.wait_ge(y_out, i * 48 + (16 * t + 16))
                        pool.sem_inc(y_stored, 1)
                    else:
                        pool.dma_start(o["y_s"][:, cols], yrow[0:NS, 0, :]).then_inc(y_out, 16)
                pool.wait_ge(y_out, i * 48 + 48)
                pool.sem_inc(y_stored, 1)
            for s, n in ((y_out, 192), (conv_out, 352), (k_out, 256), (v_out, 256), (stp_out, 64),
                         (s0_out, 64)):
                pool.wait_ge(s, n)

        @block.tensor
        def _(pe):
            mm, turn = nc.tensor.matmul, nc.tensor.transpose
            for s_ in (PT_, *NT, AT, GT, TT, ST, RT, OT, FT, DT):
                pe.sem_inc(s_.sem, len(s_.names))
            pe.sem_inc(used, BUFS)

            pe.wait_ge(con_in, 16)
            pe.wait_ge(temp_in, 16)
            pe.wait_ge(rel_in, 64)
            mm(ps[0:H_A, 0, :], relb[0:NBUCK, :], tview("hot_p", NBUCK), start=True,
               stop=True).then_inc(*PT_.step("bias_p"))
            pe.wait_ge(*PV_.upto("rel_rows"))
            mm(ps[:, 1, :], rel_rows, tview("hot_s", P)[:, 0:512], start=True, stop=True)
            mm(ps[:, 2, 0:160], rel_rows, tview("hot_s", P)[:, 512:672], start=True,
               stop=True).then_inc(*PT_.step("bias_s"))
            pe.wait_ge(vec_in, 16 * 15)
            for t, (n, c) in enumerate(((128, 0), (88, 128), (88, 216), (9, 304))):
                last = turn(ps[:, 3, c:c + n], vrow[0:n, t, :], ident[0:n, 0:n])
            last.then_inc(*PT_.step("vectors"))
            pe.wait_ge(*PA_.upto("silu_c"))
            for k in range(KD):
                last = turn(ps[:, 4, NC9 * k:NC9 * k + NC9], crow[:, P * k:P * k + P], ident[0:NC9, 0:NC9])
            last.then_inc(*PT_.step("c"))
            pe.wait_ge(x_in, 32)
            for k in range(KD):
                if k >= 3:
                    pe.wait_ge(*PV_.upto(f"x{k - 3}"))
                for t in range(3):
                    n = P if t < 2 else NS
                    last = turn(ps[:, 5 + k % 3, P * t:P * t + n], xr[0:n, t, P * k:P * k + P], ident[0:n, 0:n])
                last.then_inc(*PT_.step(f"x{k}"))

            def norm_sums(n, bank):
                for j in range(4):
                    pe.wait_ge(*NA[n].upto(f"q{j}"))
                    for k in range(4):
                        last = mm(ps[:, bank, 0:TOK], ones, sq[:, j % 2, k, :], start=(j + k == 0),
                                  stop=(j == 3 and k == 3))
                    last.then_inc(*NT[n].step(f"s{j}"))

            def ada_chunk(bank, j, chunks):
                pe.wait_ge(lo_done, chunks + j + 1)
                for k in range(2):
                    kk = 2 * (j % 8) + k
                    for n, part in enumerate((whi, wlo)):
                        last = mm(ps[0:2 * NC9, bank, :], c18[:, kk, :], part[:, j % BUFS, 512 * k:512 * k + 512],
                                  start=(kk + n == 0), stop=(kk == KD - 1 and n == 1))
                last.then_inc(used, 1)

            def ada_turn(bank):
                pe.sem_inc(row_turns, 1)
                for n in range(4):
                    last = turn(ps[:, bank, 18 * n:18 * n + 18], mrow[:, P * n:P * n + P],
                                ident[0:2 * NC9, 0:2 * NC9])
                return last

            norm_sums(0, 4)
            pe.wait_ge(*CV.upto("c_lo"))
            with pe.Fori(0, 4) as i:
                pe.wait_ge(*AA.upto("rows_a", i - 1))
                for j in range(8):
                    ada_chunk(0, j, i * 16)
                pe.wait_ge(*AA.upto("rows_b", i - 1))
                for j in range(8, 12):
                    ada_chunk(1, j, i * 16)
                pe.wait_ge(*AA.upto("rows_a", i))
                pe.wait_ge(*AV.upto("mod", i - 1))
                ada_turn(2).then_inc(*AT.step("turn_a"))
                for j in range(12, 16):
                    ada_chunk(1, j, i * 16)
                pe.wait_ge(*AA.upto("rows_b", i))
                ada_turn(3).then_inc(*AT.step("turn_b"))

            def three(out, w_hi, w_lo, x_hi, x_lo, start, stop):
                mm(out, w_hi, x_hi, start=start, stop=False)
                mm(out, w_hi, x_lo, start=False, stop=False)
                return mm(out, w_lo, x_hi, start=False, stop=stop)

            def unit(bank, u, chunks):
                for c in range(4):
                    j = 4 * u + c
                    pe.wait_ge(lo_done, chunks + j + 1)
                    for k in range(4):
                        for n in range(2):
                            w = slice(256 * k + P * n, 256 * k + P * n + P)
                            last = three(ps[:, bank + n, 0:TOK], whi[:, j % BUFS, w], wlo[:, j % BUFS, w],
                                         hhi[:, 4 * c + k, :], hlo[:, 4 * c + k, :], c + k == 0, c + k == 6)
                    last.then_inc(used, 1)

            def input_projection(n, chunks):
                with pe.Fori(0, 3) as i:
                    for u in range(4):
                        if u >= 2:
                            pe.wait_ge(*WV[n].upto(f"u{u - 2}", i))
                        else:
                            pe.wait_ge(*WV[n].upto(f"u{u + 2}", i - 1))
                        unit(2 * (u % 2), u, i * 16 + chunks)

            for j in range(4):
                pe.wait_ge(*NV[0].upto(f"l{j}"))
            pe.wait_ge(*AA.upto("rows_b", 3))
            input_projection(0, CH_IN)

            pe.wait_ge(*WV[0].upto("u3", 2))
            with pe.Fori(0, PAIRS) as p:
                def ada(lo, hi):
                    for j in range(lo, hi):
                        ada_chunk(j // 8, j, p * 16 + CH_ADA2)

                pe.wait_ge(*TA.upto("rows_a", p - 1))
                ada(0, 2)
                pe.wait_ge(*TV.upto("squares", p))
                pe.wait_ge(*TV.upto("out", p - 1))
                for g in range(2):
                    last = mm(ps[:, 4 + g, 0:TOK], halves, sqqk[:, g, :], start=True, stop=True)
                last.then_inc(*TT.step("sums"))
                ada(2, 6)
                pe.wait_ge(*TV.upto("k", p))
                pe.wait_ge(*TA.upto("vstage", p))
                pe.wait_ge(*TA.upto("probT", p - 1))
                for g, src in enumerate((qkst[:, 1, :], vst)):
                    for t in range(3):
                        n = P if t < 2 else NS
                        last = turn(ps[0:n, 6 + g, P * t:P * t + P], src[:, P * t:P * t + n], ident)
                last.then_inc(*TT.step("kv_rows"))
                ada(6, 8)
                for e in range(2):
                    h = slice(HD * e, HD * e + HD)
                    for qt in range(2):
                        last = mm(ps[:, 4 + e, P * qt:P * qt + P * (qt + 1)], qkst[h, 0, P * qt:P * qt + P],
                                  qkst[h, 1, 0:P * (qt + 1)], start=True, stop=True)
                last.then_inc(*TT.step("scores"))
                pe.wait_ge(*TA.upto("rows_b", p - 1))
                ada(8, 11)
                pe.wait_ge(*TA.upto("rows_a", p))
                pe.wait_ge(*TV.upto("mod", p - 1))
                ada_turn(2).then_inc(*TT.step("turn_a"))
                ada(11, 13)
                pe.wait_ge(*TV.upto("norm", p))
                for e in range(2):
                    for n in range(3):
                        last = turn(ps[:, 6 + e, P * n:P * n + P], prob[:, e, P * n:P * n + P], ident)
                last.then_inc(*TT.step("probT"))
                ada(13, 16)
                pe.wait_ge(*TA.upto("probT", p))
                for e in range(2):
                    mm(ps[:, 4 + e, 0:SEQ], vrows[:, 0, :], probT[:, e, 0:SEQ], start=True, stop=False)
                    last = mm(ps[:, 4 + e, P:SEQ], vrows[:, 1, :], probT[:, e, SEQ:3 * P], start=False, stop=True)
                last.then_inc(*TT.step("out"))
                pe.wait_ge(*TA.upto("rows_b", p))
                ada_turn(3).then_inc(*TT.step("turn_b"))

            input_projection(1, CH_IN2)
            pe.wait_ge(*CV.upto("glr_lo"))
            for k in range(KD):
                last = three(ps[0:RANK, 4, 0:TOK], ghi[:, k, :], glo[:, k, :], hhi[:, k, :], hlo[:, k, :],
                             k == 0, k == KD - 1)
            last.then_inc(*GT.step("done"))

            pe.wait_ge(*WV[1].upto("u3", 2))
            pe.wait_ge(*GA.upto("rows"))
            pe.wait_ge(vrow_in, 16)
            with pe.Fori(0, NB // 2) as g:
                def key_turns(n):
                    u, j = n // 4, n % 4
                    if j == 0:
                        pe.wait_ge(far_in[u], g * 32 + 16)
                        pe.wait_ge(full[u], g * 32 + (SL_SAMP // SLOTS * 16 + 16))
                    if n >= 2:
                        pe.wait_ge(*SK.upto(f"k{n - 2}", g))
                    elif n == 0:
                        pe.wait_ge(*SV.upto("out", g - 1))
                    for t in range(KT):
                        last = turn(ps[:, 2 * (n % 2) + t // 4, P * (t % 4):P * (t % 4) + P],
                                    slab(u, KT, 512)[:, t, P * j:P * j + P], ident)
                    last.then_inc(*ST.step(f"k{n}"))

                def scores(n):
                    u, j = n // 4, n % 4
                    if n == 0:
                        pe.wait_ge(*SV.upto("qd", g))
                        pe.wait_ge(*SV.upto("biased", g - 1))
                    pe.wait_ge(*SK.upto(f"k{n}", g))
                    q = qd[:, 32 * n:32 * n + 32]
                    rows = slice(32 * u, 32 * u + 32)
                    mm(ps[rows, 4, :], q, kcT[:, n % 2, 0:512], start=(j == 0), stop=(j == 3))
                    mm(ps[rows, 5, 0:160], q, kcT[:, n % 2, 512:CK + NS], start=(j == 0),
                       stop=(j == 3)).then_inc(*ST.step(f"s{n}"))

                for n in range(16):
                    key_turns(n)
                    if n:
                        scores(n - 1)
                scores(15)
                pe.wait_ge(*SV.upto("norm", g))
                for t in range(KT):
                    turn(ps[:, t // 4, P * (t % 4):P * (t % 4) + P], sc[:, P * t:P * t + P], ident)
                turn(ps[0:NS, 2, 0:P], sc[:, CK:CK + NS], ident).then_inc(*ST.step("probT"))
                pe.wait_ge(*SA.upto("probT", g))
                pe.wait_ge(*SA.upto("orow", g - 1))
                for u in range(4):
                    pe.wait_ge(far_in[u], g * 32 + 32)
                    pe.wait_ge(full[u], g * 32 + (SL_SAMP // SLOTS * 16 + 32))
                    rows = slice(32 * u, 32 * u + 32)
                    for t in range(KT):
                        mm(ps[rows, 7, :], sT[:, t, rows], slab(u, KT, 512)[:, t, :], start=(t == 0), stop=False)
                    mm(ps[rows, 7, :], sT[0:NS, KT, rows], vrow_s[:, 512 * (u % 2):512 * (u % 2) + 512],
                       start=False, stop=True).then_inc(*ST.step(f"v{u}"))
                pe.wait_ge(*SA.upto("orow", g))
                for j in range(4):
                    last = turn(ps[:, 0, P * j:P * j + P], orow[:, P * j:P * j + P], ident)
                last.then_inc(*ST.step("oT"))

            pe.wait_ge(*OA.upto("sq"))
            pe.wait_ge(*SV.upto("out", 3))
            for n in range(PAIRS):
                last = mm(ps[:, n, 0:TOK], halves, projf[:, kv0 + TOK * n:kv0 + TOK * n + TOK], start=True, stop=True)
            last.then_inc(*OT.step("sums"))

            pe.wait_ge(*OV.upto("ms"))
            with pe.Fori(0, H_B) as h:
                pe.wait_ge(*RV.upto("wgs", h))
                pe.wait_ge(*RA.upto("stp", h - 1))
                mm(ps[:, 0, 0:TOK], wgs, glrT, start=True, stop=True).then_inc(*RT.step("z"))
                pe.wait_ge(*RA.upto("vstage", h))
                for t in range(3):
                    n = P if t < 2 else NS
                    for v in range(2):
                        last = turn(ps[0:n, 1 + t // 2, 256 * (t % 2) + P * v:256 * (t % 2) + P * v + P],
                                    vbst[:, v, P * t:P * t + n], ident)
                last.then_inc(*RT.step("vrows"))
                for c in range(8):
                    pe.wait_ge(*RV.upto(f"ki{c}", h))
                    q = qp[:, 32 * c:32 * c + 32]
                    n = min(P, 32 * (c + 1))
                    last = mm(ps[0:n, 3, 32 * c:32 * c + 32], ki[:, c % 2, 0:n], q, start=True, stop=True)
                    if c >= 4:
                        n = 32 * (c - 3)
                        last = mm(ps[0:n, 3, P + 32 * c:P + 32 * c + 32], ki[:, c % 2, P:P + n], q, start=True,
                                  stop=True)
                    last.then_inc(*RT.step(f"att{c}"))
                for t in range(3):
                    n = P if t < 2 else NS
                    last = turn(ps[0:n, 6, P * t:P * t + P], kd[:, P * t:P * t + n], ident)
                last.then_inc(*RT.step("kdrows"))
                mm(ps[0:NS, 7, 0:NS], ke, qe, start=True, stop=True).then_inc(*RT.step("att_s"))
                pe.wait_ge(*RV.upto("att_s", h))
                pe.wait_ge(*RA.upto("vrows", h))
                pe.wait_ge(s0_in, h * 16 + 16)
                for v in range(2):
                    c = slice(P * v, P * v + P)
                    mm(ps[:, 4 + v, 0:SEQ], vbr[:, 0, c], attT[:, 0:SEQ], start=True, stop=False)
                    mm(ps[:, 4 + v, P:SEQ], vbr[:, 1, c], attT[:, SEQ:3 * P], start=False, stop=True)
                    for b in range(NB):
                        mm(ps[:, 4 + v, SEQ + TS * b:SEQ + TS * b + TS], s0[:, b, c],
                           qe[:, TS * b:TS * b + TS], start=(b == 0), stop=False)
                    last = mm(ps[:, 4 + v, SEQ:TOK], vbr[0:NS, 2, c], attS, start=False, stop=True)
                last.then_inc(*RT.step("o"))
                pe.wait_ge(*RV.upto("kdm", h))
                mm(ps[:, 0, 0:DV], kdr[:, 0, :], vbr[:, 0, :], start=True, stop=False)
                mm(ps[:, 0, 0:DV], kdr[:, 1, :], vbr[:, 1, :], start=False, stop=True).then_inc(*RT.step("state"))
                for b in range(NB):
                    bank = (1, 2, 6, 7)[b // 2]
                    last = mm(ps[:, bank, DV * (b % 2):DV * (b % 2) + DV], kdm[:, P * b:P * b + P],
                              vbr[0:NS, 2, :], start=True, stop=True)
                last.then_inc(*RT.step("states"))
                pe.wait_ge(*RA.upto("sq", h))
                for v in range(2):
                    last = mm(ps[:, 3, 0:TOK], ones, sqo[:, v, :], start=(v == 0), stop=(v == 1))
                last.then_inc(*RT.step("sum"))

            pe.wait_ge(*OV.upto("gla_lo"))
            with pe.Fori(0, 2) as i:
                for u in range(4):
                    if u >= 2:
                        pe.wait_ge(*UV.upto(f"u{u - 2}", i))
                    else:
                        pe.wait_ge(*UV.upto(f"u{u + 2}", i - 1))
                    unit(2 * (u % 2), u, i * 16 + CH_OUT)
            norm_sums(1, 4)

            for j in range(4):
                pe.wait_ge(*NV[1].upto(f"l{j}"))

            def up_turn(i, par):
                pe.wait_ge(hist_in[par], i * 8 + (16 - 8 * par))
                pe.wait_ge(*FV.upto("hist", i - 1))
                pe.sem_inc(row_turns, 1)
                for n in range(4):
                    last = turn(ps[:, 4, 16 * n:16 * n + 16], hrow[:, par, P * n:P * n + P], ident[0:16, 0:16])
                last.then_inc(*FT.step("hist"))
                for n in range(2):
                    pe.wait_ge(*FA.upto(f"g{1 - n}", i - 1 + n))
                    unit(0, 2 * n, i * 16 + CH_UP)
                    pe.wait_ge(*FV.upto(f"act{1 - n}", i - 1 + n))
                    unit(2, 2 * n + 1, i * 16 + CH_UP)
                pe.wait_ge(*FV.upto("last", i))
                pe.wait_ge(*FA.upto("rows", i - 1))
                for n in range(4):
                    last = turn(ps[0:18, 5, P * n:P * n + P], glast[:, n, :], ident)
                last.then_inc(*FT.step("rows"))

            with pe.Fori(0, 5) as i:
                for par in range(2):
                    up_turn(i * 2 + par, par)
            up_turn(10, 0)

            pe.wait_ge(*FV.upto("act1", 10))
            pe.wait_ge(*FA.upto("rows", 10))
            with pe.Fori(0, 4) as i:
                for kg in range(4):
                    for h in range(2):
                        if kg == 0:
                            pe.wait_ge(*DV_.upto(f"u{h}", i - 1))
                        for kc in range(3):
                            j, c = 6 * kg + 3 * h + kc, 3 * kg + kc
                            if h == 0:
                                pe.wait_ge(act_lo, i * 12 + (c + 1))
                            pe.wait_ge(lo_done, i * 24 + (CH_DOWN + j + 1))
                            k0, nk = KCH[c]
                            for k in range(nk):
                                for n in range(2):
                                    w = slice(256 * k + P * n, 256 * k + P * n + P)
                                    at = (k0 + k) % KD
                                    last = three(ps[:, 2 * h + n, 0:TOK], whi[:, j % BUFS, w], wlo[:, j % BUFS, w],
                                                 hhi[:, at, :], hlo[:, at, :], k0 + k == 0, k0 + k == KF - 1)
                            last.then_inc(used, 1)
                pe.wait_ge(*DV_.upto("u1", i))
                for t in range(3):
                    m = P if t < 2 else NS
                    pe.wait_ge(*DA.upto(f"r{t}", i - 1))
                    for b in range(4):
                        last = turn(ps[0:m, 4 + t, P * b:P * b + P], yst[:, b, P * t:P * t + m], ident)
                    last.then_inc(*DT.step(f"t{t}"))

        @block.scalar
        def _(act):
            f = nc.scalar.activation
            for s_ in (PA_, *NA, CA, AA, GA, TA, SA, RA, OA, FA, DA):
                act.sem_inc(s_.sem, len(s_.names))
            for r, name in ((slice(0, 1), "c_prompt"), (slice(1, NC9), "c_sample")):
                act.dma_start(crow[r, :], a[name]).then_inc(c_in, 16)
            act.dma_start(temp, a["tables"][:, c0:cn[0] + cn[1]]).then_inc(temp_in, 16)
            for t in range(4):
                act.dma_start(relb[32 * t:32 * t + 32, :], a["rel_bias"]).then_inc(rel_in, 16)
            for dst, src in [
                    (vrow[0:16, 0, :], a["norm1_g"]), (vrow[16:32, 0, :], a["norm2_g"]), (vrow[32:128, 0, :], a["b_ada"]),
                    (vrow[0:44, 1, :], a["conv_w"][0, 0:1, :]), (vrow[44:88, 1, :], a["conv_w"][0, 1:2, :]),
                    (vrow[0:44, 2, :], a["conv_w"][0, 2:3, :]), (vrow[44:88, 2, :], a["conv_b"]),
                    (vrow[3:5, 3, :], a["gla_out_g"]), (vrow[5:9, 3, :], a["b_gate2"])]:
                act.dma_start(dst, src.rearrange("a (n p) -> (a n) p", p=P)).then_inc(vec_in, 16)
            for j, name in enumerate(("q_norm_g", "k_norm_g", "a_out_g")):
                for e in range(2):
                    act.dma_start(vrow[j:j + 1, 3, HD * e:HD * e + HD], a[name]).then_inc(vec_in, 16)
            act.dma_start(wglr, w_in[:, :, 6144:6160]).then_inc(wglr_in, 16)
            act.wait_ge(c_in, 32)
            f(crow, crow, ACT.Silu).then_inc(*PA_.step("silu_c"))

            def norm_squares(n):
                for j in range(4):
                    if n == 0:
                        act.wait_ge(*PV_.upto(f"x{4 * j + 3}"))
                    if j >= 2:
                        act.wait_ge(*NT[n].upto(f"s{j - 2}"))
                    f(sq[:, j % 2], xT[:, 4 * j:4 * j + 4, :], ACT.Square).then_inc(*NA[n].step(f"q{j}"))
                act.wait_ge(*NV[n].upto("ms"))
                f(rs, rs, ACT.Ln).then_inc(*NA[n].step("ln"))
                act.wait_ge(*NA[n].upto("ln"))
                f(rs, rs, ACT.Exp, scale=-0.5).then_inc(*NA[n].step("rs"))

            def norm_hi(n):
                for j in range(4):
                    k = slice(4 * j, 4 * j + 4)
                    act.wait_ge(*NV[n].upto(f"d{j}"))
                    f(hhi[:, k, :], hraw[:, k, :], ACT.Copy).then_inc(*NA[n].step(f"h{j}"))

            def hi(i, j, slabs, chunks):
                s = j // 2
                act.wait_ge(full[s % SLOTS], landed(slabs, i, s))
                act.wait_ge(used, i * 16 + (chunks + j + 1))
                f(whi[:, j % BUFS, :], ring[:, s % SLOTS, CHUNK * (j % 2):CHUNK * (j % 2) + CHUNK],
                  ACT.Copy).then_inc(hi_done, 1)

            def spent(i, chunks, j, eng=act):
                eng.wait_ge(used, i * 16 + (chunks + BUFS + j))

            act.wait_ge(*PV_.upto("c"))
            f(c18[:, :, 0:NC9], cT, ACT.Copy).then_inc(*CA.step("c_hi"))
            act.wait_ge(wglr_in, 16)
            f(ghi[:, :, :], wglr, ACT.Copy).then_inc(*CA.step("glr_hi"))
            norm_squares(0)
            for j in range(LEAD):
                hi(0, j, 0, 0)
            with act.Fori(0, 4) as i:
                for j in range(LEAD, 10):
                    hi(i, j, 0, 0)
                spent(i, 0, 8)
                act.wait_ge(*AT.upto("turn_b", i - 1))
                f(mrow[:, :], ps[0:2 * NC9, 0, :], ACT.Copy).then_inc(*AA.step("rows_a"))
                for j in range(10, 16 + LEAD):
                    hi(i, j, 0, 0)
                spent(i, 0, 16)
                act.wait_ge(*AT.upto("turn_a", i))
                f(mrow[:, :], ps[0:2 * NC9, 1, :], ACT.Copy).then_inc(*AA.step("rows_b"))
            norm_hi(0)

            def input_evac(n, u, i, chunks):
                spent(i, chunks, 4 * u + 4)
                act.wait_ge(*WV[n].upto("u1" if u else "u3", i if u else i - 1))
                f(proj[:, bass.ds(i * 8 + (24 * n + 2 * u), 2), :], ps[:, 0:2, 0:TOK], ACT.Copy).then_inc(WV[n].sem, 1)

            def input_turn(n, i, slabs, chunks, lead):
                for j in range(LEAD, 16 + lead):
                    hi(i, j, slabs, chunks)
                    if j in (5, 13):
                        input_evac(n, (j - 5) // 4, i, chunks)

            with act.Fori(0, 3) as i:
                input_turn(0, i, SL_IN, CH_IN, LEAD)

            with act.Fori(0, PAIRS) as p:
                def his(lo, end):
                    for j in range(lo, end):
                        hi(p, j, SL_ADA2, CH_ADA2)

                his(2, 6)
                act.wait_ge(*TV.upto("ms", p))
                f(rsqk, rsqk, ACT.Ln).then_inc(*TA.step("ln"))
                act.wait_ge(*TA.upto("ln", p))
                f(rsqk, rsqk, ACT.Exp, scale=-0.5).then_inc(*TA.step("rs"))
                act.wait_ge(*TT.upto("kv_rows", p - 1))
                f(vst, proj[:, bass.ds(p + 16, 1), :].rearrange("p a c -> p (a c)"),
                  ACT.Copy).then_inc(*TA.step("vstage"))
                his(6, 10)
                spent(p, CH_ADA2, 8)
                act.wait_ge(*TT.upto("turn_b", p - 1))
                f(mrow[:, :], ps[0:2 * NC9, 0, :], ACT.Copy).then_inc(*TA.step("rows_a"))
                his(10, 13)
                act.wait_ge(*TV.upto("max", p))
                for e in range(2):
                    for q in range(2):
                        part = prob[:, e, P * q:P * q + P * (q + 1)]
                        c = 2 * e + q
                        last = f(part, part, ACT.Exp, bias=stat[:, c:c + 1], accum_out=stat[:, 4 + c:5 + c])
                last.then_inc(*TA.step("exp"))
                his(13, 16)
                act.wait_ge(*TT.upto("probT", p))
                act.wait_ge(*TT.upto("out", p - 1))
                f(probT, ps[:, 6:8, 0:384], ACT.Copy).then_inc(*TA.step("probT"))
                his(16, 18)
                spent(p, CH_ADA2, 16)
                act.wait_ge(*TT.upto("turn_a", p))
                f(mrow[:, :], ps[0:2 * NC9, 1, :], ACT.Copy).then_inc(*TA.step("rows_b"))

            act.wait_ge(kv_stored, PAIRS + 1)
            act.wait_ge(*TV.upto("mod", PAIRS - 1))
            with act.Fori(0, 2) as i:
                input_turn(1, i, SL_IN2, CH_IN2, LEAD)
            input_turn(1, 2, SL_IN2, CH_IN2, 0)
            act.wait_ge(*GT.upto("done"))
            act.wait_ge(*TV.upto("out", PAIRS - 1))
            f(glrT, ps[0:RANK, 4, 0:TOK], ACT.Copy).then_inc(*GA.step("rows"))
            act.wait_ge(*WV[1].upto("u3", 2))
            f(proj[:, 40:48, :], proj[:, 40:48, :], ACT.Silu).then_inc(*GA.step("silu_r"))

            with act.Fori(0, NB // 2) as g:
                for n in range(0, 16, 2):
                    act.wait_ge(*ST.upto(f"k{n}", g))
                    if n >= 2:
                        act.wait_ge(*ST.upto(f"s{n - 2}", g))
                    act.wait_ge(*SK.upto(f"k{n - 1 if n else 15}", g if n else g - 1))
                    f(kcT[:, 0, 0:512], ps[:, 0, :], ACT.Copy)
                    f(kcT[:, 0, CK:CK + NS], kS[:, 4 * (n // 4 % 2) + n % 4, :], ACT.Copy)
                    f(kcT[:, 0, 512:CK], ps[:, 1, 0:P], ACT.Copy).then_inc(SK.sem, 1)
                act.wait_ge(*SV.upto("max", g))
                f(sc, sc, ACT.Exp, bias=stat[:, 0:1], accum_out=stat[:, 1:2]).then_inc(*SA.step("exp"))
                act.wait_ge(*ST.upto("probT", g))
                act.wait_ge(*ST.upto("v3", g - 1))
                f(sT[:, 0:4, :].rearrange("p t c -> p (t c)"), ps[:, 0, :], ACT.Copy)
                f(sT[:, 4, :], ps[:, 1, 0:P], ACT.Copy)
                f(sT[0:NS, 5, :], ps[0:NS, 2, 0:P], ACT.Copy).then_inc(*SA.step("probT"))
                act.wait_ge(*ST.upto("v3", g))
                act.wait_ge(*ST.upto("oT", g - 1))
                f(orow, ps[:, 7, :], ACT.Copy).then_inc(*SA.step("orow"))

            att8 = slice(kv0, kv0 + 8 * TOK)
            act.wait_ge(*SV.upto("out", 3))
            f(projf[:, att8], projf[:, 0:8 * TOK], ACT.Square).then_inc(*OA.step("sq"))
            act.wait_ge(*OV.upto("ms"))
            f(projf[:, att8], projf[:, att8], ACT.Ln).then_inc(*OA.step("ln"))
            act.wait_ge(*OA.upto("ln"))
            f(projf[:, att8], projf[:, att8], ACT.Exp, scale=-0.5).then_inc(*OA.step("rs"))
            act.wait_ge(*OV.upto("done"))
            f(hhi[:, 0:8, :], proj[:, 0:8, :], ACT.Copy).then_inc(*OA.step("hi"))
            act.wait_ge(*OV.upto("lo"))

            with act.Fori(0, H_B) as h:
                cum, cums = cumz[:, 1:1 + SEQ], cumz[:, 1 + SEQ:1 + TOK]
                act.wait_ge(*RT.upto("vrows", h - 1))
                f(vbst, proj[:, bass.ds(h * 2 + 32, 2), :], ACT.Copy).then_inc(*RA.step("vstage"))
                act.wait_ge(*RV.upto("z", h))
                f(ex, zb, ACT.Abs).then_inc(*RA.step("abs"))
                act.wait_ge(*RA.upto("abs", h))
                f(ex, ex, ACT.Exp, scale=-1.0).then_inc(*RA.step("exp"))
                act.wait_ge(*RA.upto("exp", h))
                f(ex, ex, ACT.Ln, bias=1.0).then_inc(*RA.step("ln"))
                act.wait_ge(*RT.upto("vrows", h))
                act.wait_ge(*RV.upto("o1", h - 1))
                f(vbr[:, 0:2, :].rearrange("p t c -> p (t c)"), ps[:, 1, :], ACT.Copy)
                f(vbr[0:NS, 2, :], ps[0:NS, 2, 0:256], ACT.Copy).then_inc(*RA.step("vrows"))
                act.wait_ge(*RV.upto("dd", h))
                f(qp, qp, ACT.Exp, scale=1 / TAU).then_inc(*RA.step("eq"))
                f(qe, cums, ACT.Exp, scale=1 / TAU).then_inc(*RA.step("eqs"))
                f(ke, cums, ACT.Exp, scale=-1 / TAU).then_inc(*RA.step("eks"))
                f(kd[:, 0:SEQ], cum, ACT.Exp, scale=-1 / TAU, bias=rb[:, 8:9]).then_inc(*RA.step("ekd"))
                f(kd[:, SEQ:TOK], kd[:, SEQ:TOK], ACT.Exp, scale=1 / TAU).then_inc(*RA.step("ekds"))
                f(dec, cums.rearrange("p (b t) -> p b t", t=TS)[:, :, TS - 1], ACT.Exp,
                  scale=1 / TAU).then_inc(*RA.step("dec"))
                for c in range(8):
                    if c >= 2:
                        act.wait_ge(*RT.upto(f"att{c - 2}", h))
                    n = 32 * (c + 1)
                    f(ki[:, c % 2, 0:n], cum[:, 0:n], ACT.Exp, scale=-1 / TAU,
                      bias=rb[:, c:c + 1]).then_inc(*RA.step(f"ki{c}"))
                act.wait_ge(*RT.upto("o", h))
                for v in range(2):
                    last = f(sqo[:, v, :], ps[:, 4 + v, 0:TOK], ACT.Square)
                last.then_inc(*RA.step("sq"))
                act.wait_ge(*RT.upto("state", h))
                act.wait_ge(stp_stored, h + 1)
                f(stp, ps[:, 0, 0:DV], ACT.Copy).then_inc(*RA.step("stp"))
                act.wait_ge(*RV.upto("ms", h))
                f(rso, rso, ACT.Ln).then_inc(*RA.step("lnr"))
                act.wait_ge(*RA.upto("lnr", h))
                f(rso, rso, ACT.Exp, scale=-0.5).then_inc(*RA.step("rs"))
            act.wait_ge(*RV.upto("o1", 3))
            f(hhi[:, 8:16, :], proj[:, 40:48, :], ACT.Copy).then_inc(*OA.step("gla_hi"))

            for j in range(LEAD):
                hi(0, j, SL_OUT, CH_OUT)
            with act.Fori(0, 2) as i:
                for j in range(LEAD, 16 + LEAD):
                    hi(i, j, SL_OUT, CH_OUT)
            act.wait_ge(*UV.upto("u3", 1))
            act.wait_ge(s0_out, 64)
            act.wait_ge(stp_out, 64)
            norm_squares(1)
            norm_hi(1)

            with act.Fori(0, 11) as i:
                def his(lo, end):
                    for j in range(lo, end):
                        hi(i, j, SL_UP, CH_UP)

                def gate(n):
                    spent(i, CH_UP, 8 * n + 4)
                    act.wait_ge(*FV.upto("last", i - 1))
                    f(gpad[:, 2 * n:2 * n + 2, 2:2 + SEQ], ps[:, 0:2, 0:SEQ], ACT.Copy)
                    f(gpad[:, 2 * n:2 * n + 2, 2 + SEQ:GW].rearrange("p n (b t) -> p n b t", t=6)[:, :, :, 2:6],
                      ps[:, 0:2, SEQ:TOK].rearrange("p n (b t) -> p n b t", t=TS),
                      ACT.Copy).then_inc(*FA.step(f"g{n}"))

                def silu(n):
                    act.wait_ge(*FV.upto(f"conv{n}", i))
                    f(cv, cv, ACT.Silu).then_inc(*FA.step(f"silu{n}"))

                his(2, 6)
                gate(0)
                his(6, 8)
                silu(0)
                his(8, 14)
                gate(1)
                his(14, 16)
                silu(1)
                his(16, 18)
                act.wait_ge(*FT.upto("rows", i))
                act.wait_ge(conv_stored, i + 1)
                f(crows, ps[0:18, 5, :], ACT.Copy).then_inc(*FA.step("rows"))

            def act_parts(c, wait, i):
                act.wait_ge(used, wait)
                for k0, at, m in pieces(*KCH[c]):
                    last = f(hhi[:, at:at + m, :], actT[:, k0:k0 + m, :], ACT.Copy)
                last.then_inc(act_hi, 1)

            def down_hi(i, j):
                jj = j % 24
                kg, h, kc = jj // 6, jj // 3 % 2, jj % 3
                s = 2 * kg + h
                act.wait_ge(full[s % SLOTS], i * 32 + (SL_DOWN // SLOTS * 16 + 32 * (j // 24) + 16 * (s // SLOTS) + 16))
                act.wait_ge(used, i * 24 + (CH_DOWN + j + 1))
                n = 256 * KCH[3 * kg + kc][1]
                f(whi[:, jj % BUFS, 0:n], ring[:, s % SLOTS, CHUNK * kc:CHUNK * kc + n],
                  ACT.Copy).then_inc(hi_done, 1)

            def down_turn(i, end):
                for j in range(LEAD, end):
                    jj = j % 24
                    if jj // 3 % 2 == 0:
                        c = 3 * (jj // 6) + jj % 3
                        act_parts(c, i * 24 + (CH_DOWN + BUFS + 24 * (j // 24) + last_use(c)), i)
                    down_hi(i, j)

            act.wait_ge(*FV.upto("act1", 10))
            spent(0, CH_DOWN, 0)
            for c in range(LEAD):
                act_parts(c, CH_DOWN + BUFS, 0)
            with act.Fori(0, 3) as i:
                down_turn(i, 24 + LEAD)
                for t in range(3):
                    act.wait_ge(*DT.upto(f"t{t}", i))
                    act.wait_ge(y_stored, i * 3 + (t if t else 1))
                    m = P if t < 2 else NS
                    f(yrow[0:m, t % 2, :], ps[0:m, 4 + t, :], ACT.Copy).then_inc(*DA.step(f"r{t}"))
            down_turn(3, 24)
            for t in range(3):
                act.wait_ge(*DT.upto(f"t{t}", 3))
                act.wait_ge(y_stored, 9 + (t if t else 1))
                m = P if t < 2 else NS
                f(yrow[0:m, t % 2, :], ps[0:m, 4 + t, :], ACT.Copy).then_inc(*DA.step(f"r{t}"))

        @block.vector
        def _(dve):
            v = nc.vector
            for s_ in (PV_, *NV, CV, AV, *WV, TV, SV, SK, RV, OV, UV, FV, FZ, DV_):
                dve.sem_inc(s_.sem, len(s_.names))
            v.memset(rel_rows, 0.0).then_inc(*PV_.step("zero_rel"))
            dve.wait_ge(*PV_.upto("zero_rel"))
            dve.wait_ge(rel_in, 64)
            for t in range(TS):
                b = slice(32 * t, 32 * t + 32)
                dst = rel_rows[b, :].rearrange("p (b h t) -> p b h t", b=2, h=H_A)[:, :, :, t]
                src = relb[b, :].rearrange("p (a h) -> p a h", a=1).to_broadcast([32, 2, H_A])
                last = v.tensor_copy(dst, src)
            last.then_inc(*PV_.step("rel_rows"))
            dve.wait_ge(*PT_.upto("bias_p"))
            v.tensor_tensor(btab, ps[0:H_A, 0, :], tview("mult_p", H_A), ALU.add).then_inc(*PV_.step("bias_p"))
            dve.wait_ge(*PT_.upto("bias_s"))
            ms = tview("mult_s", P)
            v.tensor_tensor(bias_s[:, 0:512], ps[:, 1, :], ms[:, 0:512], ALU.add)
            v.tensor_tensor(bias_s[:, 512:CK], ps[:, 2, 0:P], ms[:, 512:CK], ALU.add).then_inc(*PV_.step("bias_s0"))
            new = ps[:, 2, P:P + NS].rearrange("p (a c) -> p a c", a=1).to_broadcast([P, 4, NS])
            v.tensor_tensor(bias_s[:, CK:].rearrange("p (g c) -> p g c", g=4), new,
                            ms[:, CK:].rearrange("p (g c) -> p g c", g=4), ALU.add).then_inc(*PV_.step("bias_s"))
            dve.wait_ge(*PT_.upto("vectors"))
            v.tensor_copy(small[:, :], ps[:, 3, 0:313]).then_inc(*PV_.step("vectors"))
            dve.wait_ge(*PT_.upto("c"))
            v.tensor_copy(cT.rearrange("p k c -> p (k c)"), ps[:, 4, 0:KD * NC9]).then_inc(*PV_.step("c"))
            for k in range(KD):
                dve.wait_ge(*PT_.upto(f"x{k}"))
                v.tensor_copy(xT[:, k, :], ps[:, 5 + k % 3, 0:TOK]).then_inc(*PV_.step(f"x{k}"))
            dve.wait_ge(*CA.upto("c_hi"))
            v.tensor_tensor(c18[:, :, NC9:2 * NC9], cT, c18[:, :, 0:NC9].bitcast(F32),
                            ALU.subtract).then_inc(*CV.step("c_lo"))
            dve.wait_ge(*CA.upto("glr_hi"))
            v.tensor_tensor(glo[:, :, :], wglr, ghi[:, :, :].bitcast(F32), ALU.subtract).then_inc(*CV.step("glr_lo"))

            def lo(i, j, chunks):
                s = j // 2
                dve.wait_ge(hi_done, i * 16 + (chunks + j + 1))
                v.tensor_tensor(wlo[:, j % BUFS, :], ring[:, s % SLOTS, CHUNK * (j % 2):CHUNK * (j % 2) + CHUNK],
                                whi[:, j % BUFS, :].bitcast(F32), ALU.subtract).then_inc(lo_done, 1)

            def spent(i, chunks, j):
                dve.wait_ge(used, i * 16 + (chunks + BUFS + j))

            def mod(group, steps, i):
                tiles = [(bass.ds(group * 8 + 4 * n, 4), ps[:, 2 + n, 0:72].rearrange("p (n c) -> p n c", n=4))
                         for n in range(2)]
                for n, (t, src) in enumerate(tiles):
                    bias = small[:, bass.ds(group * 8 + (BA + 4 * n), 4)].rearrange("p (n a) -> p n a", a=1)
                    last = v.tensor_tensor(modT[:, t, :], src[:, :, 0:NC9], bias.to_broadcast([P, 4, NC9]), ALU.add)
                last.then_inc(*steps.step("base"))
                dve.wait_ge(*steps.upto("base", i))
                for t, src in tiles:
                    last = v.tensor_tensor(modT[:, t, :], src[:, :, NC9:2 * NC9], modT[:, t, :], ALU.add)
                last.then_inc(*steps.step("mod"))

            def norm_mean(n, bank):
                dve.wait_ge(*NT[n].upto("s3"))
                v.tensor_scalar(rs, ps[:, bank, 0:TOK], 1 / D, EPS, ALU.mult, ALU.add).then_inc(*NV[n].step("ms"))

            def norm(n):
                sh, scl, g = (0, KD, N1) if n == 0 else (3 * KD, 4 * KD, N2)
                N = NV[n]
                gain = small[:, g:g + KD].rearrange("p (k a) -> p k a", a=1).to_broadcast([P, KD, NC9])
                v.scalar_tensor_tensor(out=modT[:, scl:scl + KD, :], in0=modT[:, scl:scl + KD, :], scalar=1.0,
                                       in1=gain, op0=ALU.add, op1=ALU.mult).then_inc(*N.step("scale"))
                dve.wait_ge(*NA[n].upto("rs"))
                r = rs.rearrange("p (a c) -> p a c", a=1).to_broadcast([P, 4, TOK])
                dve.wait_ge(*N.upto("scale"))
                for j in range(4):
                    ks = slice(4 * j, 4 * j + 4)
                    v.tensor_tensor(hraw[:, ks, :], xT[:, ks, :], r, ALU.mult).then_inc(*N.step(f"t{j}"))
                    dve.wait_ge(*N.upto(f"t{j}"))
                    for k in range(4 * j, 4 * j + 4):
                        last = v.tensor_scalar(hraw[:, k, 0:SEQ], hraw[:, k, 0:SEQ], modT[:, scl + k, 0:1],
                                               modT[:, sh + k, 0:1], ALU.mult, ALU.add)
                    last.then_inc(*N.step(f"p{j}"))
                    hs = hraw[:, ks, SEQ:TOK].rearrange("p k (b t) -> p k b t", t=TS)
                    for k0, name in ((scl, f"s{j}"), (sh, f"d{j}")):
                        m = modT[:, k0 + 4 * j:k0 + 4 * j + 4, 1:NC9].rearrange("p k (b a) -> p k b a", a=1)
                        v.tensor_tensor(hs, hs, m.to_broadcast([P, 4, NB, TS]),
                                        ALU.mult if k0 == scl else ALU.add).then_inc(*N.step(name))
                        dve.wait_ge(*N.upto(name))
                    dve.wait_ge(*NA[n].upto(f"h{j}"))
                    v.tensor_tensor(hlo[:, ks, :], hraw[:, ks, :], hhi[:, ks, :].bitcast(F32),
                                    ALU.subtract).then_inc(*N.step(f"l{j}"))

            norm_mean(0, 4)
            for j in range(LEAD):
                lo(0, j, 0)
            with dve.Fori(0, 4) as i:
                for j in range(LEAD, 16 + LEAD):
                    lo(i, j, 0)
                dve.wait_ge(*AT.upto("turn_b", i))
                mod(i, AV, i)
            dve.wait_ge(*AV.upto("mod", 3))
            norm(0)

            def input_turn(n, i, chunks, lead):
                for j in range(LEAD, 16 + lead):
                    lo(i, j, chunks)
                    if j == 9 or j == 15 + lead:
                        u = 1 if j == 9 else 3
                        spent(i, chunks, 4 * u + 4)
                        dve.wait_ge(*WV[n].upto(f"u{u - 1}", i))
                        v.tensor_copy(proj[:, bass.ds(i * 8 + (24 * n + 2 * u), 2), :],
                                      ps[:, 2:4, 0:TOK]).then_inc(WV[n].sem, 1)

            with dve.Fori(0, 3) as i:
                input_turn(0, i, CH_IN, LEAD)

            pg = proj[:, :, :].rearrange("p (g n) c -> p g n c", n=8)
            dve.wait_ge(*WV[0].upto("u3", 2))
            with dve.Fori(0, PAIRS // 2) as i:
                for par in range(2):
                    p = i * 2 + par

                    def los(first, end):
                        for j in range(first, end):
                            lo(p, j, CH_ADA2)

                    qk = pg[:, 0:2, bass.ds(p, 1), :].rearrange("p g a c -> p g (a c)")
                    v.tensor_tensor(sqqk, qk, qk, ALU.mult).then_inc(*TV.step("squares"))
                    los(2, 6)
                    dve.wait_ge(*TT.upto("sums", p))
                    v.tensor_scalar(rsqk, ps[:, 4:6, 0:TOK], 1 / HD, EPS, ALU.mult, ALU.add).then_inc(*TV.step("ms"))
                    dve.wait_ge(*TA.upto("rs", p))
                    for g, name in enumerate("qk"):
                        v.scalar_tensor_tensor(
                            out=qkst[:, g, :], in0=proj[:, bass.ds(p + 8 * g, 1), :].rearrange("p a c -> p (a c)"),
                            scalar=small[:, QG + g:QG + g + 1], in1=rsqk[:, g, :], op0=ALU.mult,
                            op1=ALU.mult).then_inc(*TV.step(name))
                    dve.wait_ge(*TV.upto("k", p))
                    for g, dst in enumerate((qS, kS)):
                        last = v.tensor_copy(dst[:, bass.ds(p, 1), :].rearrange("p a c -> p (a c)"),
                                             qkst[:, g, SEQ:TOK])
                    last.then_inc(*TV.step("samples"))
                    los(6, 8)
                    dve.wait_ge(*TT.upto("kv_rows", p))
                    for g, (dst, name) in enumerate(((krows, "krows"), (vrows, "vrows"))):
                        dve.wait_ge(kv_stored, p + 1)
                        v.tensor_copy(dst[:, 0:2, :], ps[:, 6 + g, 0:256].rearrange("p (t c) -> p t c", t=2))
                        v.tensor_copy(dst[0:NS, 2, :], ps[0:NS, 6 + g, 256:384]).then_inc(*TV.step(name))
                    los(8, 10)
                    dve.wait_ge(*TT.upto("scores", p))
                    dve.wait_ge(biasp_in[par], i * 16 + 16)
                    for e in range(2):
                        v.scalar_tensor_tensor(out=prob[:, e, 0:P], in0=ps[:, 4 + e, 0:P], scalar=HD ** -0.5,
                                               in1=bias_p[:, par, e, P:SEQ], op0=ALU.mult, op1=ALU.add)
                        last = v.scalar_tensor_tensor(out=prob[:, e, P:3 * P], in0=ps[:, 4 + e, P:3 * P],
                                                      scalar=HD ** -0.5, in1=bias_p[:, par, e, :], op0=ALU.mult,
                                                      op1=ALU.add)
                    last.then_inc(*TV.step("biased"))
                    dve.wait_ge(*TV.upto("biased", p))
                    for e in range(2):
                        for q in range(2):
                            c = 2 * e + q
                            last = v.tensor_reduce(out=stat[:, c:c + 1], in_=prob[:, e, P * q:P * q + P * (q + 1)],
                                                   axis=AX_X, op=ALU.max, negate=True)
                    last.then_inc(*TV.step("max"))
                    los(10, 13)
                    dve.wait_ge(*TA.upto("exp", p))
                    v.reciprocal(stat[:, 8:12], stat[:, 4:8]).then_inc(*TV.step("recip"))
                    dve.wait_ge(*TV.upto("recip", p))
                    for e in range(2):
                        for q in range(2):
                            c = 2 * e + q
                            part = prob[:, e, P * q:P * q + P * (q + 1)]
                            last = v.tensor_scalar(part, part, stat[:, 8 + c:9 + c], None, ALU.mult)
                    last.then_inc(*TV.step("norm"))
                    los(13, 18)
                    dve.wait_ge(*TT.upto("out", p))
                    dve.sem_inc(copy_turns, 1)
                    for e in range(2):
                        h = slice(HD * e, HD * e + HD)
                        last = v.tensor_copy(proj[h, bass.ds(p, 1), 0:SEQ].rearrange("p a c -> p (a c)"),
                                             ps[h, 4 + e, 0:SEQ])
                    last.then_inc(*TV.step("out"))
                    dve.wait_ge(*TT.upto("turn_b", p))
                    mod(p + 4, TV, p)

            dve.wait_ge(kv_stored, PAIRS + 1)
            with dve.Fori(0, 2) as i:
                input_turn(1, i, CH_IN2, LEAD)
            input_turn(1, 2, CH_IN2, 0)

            dve.wait_ge(*PV_.upto("bias_s"))
            dve.wait_ge(*TT.upto("kv_rows", PAIRS - 1))
            dve.wait_ge(*SV.upto("out", -1))
            v.memset(qd, 0.0).then_inc(*FZ.step("zero_qd"))
            dve.wait_ge(*FZ.upto("zero_qd"))
            with dve.Fori(0, NB // 2) as g:
                dve.wait_ge(*ST.upto("s15", g - 1))
                for e in range(2):
                    h = slice(HD * e, HD * e + HD)
                    for b in range(2):
                        src = qS[h, :, bass.ds(g * 8 + TS * b, TS)].rearrange("p (h j) t -> p h j t", h=2)
                        last = v.tensor_copy(qd_blocks(qd, h, 256 * b + TS * e), src)
                last.then_inc(*SV.step("qd"))
                for n in range(1, 16, 2):
                    dve.wait_ge(*ST.upto(f"k{n}", g))
                    if n >= 2:
                        dve.wait_ge(*ST.upto(f"s{n - 2}", g))
                    dve.wait_ge(*SK.upto(f"k{n - 1}", g))
                    v.tensor_copy(kcT[:, 1, 0:512], ps[:, 2, :])
                    v.tensor_copy(kcT[:, 1, CK:CK + NS], kS[:, 4 * (n // 4 % 2) + n % 4, :])
                    v.tensor_copy(kcT[:, 1, 512:CK], ps[:, 3, 0:P]).then_inc(SK.sem, 1)
                dve.wait_ge(*ST.upto("s15", g))
                sd = HD ** -0.5
                for out, src, bias in ((sc[:, 0:512], ps[:, 4, :], bias_s[:, 0:512]),
                                       (sc[:, 512:CK], ps[:, 5, 0:P], bias_s[:, 512:CK]),
                                       (sc[:, CK:CK + NS], ps[:, 5, P:160], bias_s[:, bass.ds(g * NS + CK, NS)])):
                    last = v.scalar_tensor_tensor(out=out, in0=src, scalar=sd, in1=bias, op0=ALU.mult, op1=ALU.add)
                last.then_inc(*SV.step("biased"))
                dve.wait_ge(*SV.upto("biased", g))
                v.tensor_reduce(out=stat[:, 0:1], in_=sc, axis=AX_X, op=ALU.max,
                                negate=True).then_inc(*SV.step("max"))
                dve.wait_ge(*SA.upto("exp", g))
                v.reciprocal(stat[:, 2:3], stat[:, 1:2]).then_inc(*SV.step("recip"))
                dve.wait_ge(*SV.upto("recip", g))
                v.tensor_scalar(sc, sc, stat[:, 2:3], None, ALU.mult).then_inc(*SV.step("norm"))
                dve.wait_ge(*ST.upto("oT", g))
                for e in range(2):
                    h = slice(HD * e, HD * e + HD)
                    for u in range(4):
                        b = u // 2
                        last = v.tensor_copy(
                            proj[h, 4 * (u % 2):4 * (u % 2) + 4, bass.ds(g * 8 + (SEQ + TS * b), TS)],
                            own_heads(ps, h, 32 * u + TS * e))
                last.then_inc(*SV.step("out"))

            dve.wait_ge(*OT.upto("sums"))
            q8 = projf[:, kv0:kv0 + 8 * TOK].rearrange("p (n c) -> p n c", n=8)
            v.tensor_scalar(q8, ps[:, :, 0:TOK], 1 / HD, EPS, ALU.mult, ALU.add).then_inc(*OV.step("ms"))
            dve.wait_ge(*OA.upto("rs"))
            v.scalar_tensor_tensor(out=projf[:, 0:8 * TOK], in0=projf[:, 0:8 * TOK], scalar=small[:, AO:AO + 1],
                                   in1=projf[:, kv0:kv0 + 8 * TOK], op0=ALU.mult,
                                   op1=ALU.mult).then_inc(*OV.step("done"))
            dve.wait_ge(*OA.upto("hi"))
            v.tensor_tensor(hlo[:, 0:8, :], proj[:, 0:8, :], hhi[:, 0:8, :].bitcast(F32),
                            ALU.subtract).then_inc(*OV.step("lo"))

            dve.wait_ge(*OV.upto("lo"))
            kept = keep_g[:, SEQ:TOK].rearrange("p (b t) -> p b t", t=TS)
            v.memset(cumz[:, 0:1], 0.0)
            v.memset(keep_g[:, 0:SEQ], 1.0)
            v.memset(kept[:, :, 1:TS], 1.0)
            v.memset(kept[:, :, 0:1], 0.0).then_inc(*FZ.step("keep"))
            dve.wait_ge(*FZ.upto("keep"))
            dve.wait_ge(wg2_in, 16)
            with dve.Fori(0, H_B) as h:
                cum = cumz[:, 1:1 + TOK]
                qb = proj[:, bass.ds(h + 24, 1), :].rearrange("p a c -> p (a c)")
                kb = proj[:, bass.ds(h + 28, 1), :].rearrange("p a c -> p (a c)")
                dve.wait_ge(*RT.upto("z", h - 1))
                v.tensor_copy(wgs, wg2[:, bass.ds(h * P, P)]).then_inc(*RV.step("wgs"))
                dve.wait_ge(*RT.upto("z", h))
                v.tensor_scalar(zb, ps[:, 0, 0:TOK], small[:, bass.ds(h + BG, 1)], None,
                                ALU.add).then_inc(*RV.step("z"))
                dve.wait_ge(*RA.upto("ln", h))
                v.scalar_tensor_tensor(out=ex, in0=zb, scalar=0.0, in1=ex, op0=ALU.min,
                                       op1=ALU.subtract).then_inc(*RV.step("la"))
                dve.wait_ge(*RV.upto("la", h))
                v.tensor_tensor_scan(cum, keep_g, ex, 0.0, ALU.mult, ALU.add).then_inc(*RV.step("cum"))
                dve.wait_ge(*RV.upto("cum", h))
                mid = cum[:, 15:SEQ:32]
                v.tensor_scalar(rb[:, 0:8], mid, 1 / TAU, None, ALU.mult)
                v.tensor_scalar(rb[:, 8:9], cum[:, SEQ - 1:SEQ], 1 / TAU, None, ALU.mult).then_inc(*RV.step("rb"))
                v.tensor_tensor(qp.rearrange("p (n c) -> p n c", c=32),
                                cum[:, 0:SEQ].rearrange("p (n c) -> p n c", c=32),
                                mid.rearrange("p (n a) -> p n a", a=1).to_broadcast([P, 8, 32]),
                                ALU.subtract).then_inc(*RV.step("dq"))
                cs = cum[:, SEQ:TOK].rearrange("p (b t) -> p b t", t=TS)
                v.tensor_tensor(kd[:, SEQ:TOK].rearrange("p (b t) -> p b t", t=TS),
                                cs[:, :, TS - 1:TS].to_broadcast([P, NB, TS]), cs,
                                ALU.subtract).then_inc(*RV.step("dd"))
                sd = DK ** -0.5
                dve.wait_ge(*RA.upto("dec", h))
                v.scalar_tensor_tensor(out=qp, in0=qb[:, 0:SEQ], scalar=sd, in1=qp, op0=ALU.mult,
                                       op1=ALU.mult).then_inc(*RV.step("qp"))
                v.scalar_tensor_tensor(out=qe, in0=qb[:, SEQ:TOK], scalar=sd, in1=qe, op0=ALU.mult,
                                       op1=ALU.mult).then_inc(*RV.step("qe"))
                v.tensor_tensor(ke, kb[:, SEQ:TOK], ke, ALU.mult).then_inc(*RV.step("ke"))
                v.tensor_tensor(kd, kb, kd, ALU.mult).then_inc(*RV.step("kd"))
                v.memset(ps[:, 3, 0:384], 0.0).then_inc(*RV.step("zero_att"))
                dve.wait_ge(*RV.upto("zero_att", h))
                for c in range(8):
                    dve.wait_ge(*RA.upto(f"ki{c}", h))
                    n = 32 * (c + 1)
                    v.tensor_tensor(ki[:, c % 2, 0:n], kb[:, 0:n], ki[:, c % 2, 0:n],
                                    ALU.mult).then_inc(*RV.step(f"ki{c}"))
                dve.wait_ge(*RT.upto("att7", h))
                v.tensor_tensor(attT, ps[:, 3, 0:384], causal, ALU.mult).then_inc(*RV.step("att"))
                dve.wait_ge(*RT.upto("att_s", h))
                v.tensor_tensor(attS, ps[0:NS, 7, 0:NS], causal_s, ALU.mult).then_inc(*RV.step("att_s"))
                v.tensor_copy(kdr[:, 0:2, :].rearrange("p t c -> p (t c)"), ps[:, 6, 0:256])
                v.tensor_copy(kdr[0:NS, 2, :], ps[0:NS, 6, 256:384]).then_inc(*RV.step("kdr"))
                dve.wait_ge(*RV.upto("kdr", h))
                v.tensor_tensor(kdm.rearrange("p (b c) -> p b c", b=NB),
                                kdr[0:NS, 2:3, :].to_broadcast([NS, NB, P]),
                                own_batch.rearrange("p (b a) -> p b a", a=1).to_broadcast([NS, NB, P]),
                                ALU.mult).then_inc(*RV.step("kdm"))
                dve.wait_ge(*RT.upto("states", h))
                for b in range(NB):
                    bank = (1, 2, 6, 7)[b // 2]
                    last = v.scalar_tensor_tensor(out=s0[:, b, :], in0=s0[:, b, :], scalar=dec[:, b:b + 1],
                                                  in1=ps[:, bank, DV * (b % 2):DV * (b % 2) + DV],
                                                  op0=ALU.mult, op1=ALU.add)
                last.then_inc(*RV.step("new_state"))
                dve.wait_ge(*RT.upto("sum", h))
                v.tensor_scalar(rso, ps[:, 3, 0:TOK], 1 / DV, EPS, ALU.mult, ALU.add).then_inc(*RV.step("ms"))
                dve.wait_ge(*RA.upto("rs", h))
                for j in range(2):
                    r = proj[:, bass.ds(h * 2 + 40 + j, 1), :].rearrange("p a c -> p (a c)")
                    tmp = sqo[:, j, :]
                    v.scalar_tensor_tensor(out=tmp, in0=ps[:, 4 + j, 0:TOK], scalar=small[:, GO + j:GO + j + 1],
                                           in1=rso, op0=ALU.mult, op1=ALU.mult).then_inc(*RV.step(f"g{j}"))
                    dve.wait_ge(*RV.upto(f"g{j}", h))
                    v.tensor_tensor(r, tmp, r, ALU.mult).then_inc(*RV.step(f"o{j}"))
            dve.wait_ge(*OA.upto("gla_hi"))
            v.tensor_tensor(hlo[:, 8:16, :], proj[:, 40:48, :], hhi[:, 8:16, :].bitcast(F32),
                            ALU.subtract).then_inc(*OV.step("gla_lo"))

            def gated(gate, tile, psum, out, steps, n, i):
                tmp = tmp_s[:, 64 * (n % 2):64 * (n % 2) + 64]
                ts = tmp.rearrange("p (n b t) -> p n b t", n=2, b=NB)
                gs = modT[:, bass.ds(tile + gate, 2), 1:NC9].rearrange("p n (b a) -> p n b a", a=1)
                v.tensor_tensor(ts, psum[:, :, SEQ:TOK].rearrange("p n (b t) -> p n b t", t=TS),
                                gs.to_broadcast([P, 2, NB, TS]), ALU.mult).then_inc(*steps.step(f"s{n}"))
                for m in range(2):
                    v.scalar_tensor_tensor(
                        out=out(m)[:, 0:SEQ], in0=psum[:, m, 0:SEQ],
                        scalar=modT[:, bass.ds(tile + (gate + m), 1), 0:1].rearrange("p a b -> p (a b)"),
                        in1=xT[:, bass.ds(tile + m, 1), 0:SEQ].rearrange("p a c -> p (a c)"),
                        op0=ALU.mult, op1=ALU.add)
                dve.wait_ge(*steps.upto(f"s{n}", i))
                for m in range(2):
                    last = v.tensor_tensor(out(m)[:, SEQ:TOK], tmp[:, NS * m:NS * m + NS],
                                           xT[:, bass.ds(tile + m, 1), SEQ:TOK].rearrange("p a c -> p (a c)"), ALU.add)
                last.then_inc(*steps.step(f"u{n}"))

            for j in range(LEAD):
                lo(0, j, CH_OUT)
            with dve.Fori(0, 2) as i:
                for j in range(LEAD, 16 + LEAD):
                    lo(i, j, CH_OUT)
                    if j % 4 == 1:
                        u = (j - 5) // 4
                        spent(i, CH_OUT, 4 * u + 4)
                        dve.wait_ge(*UV.upto(f"u{(u + 3) % 4}", i if u else i - 1))
                        t = i * 8 + 2 * u
                        gated(2 * KD, t, ps[:, 2 * (u % 2):2 * (u % 2) + 2, :],
                              lambda m, t=t: xT[:, bass.ds(t + m, 1), :].rearrange("p a c -> p (a c)"), UV, u, i)
            norm_mean(1, 4)
            norm(1)

            dve.wait_ge(*UV.upto("u3", 1))
            v.memset(gpad[:, :, 0:2], 0.0).then_inc(*FZ.step("zero"))
            dve.wait_ge(*FZ.upto("zero"))
            with dve.Fori(0, 11) as i:
                def los(first, end):
                    for j in range(first, end):
                        lo(i, j, CH_UP)

                w = lambda j, m: small[:, bass.ds(i * 4 + (CW + KF * j + m), 1)]

                def conv(n):
                    dve.wait_ge(*FA.upto(f"g{n}", i))
                    dve.wait_ge(*FV.upto(f"act{1 - n}", i - 1 + n))
                    for j, name in ((0, "a"), (1, "b"), (2, "conv")):
                        for m in range(2):
                            g = gpad[:, 2 * n + m, j:j + GW - 2]
                            if j == 0:
                                last = v.tensor_scalar(cv[:, m, :], g, w(0, 2 * n + m), w(3, 2 * n + m), ALU.mult,
                                                       ALU.add)
                            else:
                                last = v.scalar_tensor_tensor(out=cv[:, m, :], in0=g, scalar=w(j, 2 * n + m),
                                                              in1=cv[:, m, :], op0=ALU.mult, op1=ALU.add)
                        last.then_inc(*FV.step(f"{name}{n}"))
                        dve.wait_ge(*FV.upto(f"{name}{n}", i))

                def gate(n):
                    spent(i, CH_UP, 8 * n + 8)
                    dve.wait_ge(*FA.upto(f"silu{n}", i))
                    dst = actT[:, bass.ds(i * 4 + 2 * n, 2), :]
                    v.tensor_tensor(dst[:, :, 0:SEQ], ps[:, 2:4, 0:SEQ], cv[:, :, 0:SEQ], ALU.mult)
                    v.tensor_tensor(dst[:, :, SEQ:TOK].rearrange("p n (b t) -> p n b t", t=TS),
                                    ps[:, 2:4, SEQ:TOK].rearrange("p n (b t) -> p n b t", t=TS),
                                    samples_of(cv, 2 + SEQ), ALU.mult).then_inc(*FV.step(f"act{n}"))

                dve.wait_ge(*FT.upto("hist", i))
                v.tensor_copy(gpad[:, :, 2 + SEQ:GW].rearrange("p n (b t) -> p n b t", t=6)[:, :, :, 0:2],
                              ps[:, 4, 0:64].rearrange("p (n b r) -> p n b r", n=4, b=NB)).then_inc(*FV.step("hist"))
                los(2, 6)
                conv(0)
                los(6, 10)
                gate(0)
                los(10, 14)
                conv(1)
                dve.wait_ge(*FT.upto("rows", i - 1))
                v.tensor_copy(glast[:, :, 0:2], gpad[:, :, SEQ:SEQ + 2])
                v.tensor_copy(glast[:, :, 2:18].rearrange("p n (b r) -> p n b r", r=2),
                              gpad[:, :, 2 + SEQ:GW].rearrange("p n (b t) -> p n b t", t=6)[:, :, :, 4:6]
                              ).then_inc(*FV.step("last"))
                los(14, 18)
                gate(1)

            def act_parts(c, i):
                dve.wait_ge(act_hi, i * 12 + (c + 1))
                for k0, at, m in pieces(*KCH[c % 12]):
                    last = v.tensor_tensor(hlo[:, at:at + m, :], actT[:, k0:k0 + m, :],
                                           hhi[:, at:at + m, :].bitcast(F32), ALU.subtract)
                last.then_inc(act_lo, 1)

            def down_turn(i, end):
                def out(h):
                    dve.wait_ge(used, i * 24 + (CH_DOWN + BUFS + 21 + 3 * h))
                    dve.wait_ge(*DT.upto("t2", i - 1))
                    dve.wait_ge(*DV_.upto("u0" if h else "u1", i - 1 + h))
                    gated(5 * KD, i * 4 + 2 * h, ps[:, 2 * h:2 * h + 2, :], lambda m, h=h: yst[:, 2 * h + m, :],
                          DV_, h, i)

                for j in range(LEAD, end):
                    jj = j % 24
                    kg, h, kc = jj // 6, jj // 3 % 2, jj % 3
                    if j == 24:
                        out(0)
                    if h == 0:
                        act_parts(3 * kg + kc + 12 * (j // 24), i)
                    dve.wait_ge(hi_done, i * 24 + (CH_DOWN + j + 1))
                    n = 256 * KCH[3 * kg + kc][1]
                    v.tensor_tensor(wlo[:, jj % BUFS, 0:n], ring[:, (2 * kg + h) % SLOTS, CHUNK * kc:CHUNK * kc + n],
                                    whi[:, jj % BUFS, 0:n].bitcast(F32), ALU.subtract).then_inc(lo_done, 1)
                if end == 24:
                    out(0)
                out(1)

            dve.wait_ge(*FV.upto("act1", 10))
            dve.wait_ge(*FT.upto("rows", 10))
            for c in range(LEAD):
                act_parts(c, 0)
            with dve.Fori(0, 3) as i:
                down_turn(i, 24 + LEAD)
            down_turn(3, 24)


def qd_blocks(qd, h, lo):
    v = qd[h, lo:lo + 8]
    return bass.AP(v.tensor, v.offset, [list(v.ap[0]), [128, 2], [40, 4], [1, TS]])


def own_heads(ps, h, lo):
    v = ps[h, 0, lo:lo + 8]
    return bass.AP(v.tensor, v.offset, [list(v.ap[0]), [136, 4], [1, TS]])


def samples_of(cv, lo):
    v = cv[:, :, lo:lo + TS]
    part, blk = list(v.ap[0]), list(v.ap[1])
    return bass.AP(v.tensor, v.offset, [part, blk, [6, NB], [1, TS]])


_OUTS = [("y_p", (SEQ, D)), ("y_s", (NS, D)), ("new_k_p", (SEQ, 1024)), ("new_v_p", (SEQ, 1024)),
         ("new_gla_p", (H_B, DK, DV)), ("new_conv_p", (2, D_FF)), ("new_k_s", (NS, 1024)), ("new_v_s", (NS, 1024)),
         ("new_gla_s", (NB, H_B, DK, DV)), ("new_conv_s", (2 * NB, D_FF))]


def kernel(**inputs):
    import concourse.bacc as bacc
    from concourse.bass_utils import run_bass_kernel_spmd

    nc = bacc.Bacc("TRN2", target_bir_lowering=False, num_devices=1)
    tables = constants()
    arrays, a, o = {}, {}, {}
    for name, x in {**inputs, "tables": tables}.items():
        x = np.ascontiguousarray(x)
        arrays[f"in_{name}"] = x
        a[name] = nc.dram_tensor(f"in_{name}", x.shape, mybir.dt.from_np(x.dtype), kind="ExternalInput").ap()
    for name, shape in _OUTS:
        o[name] = nc.dram_tensor(f"out_{name}", shape, F32, kind="ExternalOutput").ap()
    bias_rows = nc.dram_tensor("bias_rows", [H_A, 512], F32)
    bias_full = nc.dram_tensor("bias_full", [H_A, P, SEQ], F32)
    build(nc, a, o, bias_rows, bias_full)
    r = run_bass_kernel_spmd(nc, [arrays], core_ids=[0]).results[0]
    g = {name: r[f"out_{name}"] for name, _ in _OUTS}
    return (g["y_p"].reshape(1, SEQ, D), g["y_s"].reshape(NB, TS, D),
            g["new_k_p"].reshape(1, 1, SEQ, H_A, HD), g["new_v_p"].reshape(1, 1, SEQ, H_A, HD),
            g["new_gla_p"].reshape(1, 1, H_B, DK, DV), g["new_conv_p"].reshape(1, 1, 2, D_FF),
            g["new_k_s"].reshape(1, NB, TS, H_A, HD), g["new_v_s"].reshape(1, NB, TS, H_A, HD),
            g["new_gla_s"].reshape(1, NB, H_B, DK, DV), g["new_conv_s"].reshape(1, NB, 2, D_FF))
```

```python
import math
from contextlib import ExitStack

import concourse.bass as bass
import numpy as np
from concourse import mybir

F32 = mybir.dt.float32
F32R = mybir.dt.float32r
ACT = mybir.ActivationFunctionType
ALU = mybir.AluOpType
AX_X = mybir.AxisListType.X

P = 128
D = 2048
SEQ = 256
NB, TS = 8, 4
NS = NB * TS
TOK = SEQ + NS
PAST = 1024
H_A, HD = 16, 64
PAIRS = H_A // 2
H_B, DK, DV = 4, 128, 256
RANK = 16
D_FF = 5632
EPS = 1e-6
TAU = 16.0
KD = D // P
KF = D_FF // P
NC9 = 1 + NB
DIL = ((128, 1), (512, 4), (2048, 16))
NBUCK, MAXD = 32, 2048
NEG = -1e30

SLOTS, SLOT = 4, 11 * 256
BUFS, CHUNK = 4, 1024

N1, N2, BA = 0, KD, 2 * KD
CW, CB = 128, 128 + 3 * KF
QG, KG, AO, GO, BG = 304, 305, 306, 307, 309

FAR = PAST // 2 // 16 * TS
CK = FAR + PAST // 2
KT = CK // P


def bucket(dist):
    dist = np.asarray(dist)
    exact = NBUCK // 2
    df = np.maximum(dist, 1).astype(np.float32)
    large = exact + (np.log(df / exact) / math.log(MAXD / exact) * (NBUCK - exact)).astype(np.int32)
    return np.where(dist < exact, dist, np.minimum(large, NBUCK - 1))


def multiplicity(dist):
    dist = np.asarray(dist)
    n = sum(((dist >= 0) & (dist <= w) & (dist % d == 0)).astype(np.int32) for w, d in DIL)
    return np.where(n > 0, np.log(np.maximum(n, 1)), NEG).astype(np.float32)


def one_hot(dist):
    d = np.asarray(dist)
    return ((bucket(np.maximum(d, 0))[None] == np.arange(NBUCK)[:, None]) & (d[None] >= 0)).astype(np.float32)


CONST_LAYOUT = {}


def constants():
    parts = []

    def add(name, a):
        full = np.zeros((P, a.shape[1]), np.float32)
        full[:a.shape[0]] = a
        CONST_LAYOUT[name] = (sum(p.shape[1] for p in parts), a.shape[1])
        parts.append(full)

    i = np.arange(P)
    add("ident", np.eye(P, dtype=np.float32))
    add("halves", (i[:, None] // HD == i[None] // HD).astype(np.float32))
    add("ones", np.ones((P, P), np.float32))
    s, c = np.arange(P)[:, None], np.arange(SEQ)[None]
    add("causal", np.concatenate([s <= c, s + P <= c[:, P:]], 1).astype(np.float32))
    a = np.arange(NS)
    same = a[:, None] // TS == a[None] // TS
    add("causal_s", (same & (a[:, None] <= a[None])).astype(np.float32))
    add("own_batch", (a[:, None] // TS == np.arange(NB)[None]).astype(np.float32))
    dist = 2 * P - 1 - np.arange(512)
    add("hot_p", one_hot(dist))
    add("mult_p", np.tile(multiplicity(dist), (H_A, 1)))
    r = np.arange(P)
    far = 16 * (r % 32) + r // 32
    pos = np.concatenate([far, PAST // 2 + np.arange(PAST // 2)])
    t = np.arange(TS)
    add("hot_s", np.concatenate(
        [np.concatenate([one_hot(PAST + k - pos), one_hot(k - a % TS)], 1) for k in t], 0))
    old = multiplicity(PAST + t[:, None] - pos[None])[r % TS]
    new = []
    for g in range(NB // 2):
        b = 2 * g + r // 64
        m = multiplicity((r % TS)[:, None] - (a % TS)[None])
        new.append(np.where(b[:, None] == a[None] // TS, m, NEG))
    add("mult_s", np.concatenate([old] + new, 1).astype(np.float32))
    return np.concatenate(parts, 1)


class Steps:

    def __init__(self, sem, *names):
        self.sem, self.names, self.at = sem, names, 0

    def step(self, name):
        assert self.names[self.at] == name, (self.names[self.at], name)
        self.at = (self.at + 1) % len(self.names)
        return self.sem, 1

    def upto(self, name, turn=0):
        return self.sem, (turn + 1) * len(self.names) + self.names.index(name) + 1


def build(nc, a, o, bias_rows, bias_full):
    ctx = ExitStack()
    with ctx:
        def sb(name, shape):
            return ctx.enter_context(nc.sbuf_tensor(name, shape, F32))

        def sem(name):
            return ctx.enter_context(nc.semaphore(name))

        def sbr(name, shape, within=ctx):
            return within.enter_context(nc.sbuf_tensor(name, shape, F32R))

        ring = sb("ring", [P, SLOTS, SLOT])
        xT = sb("xT", [P, KD, TOK])
        proj = sb("proj", [P, 48, TOK])
        work = sb("work", [P, 2048])
        keep = CONST_LAYOUT["own_batch"][0] + NB
        con = sb("con", [P, keep])
        small = sb("small", [P, 313])
        c18 = sbr("c18", [P, KD, 2 * NC9])
        modT = sb("modT", [P, 6 * KD, NC9])
        ghi = sbr("ghi", [P, KD, RANK])
        glo = sbr("glo", [P, KD, RANK])
        qkS = sb("qkS", [P, 512])
        qS = qkS[:, 0:256].rearrange("p (n c) -> p n c", n=PAIRS)
        kS = qkS[:, 256:512].rearrange("p (n c) -> p n c", n=PAIRS)
        mrow = sb("mrow", [2 * NC9, 512])
        with ExitStack() as parts:
            hhi = sbr("hhi", [P, KD, TOK], parts)
            hlo = sbr("hlo", [P, KD, TOK], parts)
            whi = sbr("whi", [P, BUFS, CHUNK], parts)
            wlo = sbr("wlo", [P, BUFS, CHUNK], parts)
        vals = sb("vals", [P, 4, KT * 512])
        ps = ctx.enter_context(nc.psum_tensor("ps", [P, 8, 512], F32))

        def cview(name, rows=P):
            at, n = CONST_LAYOUT[name]
            return con[0:rows, at:at + n]

        ident, halves, ones = cview("ident"), cview("halves"), cview("ones")
        causal, causal_s, own_batch = cview("causal"), cview("causal_s", NS), cview("own_batch", NS)
        projf = proj[:, :, :].rearrange("p n c -> p (n c)")

        xr = projf[:, 0:3 * D].rearrange("p (t d) -> p t d", t=3)
        crow = projf[0:NC9, 6144:6144 + D]
        vrow = projf[:, 8192:8704].rearrange("p (t d) -> p t d", t=4)
        c0, cn = CONST_LAYOUT["hot_p"][0], CONST_LAYOUT["mult_s"]
        temp = projf[:, 8704:8704 + cn[0] + cn[1] - c0]

        def tview(name, rows):
            at, n = CONST_LAYOUT[name]
            return temp[0:rows, at - c0:at - c0 + n]

        relb = projf[:, 11300:11316]
        rel_rows = projf[:, 11328:11456]
        sq = projf[:, 11520:13824].rearrange("p (j n c) -> p j n c", j=2, n=4)
        hraw = projf[:, 0:KD * TOK].rearrange("p (n c) -> p n c", n=KD)
        btab = work[0:H_A, 0:512]
        cT = work[:, 512:656].rearrange("p (k c) -> p k c", k=KD)
        rs = work[:, 656:944]
        bias_s = work[:, 1248:2016]
        wglr = qkS[:, 0:256].rearrange("p (k c) -> p k c", k=KD)
        stat = work[:, 2016:2032]

        TAKEN = 4 * 3 * P

        def beside(s, lo, g, n):
            v = ring[:, s, TAKEN + lo:TAKEN + lo + g * n]
            return v.rearrange("p (g c) -> p g c", g=g)

        sqqk, rsqk = beside(0, 0, 2, TOK), beside(0, 576, 2, TOK)
        prob, krows = beside(1, 0, 2, 384), beside(1, 768, 3, P)
        probT, vrows = beside(2, 0, 2, 384), beside(2, 768, 3, P)
        qkst = beside(3, 0, 2, TOK)
        vst = ring[:, 3, TAKEN + 576:TAKEN + 864]
        bias_p = work[:, 0:1024].rearrange("p (j e c) -> p j e c", j=2, e=2)

        kv0 = 8 * TOK
        qd = projf[:, kv0:kv0 + 512]
        kcT = projf[:, kv0 + 512:kv0 + 1856].rearrange("p (j c) -> p j c", j=2)
        sc = projf[:, kv0 + 1856:kv0 + 2528]
        orow = projf[:, kv0 + 2528:kv0 + 3040]
        vrow_s = projf[0:NS, kv0 + 3296:kv0 + 4320]
        glrT = projf[0:RANK, kv0 + 4320:kv0 + 4608]
        sT = work[:, 0:768].rearrange("p (t c) -> p t c", t=6)

        s0 = projf[:, 0:2048].rearrange("p (b v) -> p b v", b=NB)
        zb, ex = projf[:, 2048:2336], projf[:, 2336:2624]
        cumz = projf[:, 2624:2913]
        qp = projf[:, 2914:3170]
        ki = projf[:, 3170:3682].rearrange("p (j c) -> p j c", j=2)
        sqo = projf[:, 3170:3746].rearrange("p (j c) -> p j c", j=2)
        attT = projf[:, 3746:4130]
        attS = projf[0:NS, 4130:4162]
        kd = projf[:, 4162:4450]
        qe, ke = projf[:, 4450:4482], projf[:, 4482:4514]
        rb = projf[:, 4514:4523]
        dec = projf[:, 4524:4532]
        stp = projf[:, 4532:4788]
        kdm = projf[0:NS, 4788:5812]
        wgs = projf[0:RANK, 5812:5940]
        keep_g = projf[:, 5940:6228]
        wg2 = qkS[0:RANK, :]
        vbst = work[:, 0:576].rearrange("p (j c) -> p j c", j=2)
        vbr = work[:, 576:1344].rearrange("p (t c) -> p t c", t=3)
        kdr = work[:, 1344:1728].rearrange("p (t c) -> p t c", t=3)
        rso = work[:, 1728:2016]

        actT = projf[:, 0:KF * TOK].rearrange("p (n c) -> p n c", n=KF)
        tail = projf[:, KF * TOK:48 * TOK]
        GW = 2 + SEQ + NB * 6
        gpad = work[:, 0:4 * GW].rearrange("p (n c) -> p n c", n=4)
        cv = work[:, 1224:1832].rearrange("p (n c) -> p n c", n=2)
        glast = work[:, 1832:1904].rearrange("p (n c) -> p n c", n=4)
        hrow = tail[0:16, 0:1024].rearrange("p (j c) -> p j c", j=2)
        crows = qkS[0:18, :]
        tmp_s = work[:, 1904:2032]

        yst = work[:, 0:1152].rearrange("p (n c) -> p n c", n=4)
        yrow = tail[:, 0:1024].rearrange("p (j c) -> p j c", j=2)

        full = [sem(f"slot_full{s}") for s in range(SLOTS)]
        far_in = [sem(f"far_rows_in{s}") for s in range(SLOTS)]
        raw_used = sem("raw_slabs_used")
        vals_in = [sem(f"values_in{u}") for u in range(4)]
        hi_done = sem("chunks_hi")
        lo_done = sem("chunks_lo")
        used = sem("chunks_used")
        act_hi, act_lo = sem("act_hi"), sem("act_lo")
        con_in, x_in, c_in, vec_in, rel_in, temp_in, wglr_in, wg2_in, vrow_in = (
            sem(n) for n in ("con_in", "x_in", "c_in", "vec_in", "rel_in", "temp_in", "wglr_in", "wg2_in",
                             "vrow_in"))
        btab_out, slant_out = sem("bias_table_out"), sem("bias_slant_out")
        biasp_in = [sem(f"bias_pair_in{j}") for j in range(2)]
        pool_turns, row_turns, copy_turns = sem("pool_turns"), sem("row_turns"), sem("copy_turns")
        k_out, v_out = sem("k_rows_out"), sem("v_rows_out")
        stp_out = sem("prompt_state_out")
        conv_out = sem("conv_rows_out")
        y_out = sem("y_rows_out")
        kv_stored, stp_stored, conv_stored, y_stored = (
            sem(f"{n}_stored") for n in ("kv_rows", "prompt_state", "conv_rows", "y_rows"))
        s0_in, s0_out = sem("state_in"), sem("state_out")
        hist_in = [sem(f"history_in{j}") for j in range(2)]

        st = lambda name, *names: Steps(sem(name), *names)
        PT_ = st("prep_tensor", "c", *(f"x{k}" for k in range(8)), "vectors",
                 *(f"x{k}" for k in range(8, KD)), "bias_p", "bias_s")
        PV_ = st("prep_vector", "c", *(f"x{k}" for k in range(8)), "vectors",
                 *(f"x{k}" for k in range(8, KD)), "zero_rel", "rel_rows", "bias_p",
                 "bias_s0", "bias_s")
        PA_ = st("prep_scalar", "silu_c")
        NT = [st(f"norm{n}_tensor", "s0", "s1", "s2", "s3") for n in (1, 2)]
        NA = [st(f"norm{n}_scalar", "q0", "q1", "q2", "q3", "ln", "rs") for n in (1, 2)]
        NM = [st(f"norm{n}_mean", "ms") for n in (1, 2)]
        NH = [st(f"norm{n}_upper", "h") for n in (1, 2)]
        NG = [st(f"norm{n}_groups", "scale", "t", "p", "s", "d") for n in (1, 2)]
        NL = [st(f"norm{n}_lower", "l") for n in (1, 2)]
        CV = st("prep_split_vector", "c_lo", "glr_lo")
        CA = st("prep_split_scalar", "c_hi", "glr_hi")
        AT = st("ada_tensor", "turn_a", "turn_b")
        AA = st("ada_scalar", "rows_a", "rows_b")
        AV = st("ada_vector", "base", "mod")
        WV = st("in_evac", "u0", "u1", "u2", "u3")
        GT = st("glr_tensor", "done")
        GA = st("glr_scalar", "rows", "silu_r")
        TT = st("pair_tensor", "sums", "kv_rows", "scores", "probT", "out")
        TV = st("pair_vector", "squares", "ms", "q", "k", "samples", "krows", "vrows", "biased",
                "max", "recip", "norm", "out")
        TA = st("pair_scalar", "ln", "rs", "vstage", "exp", "probT", "evac")
        ST = st("sample_tensor", "k0", *(x for n in range(1, 16) for x in (f"k{n}", f"s{n - 1}")), "s15")
        SO = st("sample_output_tensor", "probT", "v0", "v1", "v2", "v3", "oT")
        SQ = st("sample_queries", "qd")
        SV = st("sample_vector", "biased", "max", "recip", "norm", "out")
        SK = st("sample_key_copies", *(f"k{n}" for n in range(16)))
        SA = st("sample_scalar", "exp", "probT", "orow")
        RT = st("gla_tensor", "z", "vrows", "att_s", "att0", "att1", "turn0", *(f"att{i}" for i in range(2, 8)),
                "kdrows", "o", "state", "states", "turn1", "sum", "turn2", "turn3")
        RV = st("gla_vector", "wgs", "z", "la", "cum", "rb", "dq", "dd", "qp", "qe", "ke", "kd", "zero_att",
                "ki0", "ki1", "ki2", "ki3", "base0", "mod0", "ki4", "ki5", "ki6", "ki7", "att", "att_s", "kdr",
                "kdm", "last_state", "base1", "mod1", "new_state", "ms", "g0", "o0", "g1", "o1", "base2", "mod2",
                "base3", "mod3")
        RA = st("gla_scalar", "vstage", "abs", "exp", "ln", "vrows", "eq", "eqs", "eks", "ekd", "ekds", "dec",
                "ki0", "ki1", "rows0", *(f"ki{i}" for i in range(2, 8)), "sq", "rows1", "stp", "lnr", "rs",
                "rows2", "rows3")
        OT = st("onorm_tensor", "sums0", "sums1")
        OA = st("onorm_scalar", "sq0", "sq1", "ln0", "ln1", "rs0", "rs1", "hi0", "hi1", "gla_hi")
        OV = st("onorm_vector", "ms0", "ms1", "done0", "done1", "lo0", "lo1", "gla_lo")
        UV = st("out_vector", *(x for n in range(4) for x in (f"s{n}", f"u{n}")))
        FT = st("up_tensor", "hist", "rows")
        FV = st("up_vector", "hist", "a0", "b0", "conv0", "act0", "a1", "b1", "conv1", "last", "act1")
        FA = st("up_scalar", "g0", "silu0", "g1", "silu1", "rows")
        FZ = st("first_fills", "zero_qd", "keep", "zero")
        DT = st("down_tensor", "t0", "t1", "t2")
        DV_ = st("down_vector", "s0", "u0", "s1", "u1")
        DA = st("down_scalar", "r0", "r1", "r2")

        SL_IN, SL_IN2, SL_SAMP, SL_ADA2, SL_OUT, SL_UP, SL_DOWN = 32, 56, 88, 104, 168, 184, 272
        CH_IN, CH_IN2, CH_ADA2, CH_OUT, CH_UP, CH_DOWN = 64, 112, 176, 272, 304, 480
        LEAD = 2

        w_ada = a["w_ada"][0].rearrange("(k p) c -> p k c", p=P)
        w_in = a["w_in"][0].rearrange("(k p) c -> p k c", p=P)
        w_out = a["w_out"][0].rearrange("(k p) c -> p k c", p=P)
        w_up = a["w_up"][0].rearrange("(k p) c -> p k c", p=P)
        w_down = a["w_down"][0].rearrange("(k p) c -> p k c", p=P)

        def slab(s, k, c):
            return ring[:, s, 0:k * c].rearrange("p (k c) -> p k c", k=k)

        def pieces(k0, n):
            at, out = k0 % KD, []
            while n:
                m = min(n, KD - at)
                out.append((k0, at, m))
                k0, at, n = k0 + m, (at + m) % KD, n - m
            return out

        KCH = [(11 * g + o, n) for g in range(4) for o, n in ((0, 4), (4, 4), (8, 3))]

        def last_use(c):
            k0, n = KCH[c]
            old = k0 + n - 1 - KD if k0 >= KD or k0 + n > KD else k0 + n - 1 + 2 * KD
            back = 24 if old >= k0 + n - 1 else 0
            old = min(old, KF - 1)
            j = next(j for j, (k, m) in enumerate(KCH) if k <= old < k + m)
            return 6 * (j // 3) + 3 + j % 3 + 1 - back

        def states(b):
            return ps[:, (1, 2, 6)[b // 2], DV * (b % 2):DV * (b % 2) + DV] if b < 6 else ps[:, 3 * (b - 6), DV:2 * DV]

        block = ctx.enter_context(nc.Block())

        @block.sync
        def _(sp):
            def ada_loads(columns, chunks, slabs=range(8)):
                for s in slabs:
                    if chunks is not None:
                        sp.wait_ge(lo_done, chunks + 2 * s - 6)
                    sp.dma_start(slab(s % SLOTS, 4, 512),
                                 w_ada[:, 4 * (s % 4):4 * (s % 4) + 4, bass.ds(columns[s // 4], 512)]
                                 ).then_inc(full[s % SLOTS], 16)

            def half_loads(w, columns, chunks):
                for s in range(8):
                    sp.wait_ge(lo_done, chunks + 2 * s - 6)
                    sp.dma_start(slab(s % SLOTS, 8, 256),
                                 w[:, 8 * (s % 2):8 * (s % 2) + 8, bass.ds(columns[s // 2], 256)]
                                 ).then_inc(full[s % SLOTS], 16)

            sp.dma_start(con[:, :], a["tables"][:, 0:keep]).then_inc(con_in, 16)
            ada_loads([0, D], None, range(1))
            sp.dma_start(xr[:, 0:2, :], a["x_prompt"][0].rearrange("(t p) d -> p t d", p=P)).then_inc(x_in, 16)
            sp.dma_start(xr[0:NS, 2, :], a["x_sample"].rearrange("b t d -> (b t) d")).then_inc(x_in, 16)
            ada_loads([0, D], None, range(1, 4))
            ada_loads([0, D], 0, range(4, 8))
            with sp.Fori(1, 4) as i:
                ada_loads([i * 512, i * 512 + D], i * 16)
            with sp.Fori(0, 3) as i:
                half_loads(w_in, [i * 1024 + 256 * u for u in range(4)], i * 16 + CH_IN)
            with sp.Fori(0, PAIRS) as p:
                for s in range(4):
                    sp.wait_ge(lo_done, p * 8 + (CH_IN2 + 2 * s - 6))
                    sp.dma_start(slab(s, 4, 384), w_in[:, 4 * s:4 * s + 4, bass.ds(p * 384 + 3072, 384)]
                                 ).then_inc(full[s], 16)
            sp.wait_ge(lo_done, CH_ADA2)
            sp.wait_ge(*TT.upto("out", PAIRS - 1))
            sp.wait_ge(kv_stored, PAIRS + 1)
            sp.wait_ge(*GT.upto("done"))
            sp.wait_ge(used, CH_ADA2 + BUFS)
            with sp.Fori(0, NB // 2) as g:
                for s in range(8):
                    cache = a["cache_k_win" if s < 4 else "cache_v_win"][0]
                    u = s % 4
                    rows = cache[bass.ds(g * 2 + u // 2, 1), :, :, :].rearrange("a s h d -> (a s) (h d)")
                    cols = slice(512 * (u % 2), 512 * (u % 2) + 512)
                    if s < 4:
                        view, landed = slab(u, KT, 512), (far_in[u], full[u])
                        sp.wait_ge(*ST.upto(f"k{4 * u + 3}", g - 1))
                    else:
                        view, landed = vals[:, u, :].rearrange("p (t c) -> p t c", t=KT), (vals_in[u], vals_in[u])
                        sp.wait_ge(*SO.upto(f"v{u}", g - 1))
                    far = rows[0:PAST // 2, cols].rearrange("(a r) c -> r a c", r=16)[0:TS]
                    sp.dma_start(view[:, 0, :], far).then_inc(landed[0], 16)
                    sp.dma_start(view[:, 1:KT, :],
                                 rows[PAST // 2:PAST, cols].rearrange("(n p) c -> p n c", p=P)).then_inc(landed[1], 16)
            sp.wait_ge(*ST.upto("k15", 3))
            with sp.Fori(0, H_B) as h:
                for s in range(16):
                    if 4 <= s < 8:
                        sp.wait_ge(raw_used, h * 4 + (s - 3))
                    else:
                        sp.wait_ge(lo_done, h * 24 + (CH_ADA2 + (2 * s - 14 if s >= 8 else 2 * s - 6)))
                    sp.dma_start(slab(s % SLOTS, 4, 512),
                                 w_ada[:, 4 * (s % 4):4 * (s % 4) + 4, bass.ds(h * 2048 + (2 * D + 512 * (s // 4)), 512)]
                                 ).then_inc(full[s % SLOTS], 16)
            with sp.Fori(0, 2) as i:
                half_loads(w_out, [i * 1024 + 256 * u for u in range(4)], i * 16 + CH_OUT)
            with sp.Fori(0, 11) as i:
                half_loads(w_up, [i * 512, i * 512 + D_FF, i * 512 + 256, i * 512 + D_FF + 256], i * 16 + CH_UP)
            with sp.Fori(0, 4) as i:
                for s in range(8):
                    kg, h = s // 2, s % 2
                    sp.wait_ge(lo_done, i * 24 + (CH_DOWN + 6 * kg + 3 * h - 6))
                    sp.dma_start(slab(s % SLOTS, 11, 256),
                                 w_down[:, 11 * kg:11 * kg + 11, bass.ds(i * 512 + 256 * h, 256)]
                                 ).then_inc(full[s % SLOTS], 16)

        @block.gpsimd
        def _(pool):
            for dst, src in [
                    (vrow[0:16, 0, :], a["norm1_g"]), (vrow[16:32, 0, :], a["norm2_g"]), (vrow[32:128, 0, :], a["b_ada"]),
                    (vrow[0:44, 1, :], a["conv_w"][0, 0:1, :]), (vrow[44:88, 1, :], a["conv_w"][0, 1:2, :]),
                    (vrow[0:44, 2, :], a["conv_w"][0, 2:3, :]), (vrow[44:88, 2, :], a["conv_b"]),
                    (vrow[3:5, 3, :], a["gla_out_g"]), (vrow[5:9, 3, :], a["b_gate2"])]:
                pool.dma_start(dst, src.rearrange("a (n p) -> (a n) p", p=P)).then_inc(vec_in, 16)
            for j, name in enumerate(("q_norm_g", "k_norm_g", "a_out_g")):
                for e in range(2):
                    pool.dma_start(vrow[j:j + 1, 3, HD * e:HD * e + HD], a[name]).then_inc(vec_in, 16)
            pool.dma_start(wglr, w_in[:, :, 6144:6160]).then_inc(wglr_in, 16)
            for t in range(4):
                pool.dma_start(relb[32 * t:32 * t + 32, :], a["rel_bias"]).then_inc(rel_in, 16)
            pool.wait_ge(full[3], 16)
            pool.dma_start(temp, a["tables"][:, c0:cn[0] + cn[1]]).then_inc(temp_in, 16)
            for s_ in (kv_stored, stp_stored, conv_stored, y_stored):
                pool.sem_inc(s_, 1)
            pool.wait_ge(*PV_.upto("bias_p"))
            pool.dma_start(bias_rows[:, :], btab).then_inc(btab_out, 16)
            pool.wait_ge(btab_out, 16)
            slant = bass.AP(bias_rows[:, :].tensor, P - 1, [[512, H_A], [-1, P], [1, SEQ]])
            pool.dma_start(bias_full[:, :, :], slant).then_inc(slant_out, 16)
            pool.wait_ge(slant_out, 16)
            by_head = bias_full[:, :, :].rearrange("h p c -> p h c")
            with pool.Fori(0, PAIRS // 2) as i:
                for j in range(2):
                    p = i * 2 + j
                    if j == 0:
                        pool.wait_ge(*TV.upto("squares", i * 2))
                    else:
                        pool.wait_ge(*TV.upto("biased", i * 2))
                    pool.sem_inc(pool_turns, 1)
                    pool.dma_start(bias_p[:, j], by_head[:, bass.ds(p * 2, 2), :]).then_inc(biasp_in[j], 16)
                    pool.wait_ge(*TV.upto("krows", p))
                    pool.sem_inc(pool_turns, 1)
                    cols = bass.ds(p * P, P)
                    ko = o["new_k_p"].rearrange("(t s) c -> s t c", s=P)
                    vo = o["new_v_p"].rearrange("(t s) c -> s t c", s=P)
                    pool.dma_start(ko[:, :, cols], krows[:, 0:2, :]).then_inc(k_out, 16)
                    pool.dma_start(o["new_k_s"][:, cols], krows[0:NS, 2, :]).then_inc(k_out, 16)
                    pool.wait_ge(*TV.upto("vrows", p))
                    pool.sem_inc(pool_turns, 1)
                    pool.dma_start(vo[:, :, cols], vrows[:, 0:2, :]).then_inc(v_out, 16)
                    pool.dma_start(o["new_v_s"][:, cols], vrows[0:NS, 2, :]).then_inc(v_out, 16)
                    pool.wait_ge(k_out, i * 64 + (32 * j + 32))
                    pool.wait_ge(v_out, i * 64 + (32 * j + 32))
                    pool.sem_inc(kv_stored, 1)
            pool.wait_ge(v_out, 256)
            pool.wait_ge(*TV.upto("out", PAIRS - 1))
            pool.wait_ge(*TT.upto("kv_rows", PAIRS - 1))
            pool.dma_start(vrow_s, o["new_v_s"]).then_inc(vrow_in, 16)
            pool.wait_ge(*SV.upto("out", 3))
            pool.dma_start(wg2, a["w_gate2"][0]).then_inc(wg2_in, 16)
            pool.wait_ge(*OV.upto("lo1"))
            pool.wait_ge(*OA.upto("hi1"))
            pool.wait_ge(*SO.upto("oT", 3))
            s_in = a["state_gla"][0].rearrange("b h k v -> k h b v")
            s_out = o["new_gla_s"].rearrange("b h k v -> k h b v")
            pool.dma_start(s0, s_in[:, 0]).then_inc(s0_in, 16)
            with pool.Fori(0, H_B - 1) as h:
                pool.wait_ge(*RA.upto("stp", h))
                pool.sem_inc(pool_turns, 1)
                pool.dma_start(o["new_gla_p"][bass.ds(h, 1)].rearrange("a k v -> (a k) v"), stp).then_inc(stp_out, 16)
                pool.wait_ge(*RV.upto("new_state", h))
                pool.sem_inc(pool_turns, 1)
                pool.dma_start(s_out[:, bass.ds(h, 1)].rearrange("k a b v -> k (a b) v"), s0).then_inc(s0_out, 16)
                pool.wait_ge(stp_out, h * 16 + 16)
                pool.sem_inc(stp_stored, 1)
                pool.wait_ge(s0_out, h * 16 + 16)
                pool.sem_inc(pool_turns, 1)
                pool.dma_start(s0, s_in[:, bass.ds(h + 1, 1)].rearrange("k a b v -> k (a b) v")).then_inc(s0_in, 16)
            pool.wait_ge(*RA.upto("stp", H_B - 1))
            pool.dma_start(o["new_gla_p"][H_B - 1], stp).then_inc(stp_out, 16)
            pool.wait_ge(*RV.upto("new_state", H_B - 1))
            pool.dma_start(s_out[:, H_B - 1], s0).then_inc(s0_out, 16)
            hist = a["state_conv"][0].rearrange("b r c -> (b r) c")
            pool.wait_ge(*NT[1].upto("s3"))
            pool.dma_start(hrow[:, 0], hist[:, 0:512]).then_inc(hist_in[0], 16)

            def history(j, i):
                pool.dma_start(hrow[:, j], hist[:, bass.ds(i * 512, 512)]).then_inc(hist_in[j], 16)

            def conv_rows(i):
                pool.wait_ge(*FA.upto("rows", i))
                pool.sem_inc(pool_turns, 1)
                pool.dma_start(o["new_conv_p"][:, bass.ds(i * 512, 512)], crows[0:2]).then_inc(conv_out, 16)
                pool.dma_start(o["new_conv_s"][:, bass.ds(i * 512, 512)], crows[2:18]).then_inc(conv_out, 16)
                pool.wait_ge(conv_out, i * 32 + 32)
                pool.sem_inc(conv_stored, 1)

            with pool.Fori(0, 5) as i:
                for j in range(2):
                    pool.wait_ge(*FT.upto("hist", i * 2 + (j - 1)))
                    pool.sem_inc(pool_turns, 1)
                    history(1 - j, i * 2 + (j + 1))
                    conv_rows(i * 2 + j)
            conv_rows(10)
            yp = o["y_p"].rearrange("(t s) c -> t s c", s=P)
            pool.sem_inc(pool_turns, 1)
            with pool.Fori(0, 4) as i:
                cols = bass.ds(i * 512, 512)
                for t in range(3):
                    pool.wait_ge(*DA.upto(f"r{t}", i))
                    pool.sem_inc(pool_turns, 1)
                    if t < 2:
                        pool.dma_start(yp[t][:, cols], yrow[:, t, :]).then_inc(y_out, 16)
                        pool.wait_ge(y_out, i * 48 + (16 * t + 16))
                        pool.sem_inc(y_stored, 1)
                    else:
                        pool.dma_start(o["y_s"][:, cols], yrow[0:NS, 0, :]).then_inc(y_out, 16)
                pool.wait_ge(y_out, i * 48 + 48)
                pool.sem_inc(y_stored, 1)
            for s, n in ((y_out, 192), (conv_out, 352), (k_out, 256), (v_out, 256), (stp_out, 64),
                         (s0_out, 64)):
                pool.wait_ge(s, n)

        @block.tensor
        def _(pe):
            mm, turn = nc.tensor.matmul, nc.tensor.transpose
            for s_ in (PT_, *NT, AT, GT, TT, ST, SO, RT, OT, FT, DT):
                pe.sem_inc(s_.sem, len(s_.names))
            pe.sem_inc(used, BUFS)

            pe.wait_ge(con_in, 16)
            pe.wait_ge(*PA_.upto("silu_c"))
            for k in range(KD):
                last = turn(ps[:, 4, NC9 * k:NC9 * k + NC9], crow[:, P * k:P * k + P], ident[0:NC9, 0:NC9])
            last.then_inc(*PT_.step("c"))
            def vectors():
                pe.wait_ge(vec_in, 16 * 15)
                for t, (n, c) in enumerate(((128, 0), (88, 128), (88, 216), (9, 304))):
                    last = turn(ps[:, 3, c:c + n], vrow[0:n, t, :], ident[0:n, 0:n])
                last.then_inc(*PT_.step("vectors"))

            def x_turns(k):
                if k == 0:
                    pe.wait_ge(x_in, 32)
                if k >= 3:
                    pe.wait_ge(*PV_.upto(f"x{k - 3}"))
                for t in range(3):
                    n = P if t < 2 else NS
                    last = turn(ps[:, 5 + k % 3, P * t:P * t + n], xr[0:n, t, P * k:P * k + P], ident[0:n, 0:n])
                last.then_inc(*PT_.step(f"x{k}"))

            def biases():
                pe.wait_ge(temp_in, 16)
                pe.wait_ge(rel_in, 64)
                pe.wait_ge(*PV_.upto("x15"))
                mm(ps[0:H_A, 5, :], relb[0:NBUCK, :], tview("hot_p", NBUCK), start=True,
                   stop=True).then_inc(*PT_.step("bias_p"))
                pe.wait_ge(*PV_.upto("rel_rows"))
                mm(ps[:, 6, :], rel_rows, tview("hot_s", P)[:, 0:512], start=True, stop=True)
                mm(ps[:, 7, 0:160], rel_rows, tview("hot_s", P)[:, 512:672], start=True,
                   stop=True).then_inc(*PT_.step("bias_s"))

            def norm_sum(n, j, bank):
                pe.wait_ge(*NA[n].upto(f"q{j}"))
                for k in range(4):
                    last = mm(ps[:, bank, 0:TOK], ones, sq[:, j % 2, k, :], start=(j + k == 0),
                              stop=(j == 3 and k == 3))
                last.then_inc(*NT[n].step(f"s{j}"))

            def ada_chunk(bank, j, chunks):
                pe.wait_ge(lo_done, chunks + j + 1)
                for k in range(2):
                    kk = 2 * (j % 8) + k
                    for n, part in enumerate((whi, wlo)):
                        last = mm(ps[0:2 * NC9, bank, :], c18[:, kk, :], part[:, j % BUFS, 512 * k:512 * k + 512],
                                  start=(kk + n == 0), stop=(kk == KD - 1 and n == 1))
                last.then_inc(used, 1)

            def ada_turn(bank):
                pe.sem_inc(row_turns, 1)
                for n in range(4):
                    last = turn(ps[:, bank, 18 * n:18 * n + 18], mrow[:, P * n:P * n + P],
                                ident[0:2 * NC9, 0:2 * NC9])
                return last

            pe.wait_ge(*CV.upto("c_lo"))

            def ada_group(i, first):
                pe.wait_ge(*AA.upto("rows_a", i - 1))
                for j in range(16):
                    if j == 8:
                        pe.wait_ge(*AA.upto("rows_b", i - 1))
                    if j == 12:
                        pe.wait_ge(*AA.upto("rows_a", i))
                        pe.wait_ge(*AV.upto("mod", i - 1))
                        if first:
                            pe.wait_ge(*PV_.upto("vectors"))
                        ada_turn(2).then_inc(*AT.step("turn_a"))
                    ada_chunk(j // 8, j, i * 16)
                    if first and j == 6:
                        vectors()
                    if first and j < 14:
                        x_turns(j + 2)
                    if first and j in (7, 11, 15):
                        norm_sum(0, (j - 7) // 4, 4)
                pe.wait_ge(*AA.upto("rows_b", i))
                ada_turn(3).then_inc(*AT.step("turn_b"))

            x_turns(0)
            x_turns(1)
            ada_group(0, True)
            norm_sum(0, 3, 4)
            biases()
            with pe.Fori(1, 4) as i:
                ada_group(i, False)

            def three(out, w_hi, w_lo, x_hi, x_lo, start, stop):
                mm(out, w_hi, x_hi, start=start, stop=False)
                mm(out, w_hi, x_lo, start=False, stop=False)
                return mm(out, w_lo, x_hi, start=False, stop=stop)

            def unit(bank, u, chunks, parts=False):
                for c in range(4):
                    j = 4 * u + c
                    pe.wait_ge(lo_done, chunks + j + 1)
                    if parts:
                        pe.wait_ge(*NL[1].upto("l", c))
                    for k in range(4):
                        for n in range(2):
                            w = slice(256 * k + P * n, 256 * k + P * n + P)
                            last = three(ps[:, bank + n, 0:TOK], whi[:, j % BUFS, w], wlo[:, j % BUFS, w],
                                         hhi[:, 4 * c + k, :], hlo[:, 4 * c + k, :], c + k == 0, c + k == 6)
                    last.then_inc(used, 1)

            def input_projection():
                with pe.Fori(0, 3) as i:
                    for u in range(4):
                        if u >= 2:
                            pe.wait_ge(*WV.upto(f"u{u - 2}", i))
                        else:
                            pe.wait_ge(*WV.upto(f"u{u + 2}", i - 1))
                        unit(2 * (u % 2), u, i * 16 + CH_IN)

            pe.wait_ge(*NL[0].upto("l", 3))
            pe.wait_ge(*AA.upto("rows_b", 3))
            input_projection()

            pe.wait_ge(*WV.upto("u3", 2))
            with pe.Fori(0, PAIRS) as p:
                def project(lo, hi):
                    for c in range(lo, hi):
                        pe.wait_ge(lo_done, p * 8 + (CH_IN2 + c + 1))
                        for k in range(2):
                            for n in range(3):
                                w = slice(384 * k + P * n, 384 * k + P * n + P)
                                last = three(ps[:, n, 0:TOK], whi[:, c % BUFS, w], wlo[:, c % BUFS, w],
                                             hhi[:, 2 * c + k, :], hlo[:, 2 * c + k, :], c + k == 0, c + k == 8)
                        last.then_inc(used, 1)

                pe.wait_ge(*TA.upto("evac", p - 1))
                project(0, 1)
                pe.wait_ge(*TV.upto("squares", p))
                pe.wait_ge(*TV.upto("out", p - 1))
                for g in range(2):
                    last = mm(ps[:, 4 + g, 0:TOK], halves, sqqk[:, g, :], start=True, stop=True)
                last.then_inc(*TT.step("sums"))
                project(1, 3)
                pe.wait_ge(*TV.upto("k", p))
                pe.wait_ge(*TA.upto("vstage", p))
                pe.wait_ge(*TA.upto("probT", p - 1))
                for g, src in enumerate((qkst[:, 1, :], vst)):
                    for t in range(3):
                        n = P if t < 2 else NS
                        last = turn(ps[0:n, 6 + g, P * t:P * t + P], src[:, P * t:P * t + n], ident)
                last.then_inc(*TT.step("kv_rows"))
                for e in range(2):
                    h = slice(HD * e, HD * e + HD)
                    for qt in range(2):
                        last = mm(ps[:, 4 + e, P * qt:P * qt + P * (qt + 1)], qkst[h, 0, P * qt:P * qt + P],
                                  qkst[h, 1, 0:P * (qt + 1)], start=True, stop=True)
                last.then_inc(*TT.step("scores"))
                project(3, 6)
                pe.wait_ge(*TV.upto("norm", p))
                for e in range(2):
                    for n in range(3):
                        last = turn(ps[:, 6 + e, P * n:P * n + P], prob[:, e, P * n:P * n + P], ident)
                last.then_inc(*TT.step("probT"))
                project(6, 8)
                pe.wait_ge(*TA.upto("probT", p))
                for e in range(2):
                    mm(ps[:, 4 + e, 0:SEQ], vrows[:, 0, :], probT[:, e, 0:SEQ], start=True, stop=False)
                    last = mm(ps[:, 4 + e, P:SEQ], vrows[:, 1, :], probT[:, e, SEQ:3 * P], start=False, stop=True)
                last.then_inc(*TT.step("out"))

            pe.wait_ge(*CV.upto("glr_lo"))
            pe.wait_ge(*TV.upto("out", PAIRS - 1))
            for k in range(KD):
                last = three(ps[0:RANK, 4, 0:TOK], ghi[:, k, :], glo[:, k, :], hhi[:, k, :], hlo[:, k, :],
                             k == 0, k == KD - 1)
            last.then_inc(*GT.step("done"))
            pe.wait_ge(*TA.upto("evac", PAIRS - 1))

            pe.wait_ge(*GA.upto("rows"))
            pe.wait_ge(vrow_in, 16)
            def key_turns(g, n):
                u, j = n // 4, n % 4
                if j == 0:
                    pe.wait_ge(far_in[u], g * 16 + 16)
                    pe.wait_ge(full[u], g * 16 + (SL_SAMP // SLOTS * 16 + 16))
                pe.wait_ge(*SK.upto(f"k{(n - 2) % 16}", g if n >= 2 else g - 1))
                for t in range(KT):
                    last = turn(ps[:, 2 * (n % 2) + t // 4, P * (t % 4):P * (t % 4) + P],
                                slab(u, KT, 512)[:, t, P * j:P * j + P], ident)
                last.then_inc(*ST.step(f"k{n}"))

            def scores(g, n):
                u, j = n // 4, n % 4
                if n == 0:
                    pe.wait_ge(*SQ.upto("qd", g))
                    pe.wait_ge(*SV.upto("biased", g - 1))
                pe.wait_ge(*SK.upto(f"k{n}", g))
                q = qd[:, 32 * n:32 * n + 32]
                rows = slice(32 * u, 32 * u + 32)
                mm(ps[rows, 4, :], q, kcT[:, n % 2, 0:512], start=(j == 0), stop=(j == 3))
                mm(ps[rows, 5, 0:160], q, kcT[:, n % 2, 512:CK + NS], start=(j == 0),
                   stop=(j == 3)).then_inc(*ST.step(f"s{n}"))

            def first_keys(g):
                for n in range(4):
                    key_turns(g, n)
                    if n:
                        scores(g, n - 1)

            def other_keys(g):
                for n in range(4, 16):
                    key_turns(g, n)
                    scores(g, n - 1)
                scores(g, 15)

            def output(g):
                pe.wait_ge(*SV.upto("norm", g))
                pe.wait_ge(*SA.upto("orow", g - 1))
                for t in range(KT):
                    turn(ps[:, 6 + t // 4, P * (t % 4):P * (t % 4) + P], sc[:, P * t:P * t + P], ident)
                turn(ps[0:NS, 7, P:2 * P], sc[:, CK:CK + NS], ident).then_inc(*SO.step("probT"))
                pe.wait_ge(*SA.upto("probT", g))
                for u in range(4):
                    pe.wait_ge(vals_in[u], g * 32 + 32)
                    rows = slice(32 * u, 32 * u + 32)
                    for t in range(KT):
                        mm(ps[rows, 7, :], sT[:, t, rows], vals[:, u, 512 * t:512 * t + 512], start=(t == 0), stop=False)
                    mm(ps[rows, 7, :], sT[0:NS, KT, rows], vrow_s[:, 512 * (u % 2):512 * (u % 2) + 512],
                       start=False, stop=True).then_inc(*SO.step(f"v{u}"))
                pe.wait_ge(*SA.upto("orow", g))
                for j in range(4):
                    last = turn(ps[:, 6, P * j:P * j + P], orow[:, P * j:P * j + P], ident)
                last.then_inc(*SO.step("oT"))

            first_keys(0)
            with pe.Fori(0, NB // 2 - 1) as g:
                other_keys(g)
                first_keys(g + 1)
                output(g)
            other_keys(NB // 2 - 1)
            output(NB // 2 - 1)

            pe.wait_ge(*SV.upto("out", 3))
            for n in range(2):
                pe.wait_ge(*OA.upto(f"sq{n}"))
                for k in range(4 * n, 4 * n + 4):
                    last = mm(ps[:, k, 0:TOK], halves, proj[:, 8 + k, :], start=True, stop=True)
                last.then_inc(*OT.step(f"sums{n}"))

            pe.wait_ge(*OV.upto("ms1"))
            with pe.Fori(0, H_B) as h:
                def ada(lo, hi):
                    for j in range(lo, hi):
                        if j % 8 == 0:
                            pe.wait_ge(*RV.upto(f"mod{j // 8}", h))
                        ada_chunk(7, j, h * 24 + CH_ADA2)

                def ada_unsplit():
                    pe.wait_ge(*RV.upto("mod3", h - 1))
                    for s in range(4):
                        pe.wait_ge(full[s], h * 64 + (SL_ADA2 // SLOTS * 16 + 16))
                        for k in range(4):
                            last = mm(ps[0:2 * NC9, 7, :], c18[:, 4 * s + k, :].bitcast(F32), slab(s, 4, 512)[:, k, :],
                                      start=(s + k == 0), stop=(s + k == 6))
                        last.then_inc(raw_used, 1)

                def tiles(g):
                    pe.wait_ge(*RA.upto(f"rows{g}", h))
                    ada_turn(7).then_inc(*RT.step(f"turn{g}"))

                pe.wait_ge(*RV.upto("wgs", h))
                pe.wait_ge(*RA.upto("stp", h - 1))
                mm(ps[:, 0, 0:TOK], wgs, glrT, start=True, stop=True).then_inc(*RT.step("z"))
                pe.wait_ge(*RA.upto("vstage", h))
                for t in range(3):
                    n = P if t < 2 else NS
                    for v in range(2):
                        last = turn(ps[0:n, 1 + t // 2, 256 * (t % 2) + P * v:256 * (t % 2) + P * v + P],
                                    vbst[:, v, P * t:P * t + n], ident)
                last.then_inc(*RT.step("vrows"))
                ada_unsplit()
                pe.wait_ge(*RV.upto("ki0", h))
                mm(ps[0:NS, 3, 384:384 + NS], ke, qe, start=True, stop=True).then_inc(*RT.step("att_s"))
                for c in range(8):
                    pe.wait_ge(*RV.upto(f"ki{c}", h))
                    q = qp[:, 32 * c:32 * c + 32]
                    n = min(P, 32 * (c + 1))
                    last = mm(ps[0:n, 3, 32 * c:32 * c + 32], ki[:, c % 2, 0:n], q, start=True, stop=True)
                    if c >= 4:
                        n = 32 * (c - 3)
                        last = mm(ps[0:n, 3, P + 32 * c:P + 32 * c + 32], ki[:, c % 2, P:P + n], q, start=True,
                                  stop=True)
                    last.then_inc(*RT.step(f"att{c}"))
                    if c == 1:
                        tiles(0)
                    if 3 <= c < 7:
                        ada(c - 3, c - 2)
                for t in range(3):
                    n = P if t < 2 else NS
                    last = turn(ps[0:n, 6, P * t:P * t + P], kd[:, P * t:P * t + n], ident)
                last.then_inc(*RT.step("kdrows"))
                ada(4, 5)
                pe.wait_ge(*RV.upto("att_s", h))
                pe.wait_ge(*RA.upto("vrows", h))
                pe.wait_ge(s0_in, h * 16 + 16)
                for v in range(2):
                    c = slice(P * v, P * v + P)
                    mm(ps[:, 4 + v, 0:SEQ], vbr[:, 0, c], attT[:, 0:SEQ], start=True, stop=False)
                    mm(ps[:, 4 + v, P:SEQ], vbr[:, 1, c], attT[:, SEQ:3 * P], start=False, stop=True)
                    for b in range(NB):
                        mm(ps[:, 4 + v, SEQ + TS * b:SEQ + TS * b + TS], s0[:, b, c],
                           qe[:, TS * b:TS * b + TS], start=(b == 0), stop=False)
                    last = mm(ps[:, 4 + v, SEQ:TOK], vbr[0:NS, 2, c], attS, start=False, stop=True)
                last.then_inc(*RT.step("o"))
                ada(5, 8)
                pe.wait_ge(*RV.upto("kdm", h))
                mm(ps[:, 0, 0:DV], kdr[:, 0, :], vbr[:, 0, :], start=True, stop=False)
                mm(ps[:, 0, 0:DV], kdr[:, 1, :], vbr[:, 1, :], start=False, stop=True).then_inc(*RT.step("state"))
                for b in range(NB):
                    last = mm(states(b), kdm[:, P * b:P * b + P], vbr[0:NS, 2, :], start=True, stop=True)
                last.then_inc(*RT.step("states"))
                tiles(1)
                ada(8, 14)
                pe.wait_ge(*RA.upto("sq", h))
                pe.wait_ge(*RV.upto("last_state", h))
                for v in range(2):
                    mm(ps[:, 3, 0:SEQ], ones, sqo[:, v, 0:SEQ], start=(v == 0), stop=(v == 1))
                for v in range(2):
                    last = mm(ps[:, 4, TOK:TOK + NS], ones, sqo[:, v, SEQ:TOK], start=(v == 0), stop=(v == 1))
                last.then_inc(*RT.step("sum"))
                ada(14, 16)
                tiles(2)
                ada(16, 24)
                tiles(3)

            pe.wait_ge(*OV.upto("gla_lo"))
            for i in range(2):
                for u in range(4):
                    if u >= 2:
                        pe.wait_ge(*UV.upto(f"u{u - 2}", i))
                    else:
                        pe.wait_ge(*UV.upto(f"u{u + 2}", i - 1))
                    unit(2 * (u % 2), u, i * 16 + CH_OUT)
                    if (i, u) in ((0, 3), (1, 2), (1, 3)):
                        norm_sum(1, {3: 0, 6: 1, 7: 2}[4 * i + u], 4)
            norm_sum(1, 3, 4)
            pe.wait_ge(*NM[1].upto("ms"))

            def up_turn(i, par):
                pe.wait_ge(hist_in[par], i * 8 + (16 - 8 * par))
                pe.wait_ge(*FV.upto("hist", i - 1))
                pe.sem_inc(row_turns, 1)
                for n in range(4):
                    last = turn(ps[:, 4, 16 * n:16 * n + 16], hrow[:, par, P * n:P * n + P], ident[0:16, 0:16])
                last.then_inc(*FT.step("hist"))
                for n in range(2):
                    pe.wait_ge(*FA.upto(f"g{1 - n}", i - 1 + n))
                    unit(0, 2 * n, i * 16 + CH_UP, n == 0)
                    pe.wait_ge(*FV.upto(f"act{1 - n}", i - 1 + n))
                    unit(2, 2 * n + 1, i * 16 + CH_UP)
                pe.wait_ge(*FV.upto("last", i))
                pe.wait_ge(*FA.upto("rows", i - 1))
                for n in range(4):
                    last = turn(ps[0:18, 5, P * n:P * n + P], glast[:, n, :], ident)
                last.then_inc(*FT.step("rows"))

            with pe.Fori(0, 5) as i:
                for par in range(2):
                    up_turn(i * 2 + par, par)
            up_turn(10, 0)

            pe.wait_ge(*FV.upto("act1", 10))
            pe.wait_ge(*FA.upto("rows", 10))
            with pe.Fori(0, 4) as i:
                for kg in range(4):
                    for h in range(2):
                        if kg == 0:
                            pe.wait_ge(*DV_.upto(f"u{h}", i - 1))
                        for kc in range(3):
                            j, c = 6 * kg + 3 * h + kc, 3 * kg + kc
                            if h == 0:
                                pe.wait_ge(act_lo, i * 12 + (c + 1))
                            pe.wait_ge(lo_done, i * 24 + (CH_DOWN + j + 1))
                            k0, nk = KCH[c]
                            for k in range(nk):
                                for n in range(2):
                                    w = slice(256 * k + P * n, 256 * k + P * n + P)
                                    at = (k0 + k) % KD
                                    last = three(ps[:, 2 * h + n, 0:TOK], whi[:, j % BUFS, w], wlo[:, j % BUFS, w],
                                                 hhi[:, at, :], hlo[:, at, :], k0 + k == 0, k0 + k == KF - 1)
                            last.then_inc(used, 1)
                pe.wait_ge(*DV_.upto("u1", i))
                for t in range(3):
                    m = P if t < 2 else NS
                    pe.wait_ge(*DA.upto(f"r{t}", i - 1))
                    for b in range(4):
                        last = turn(ps[0:m, 4 + t, P * b:P * b + P], yst[:, b, P * t:P * t + m], ident)
                    last.then_inc(*DT.step(f"t{t}"))

        @block.scalar
        def _(act):
            f = nc.scalar.activation
            for r, name in ((slice(0, 1), "c_prompt"), (slice(1, NC9), "c_sample")):
                act.dma_start(crow[r, :], a[name]).then_inc(c_in, 16)
            for s_ in (PA_, *NA, *NH, CA, AA, GA, TA, SA, RA, OA, FA, DA):
                act.sem_inc(s_.sem, len(s_.names))
            act.wait_ge(c_in, 32)
            f(crow, crow, ACT.Silu).then_inc(*PA_.step("silu_c"))

            def norm_square(n, j):
                if n == 0:
                    act.wait_ge(*PV_.upto(f"x{4 * j + 3}"))
                if j >= 2:
                    act.wait_ge(*NT[n].upto(f"s{j - 2}"))
                f(sq[:, j % 2], xT[:, 4 * j:4 * j + 4, :], ACT.Square).then_inc(*NA[n].step(f"q{j}"))

            def norm_root(n):
                act.wait_ge(*NM[n].upto("ms"))
                f(rs, rs, ACT.Ln).then_inc(*NA[n].step("ln"))
                act.wait_ge(*NA[n].upto("ln"))
                f(rs, rs, ACT.Exp, scale=-0.5).then_inc(*NA[n].step("rs"))

            def norm_hi(n, j):
                k = bass.ds(j * 4, 4)
                act.wait_ge(*NG[n].upto("d", j))
                f(hhi[:, k, :], hraw[:, k, :], ACT.Copy).then_inc(*NH[n].step("h"))

            def hi(i, j, slabs, chunks, turn=16, n=CHUNK, loads=None):
                s = j // 2
                act.wait_ge(full[s % SLOTS], i * (loads or 2 * turn) + (slabs // SLOTS + s // SLOTS + 1) * 16)
                act.wait_ge(used, i * turn + (chunks + j + 1))
                f(whi[:, j % BUFS, 0:n], ring[:, s % SLOTS, n * (j % 2):n * (j % 2) + n],
                  ACT.Copy).then_inc(hi_done, 1)

            def spent(i, chunks, j):
                act.wait_ge(used, i * 16 + (chunks + BUFS + j))

            act.wait_ge(*PV_.upto("c"))
            f(c18[:, :, 0:NC9], cT, ACT.Copy).then_inc(*CA.step("c_hi"))
            for j in range(LEAD):
                hi(0, j, 0, 0)

            def ada_turn(i, first):
                for j in range(LEAD, 16 + LEAD):
                    if not first and j == 4:
                        norm_hi(0, i - 1)
                    if j == 10:
                        spent(i, 0, 8)
                        act.wait_ge(*AT.upto("turn_b", i - 1))
                        f(mrow[:, :], ps[0:2 * NC9, 0, :], ACT.Copy).then_inc(*AA.step("rows_a"))
                    hi(i, j, 0, 0)
                    if first and j in (6, 10, 14, 17):
                        norm_square(0, (j - 5) // 4)
                    if first and j == 14:
                        act.wait_ge(wglr_in, 16)
                        f(ghi[:, :, :], wglr, ACT.Copy).then_inc(*CA.step("glr_hi"))
                spent(i, 0, 16)
                act.wait_ge(*AT.upto("turn_a", i))
                f(mrow[:, :], ps[0:2 * NC9, 1, :], ACT.Copy).then_inc(*AA.step("rows_b"))

            ada_turn(0, True)
            norm_root(0)
            with act.Fori(1, 4) as i:
                ada_turn(i, False)
            norm_hi(0, 3)

            def in_turn(i, lead):
                for j in range(LEAD, 16):
                    hi(i, j, SL_IN, CH_IN)
                    if j in (5, 13):
                        u = (j - 5) // 4
                        spent(i, CH_IN, 4 * u + 4)
                        act.wait_ge(*WV.upto("u1" if u else "u3", i if u else i - 1))
                        f(proj[:, bass.ds(i * 8 + 2 * u, 2), :], ps[:, 0:2, 0:TOK], ACT.Copy).then_inc(WV.sem, 1)
                for j in range(LEAD):
                    lead(j)

            with act.Fori(0, 2) as i:
                in_turn(i, lambda j: hi(i, 16 + j, SL_IN, CH_IN))
            in_turn(2, lambda j: hi(0, j, SL_IN2, CH_IN2, 8, 768))

            def pair(p, end):
                def his(lo, end):
                    for j in range(lo, end):
                        hi(p, j, SL_IN2, CH_IN2, 8, 768)

                his(2, 3)
                act.wait_ge(*TV.upto("ms", p))
                f(rsqk, rsqk, ACT.Ln).then_inc(*TA.step("ln"))
                act.wait_ge(*TA.upto("ln", p))
                f(rsqk, rsqk, ACT.Exp, scale=-0.5).then_inc(*TA.step("rs"))
                act.wait_ge(*TT.upto("kv_rows", p - 1))
                f(vst, proj[:, bass.ds(p + 16, 1), :].rearrange("p a c -> p (a c)"),
                  ACT.Copy).then_inc(*TA.step("vstage"))
                his(3, 7)
                act.wait_ge(*TV.upto("max", p))
                for e in range(2):
                    for q in range(2):
                        part = prob[:, e, P * q:P * q + P * (q + 1)]
                        c = 2 * e + q
                        last = f(part, part, ACT.Exp, bias=stat[:, c:c + 1], accum_out=stat[:, 4 + c:5 + c])
                last.then_inc(*TA.step("exp"))
                his(7, 8)
                act.wait_ge(*TT.upto("probT", p))
                act.wait_ge(*TT.upto("out", p - 1))
                f(probT, ps[:, 6:8, 0:384], ACT.Copy).then_inc(*TA.step("probT"))
                his(8, end)
                act.wait_ge(used, p * 8 + (CH_IN2 + BUFS + 8))
                f(proj[:, bass.ds(p * 3 + 24, 3), :], ps[:, 0:3, 0:TOK], ACT.Copy).then_inc(*TA.step("evac"))

            with act.Fori(0, PAIRS - 1) as p:
                pair(p, 8 + LEAD)
            pair(PAIRS - 1, 8)
            act.wait_ge(*GT.upto("done"))
            act.wait_ge(*TV.upto("out", PAIRS - 1))
            f(glrT, ps[0:RANK, 4, 0:TOK], ACT.Copy).then_inc(*GA.step("rows"))
            act.wait_ge(*TA.upto("evac", PAIRS - 1))
            f(proj[:, 40:48, :], proj[:, 40:48, :], ACT.Silu).then_inc(*GA.step("silu_r"))

            def key_copy(g, n):
                act.wait_ge(*ST.upto(f"k{n}", g))
                if n >= 2:
                    act.wait_ge(*ST.upto(f"s{n - 2}", g))
                act.wait_ge(*SK.upto(f"k{n - 1 if n else 15}", g if n else g - 1))
                f(kcT[:, 0, 0:512], ps[:, 0, :], ACT.Copy)
                f(kcT[:, 0, CK:CK + NS], kS[:, 4 * (n // 4 % 2) + n % 4, :], ACT.Copy)
                f(kcT[:, 0, 512:CK], ps[:, 1, 0:P], ACT.Copy).then_inc(SK.sem, 1)

            def softmax(g):
                act.wait_ge(*SV.upto("max", g))
                f(sc, sc, ACT.Exp, bias=stat[:, 0:1], accum_out=stat[:, 1:2]).then_inc(*SA.step("exp"))

            def output(g):
                act.wait_ge(*SO.upto("probT", g))
                act.wait_ge(*SO.upto("v3", g - 1))
                f(sT[:, 0:4, :].rearrange("p t c -> p (t c)"), ps[:, 6, :], ACT.Copy)
                f(sT[:, 4, :], ps[:, 7, 0:P], ACT.Copy)
                f(sT[0:NS, 5, :], ps[0:NS, 7, P:2 * P], ACT.Copy).then_inc(*SA.step("probT"))
                act.wait_ge(*SO.upto("v3", g))
                act.wait_ge(*SO.upto("oT", g - 1))
                f(orow, ps[:, 7, :], ACT.Copy).then_inc(*SA.step("orow"))

            key_copy(0, 0)
            key_copy(0, 2)
            with act.Fori(0, NB // 2 - 1) as g:
                for n in range(4, 16, 2):
                    key_copy(g, n)
                key_copy(g + 1, 0)
                softmax(g)
                key_copy(g + 1, 2)
                output(g)
            for n in range(4, 16, 2):
                key_copy(NB // 2 - 1, n)
            softmax(NB // 2 - 1)
            output(NB // 2 - 1)

            act.wait_ge(*SV.upto("out", 3))
            for n in range(2):
                f(proj[:, 8 + 4 * n:12 + 4 * n, :], proj[:, 4 * n:4 * n + 4, :], ACT.Square).then_inc(*OA.step(f"sq{n}"))
            for n in range(2):
                m = proj[:, 8 + 4 * n:12 + 4 * n, :]
                act.wait_ge(*OV.upto(f"ms{n}"))
                f(m, m, ACT.Ln).then_inc(*OA.step(f"ln{n}"))
            for n in range(2):
                m = proj[:, 8 + 4 * n:12 + 4 * n, :]
                act.wait_ge(*OA.upto(f"ln{n}"))
                f(m, m, ACT.Exp, scale=-0.5).then_inc(*OA.step(f"rs{n}"))
            for n in range(2):
                act.wait_ge(*OV.upto(f"done{n}"))
                f(hhi[:, 4 * n:4 * n + 4, :], proj[:, 4 * n:4 * n + 4, :], ACT.Copy).then_inc(*OA.step(f"hi{n}"))
            act.wait_ge(*OV.upto("lo1"))

            with act.Fori(0, H_B) as h:
                cum, cums = cumz[:, 1:1 + SEQ], cumz[:, 1 + SEQ:1 + TOK]

                def his(lo, end):
                    for j in range(lo, end):
                        hi(h, j, SL_ADA2 + 4, CH_ADA2, 24, loads=64)

                def rows(g):
                    if g:
                        act.wait_ge(used, h * 24 + (CH_ADA2 + BUFS + 8 * g))
                    else:
                        act.wait_ge(raw_used, h * 4 + 4)
                    act.wait_ge(*RT.upto(f"turn{(g - 1) % 4}", h if g else h - 1))
                    f(mrow[:, :], ps[0:2 * NC9, 7, :], ACT.Copy).then_inc(*RA.step(f"rows{g}"))

                act.wait_ge(*RT.upto("vrows", h - 1))
                f(vbst, proj[:, bass.ds(h * 2 + 32, 2), :], ACT.Copy).then_inc(*RA.step("vstage"))
                act.wait_ge(*RV.upto("z", h))
                f(ex, zb, ACT.Abs).then_inc(*RA.step("abs"))
                act.wait_ge(*RA.upto("abs", h))
                f(ex, ex, ACT.Exp, scale=-1.0).then_inc(*RA.step("exp"))
                act.wait_ge(*RA.upto("exp", h))
                f(ex, ex, ACT.Ln, bias=1.0).then_inc(*RA.step("ln"))
                act.wait_ge(*RT.upto("vrows", h))
                act.wait_ge(*RV.upto("o1", h - 1))
                f(vbr[:, 0:2, :].rearrange("p t c -> p (t c)"), ps[:, 1, :], ACT.Copy)
                f(vbr[0:NS, 2, :], ps[0:NS, 2, 0:256], ACT.Copy).then_inc(*RA.step("vrows"))
                act.wait_ge(*RV.upto("dd", h))
                f(qp, qp, ACT.Exp, scale=1 / TAU).then_inc(*RA.step("eq"))
                f(qe, cums, ACT.Exp, scale=1 / TAU).then_inc(*RA.step("eqs"))
                f(ke, cums, ACT.Exp, scale=-1 / TAU).then_inc(*RA.step("eks"))
                f(kd[:, 0:SEQ], cum, ACT.Exp, scale=-1 / TAU, bias=rb[:, 8:9]).then_inc(*RA.step("ekd"))
                f(kd[:, SEQ:TOK], kd[:, SEQ:TOK], ACT.Exp, scale=1 / TAU).then_inc(*RA.step("ekds"))
                f(dec, cums.rearrange("p (b t) -> p b t", t=TS)[:, :, TS - 1], ACT.Exp,
                  scale=1 / TAU).then_inc(*RA.step("dec"))
                his(0, 2)
                for c in range(8):
                    if c >= 2:
                        act.wait_ge(*RT.upto(f"att{c - 2}", h))
                    n = 32 * (c + 1)
                    f(ki[:, c % 2, 0:n], cum[:, 0:n], ACT.Exp, scale=-1 / TAU,
                      bias=rb[:, c:c + 1]).then_inc(*RA.step(f"ki{c}"))
                    if c == 1:
                        his(2, 4)
                        rows(0)
                his(4, 8)
                act.wait_ge(*RT.upto("o", h))
                for v in range(2):
                    last = f(sqo[:, v, :], ps[:, 4 + v, 0:TOK], ACT.Square)
                last.then_inc(*RA.step("sq"))
                his(8, 10)
                rows(1)
                his(10, 12)
                act.wait_ge(*RT.upto("states", h))
                act.wait_ge(stp_stored, h + 1)
                f(stp, ps[:, 0, 0:DV], ACT.Copy).then_inc(*RA.step("stp"))
                his(12, 18)
                act.wait_ge(*RV.upto("ms", h))
                f(rso, rso, ACT.Ln).then_inc(*RA.step("lnr"))
                act.wait_ge(*RA.upto("lnr", h))
                f(rso, rso, ACT.Exp, scale=-0.5).then_inc(*RA.step("rs"))
                rows(2)
                his(18, 24)
                rows(3)
            act.wait_ge(*RV.upto("o1", 3))
            f(hhi[:, 8:16, :], proj[:, 40:48, :], ACT.Copy).then_inc(*OA.step("gla_hi"))

            for j in range(LEAD):
                hi(0, j, SL_OUT, CH_OUT)
            act.wait_ge(*OV.upto("gla_lo"))
            for i in range(2):
                for j in range(LEAD, 16 + LEAD):
                    hi(i, j, SL_OUT, CH_OUT)
                    if j == 14 or i and j == 6:
                        act.wait_ge(*UV.upto("u1" if j == 14 else "u3", i if j == 14 else i - 1))
                        norm_square(1, 2 * i if j == 14 else 2 * i - 1)
            act.wait_ge(*UV.upto("u3", 1))
            norm_square(1, 3)
            act.wait_ge(s0_out, 64)
            act.wait_ge(stp_out, 64)
            for j in range(LEAD, 4):
                hi(0, j, SL_UP, CH_UP)
            norm_root(1)
            for j in range(4):
                norm_hi(1, j)

            def up_turn(i, split):
                def his(lo, end):
                    for j in range(lo, end):
                        hi(i, j, SL_UP, CH_UP)

                def gate(n):
                    spent(i, CH_UP, 8 * n + 4)
                    act.wait_ge(*FV.upto("last", i - 1))
                    f(gpad[:, 2 * n:2 * n + 2, 2:2 + SEQ], ps[:, 0:2, 0:SEQ], ACT.Copy)
                    f(gpad[:, 2 * n:2 * n + 2, 2 + SEQ:GW].rearrange("p n (b t) -> p n b t", t=6)[:, :, :, 2:6],
                      ps[:, 0:2, SEQ:TOK].rearrange("p n (b t) -> p n b t", t=TS),
                      ACT.Copy).then_inc(*FA.step(f"g{n}"))

                def silu(n):
                    act.wait_ge(*FV.upto(f"conv{n}", i))
                    f(cv, cv, ACT.Silu).then_inc(*FA.step(f"silu{n}"))

                his(split, 6)
                gate(0)
                his(6, 8)
                silu(0)
                his(8, 14)
                gate(1)
                his(14, 16)
                silu(1)
                his(16, 18)
                act.wait_ge(*FT.upto("rows", i))
                act.wait_ge(conv_stored, i + 1)
                f(crows, ps[0:18, 5, :], ACT.Copy).then_inc(*FA.step("rows"))

            up_turn(0, 4)
            with act.Fori(1, 11) as i:
                up_turn(i, LEAD)

            def act_parts(c, wait, i):
                act.wait_ge(used, wait)
                for k0, at, m in pieces(*KCH[c]):
                    last = f(hhi[:, at:at + m, :], actT[:, k0:k0 + m, :], ACT.Copy)
                last.then_inc(act_hi, 1)

            def down_hi(i, j):
                jj = j % 24
                kg, h, kc = jj // 6, jj // 3 % 2, jj % 3
                s = 2 * kg + h
                act.wait_ge(full[s % SLOTS], i * 32 + (SL_DOWN // SLOTS * 16 + 32 * (j // 24) + 16 * (s // SLOTS) + 16))
                act.wait_ge(used, i * 24 + (CH_DOWN + j + 1))
                n = 256 * KCH[3 * kg + kc][1]
                f(whi[:, jj % BUFS, 0:n], ring[:, s % SLOTS, CHUNK * kc:CHUNK * kc + n],
                  ACT.Copy).then_inc(hi_done, 1)

            def down_turn(i, end):
                for j in range(LEAD, end):
                    jj = j % 24
                    if jj // 3 % 2 == 0:
                        c = 3 * (jj // 6) + jj % 3
                        act_parts(c, i * 24 + (CH_DOWN + BUFS + 24 * (j // 24) + last_use(c)), i)
                    down_hi(i, j)

            act.wait_ge(*FV.upto("act1", 10))
            spent(0, CH_DOWN, 0)
            for c in range(LEAD):
                act_parts(c, CH_DOWN + BUFS, 0)
            with act.Fori(0, 3) as i:
                down_turn(i, 24 + LEAD)
                for t in range(3):
                    act.wait_ge(*DT.upto(f"t{t}", i))
                    act.wait_ge(y_stored, i * 3 + (t if t else 1))
                    m = P if t < 2 else NS
                    f(yrow[0:m, t % 2, :], ps[0:m, 4 + t, :], ACT.Copy).then_inc(*DA.step(f"r{t}"))
            down_turn(3, 24)
            for t in range(3):
                act.wait_ge(*DT.upto(f"t{t}", 3))
                act.wait_ge(y_stored, 9 + (t if t else 1))
                m = P if t < 2 else NS
                f(yrow[0:m, t % 2, :], ps[0:m, 4 + t, :], ACT.Copy).then_inc(*DA.step(f"r{t}"))

        @block.vector
        def _(dve):
            v = nc.vector
            for s_ in (PV_, *NM, *NG, *NL, CV, AV, WV, TV, SQ, SV, SK, RV, OV, UV, FV, FZ, DV_):
                dve.sem_inc(s_.sem, len(s_.names))
            dve.wait_ge(*PT_.upto("c"))
            v.tensor_copy(cT.rearrange("p k c -> p (k c)"), ps[:, 4, 0:KD * NC9]).then_inc(*PV_.step("c"))
            dve.wait_ge(*CA.upto("c_hi"))
            v.tensor_tensor(c18[:, :, NC9:2 * NC9], cT, c18[:, :, 0:NC9].bitcast(F32),
                            ALU.subtract).then_inc(*CV.step("c_lo"))
            def x_copy(k):
                dve.wait_ge(*PT_.upto(f"x{k}"))
                v.tensor_copy(xT[:, k, :], ps[:, 5 + k % 3, 0:TOK]).then_inc(*PV_.step(f"x{k}"))

            def biases():
                v.memset(rel_rows, 0.0).then_inc(*PV_.step("zero_rel"))
                dve.wait_ge(*PV_.upto("zero_rel"))
                dve.wait_ge(rel_in, 64)
                for t in range(TS):
                    b = slice(32 * t, 32 * t + 32)
                    dst = rel_rows[b, :].rearrange("p (b h t) -> p b h t", b=2, h=H_A)[:, :, :, t]
                    src = relb[b, :].rearrange("p (a h) -> p a h", a=1).to_broadcast([32, 2, H_A])
                    last = v.tensor_copy(dst, src)
                last.then_inc(*PV_.step("rel_rows"))
                dve.wait_ge(*PT_.upto("bias_p"))
                v.tensor_tensor(btab, ps[0:H_A, 5, :], tview("mult_p", H_A), ALU.add).then_inc(*PV_.step("bias_p"))
                dve.wait_ge(*PT_.upto("bias_s"))
                ms = tview("mult_s", P)
                v.tensor_tensor(bias_s[:, 0:512], ps[:, 6, :], ms[:, 0:512], ALU.add)
                v.tensor_tensor(bias_s[:, 512:CK], ps[:, 7, 0:P], ms[:, 512:CK], ALU.add).then_inc(*PV_.step("bias_s0"))
                new = ps[:, 7, P:P + NS].rearrange("p (a c) -> p a c", a=1).to_broadcast([P, 4, NS])
                v.tensor_tensor(bias_s[:, CK:].rearrange("p (g c) -> p g c", g=4), new,
                                ms[:, CK:].rearrange("p (g c) -> p g c", g=4), ALU.add).then_inc(*PV_.step("bias_s"))

            def lo(i, j, chunks, turn=16, n=CHUNK):
                s = j // 2
                dve.wait_ge(hi_done, i * turn + (chunks + j + 1))
                v.tensor_tensor(wlo[:, j % BUFS, 0:n], ring[:, s % SLOTS, n * (j % 2):n * (j % 2) + n],
                                whi[:, j % BUFS, 0:n].bitcast(F32), ALU.subtract).then_inc(lo_done, 1)

            def spent(i, chunks, j):
                dve.wait_ge(used, i * 16 + (chunks + BUFS + j))

            def mod(i):
                tiles = [(i * 4 + KD * n, ps[:, 2 + n, 0:72].rearrange("p (n c) -> p n c", n=4)) for n in range(2)]
                for t, src in tiles:
                    bias = small[:, bass.ds(t + BA, 4)].rearrange("p (n a) -> p n a", a=1)
                    last = v.tensor_tensor(modT[:, bass.ds(t, 4), :], src[:, :, 0:NC9],
                                           bias.to_broadcast([P, 4, NC9]), ALU.add)
                last.then_inc(*AV.step("base"))
                dve.wait_ge(*AV.upto("base", i))
                for t, src in tiles:
                    last = v.tensor_tensor(modT[:, bass.ds(t, 4), :], src[:, :, NC9:2 * NC9],
                                           modT[:, bass.ds(t, 4), :], ALU.add)
                last.then_inc(*AV.step("mod"))

            def norm_mean(n, bank):
                dve.wait_ge(*NT[n].upto("s3"))
                v.tensor_scalar(rs, ps[:, bank, 0:TOK], 1 / D, EPS, ALU.mult, ALU.add).then_inc(*NM[n].step("ms"))

            def norm_group(n, j):
                sh, scl, g = (0, KD, N1) if n == 0 else (3 * KD, 4 * KD, N2)
                N = NG[n]
                ks = bass.ds(j * 4, 4)
                gain = small[:, bass.ds(j * 4 + g, 4)].rearrange("p (k a) -> p k a", a=1).to_broadcast([P, 4, NC9])
                scale = modT[:, bass.ds(j * 4 + scl, 4), :]
                v.scalar_tensor_tensor(out=scale, in0=scale, scalar=1.0, in1=gain, op0=ALU.add,
                                       op1=ALU.mult).then_inc(*N.step("scale"))
                r = rs.rearrange("p (a c) -> p a c", a=1).to_broadcast([P, 4, TOK])
                dve.wait_ge(*NA[n].upto("rs"))
                v.tensor_tensor(hraw[:, ks, :], xT[:, ks, :], r, ALU.mult).then_inc(*N.step("t"))
                dve.wait_ge(*N.upto("t", j))
                for k in range(4):
                    one = lambda t, k=k: modT[:, bass.ds(j * 4 + (t + k), 1), 0:1].rearrange("p a b -> p (a b)")
                    h = hraw[:, bass.ds(j * 4 + k, 1), 0:SEQ].rearrange("p a c -> p (a c)")
                    last = v.tensor_scalar(h, h, one(scl), one(sh), ALU.mult, ALU.add)
                last.then_inc(*N.step("p"))
                hs = hraw[:, ks, SEQ:TOK].rearrange("p k (b t) -> p k b t", t=TS)
                for k0, name in ((scl, "s"), (sh, "d")):
                    m = modT[:, bass.ds(j * 4 + k0, 4), 1:NC9].rearrange("p k (b a) -> p k b a", a=1)
                    v.tensor_tensor(hs, hs, m.to_broadcast([P, 4, NB, TS]),
                                    ALU.mult if k0 == scl else ALU.add).then_inc(*N.step(name))
                    if name == "s":
                        dve.wait_ge(*N.upto(name, j))

            def norm_lo(n, j):
                ks = bass.ds(j * 4, 4)
                dve.wait_ge(*NH[n].upto("h", j))
                v.tensor_tensor(hlo[:, ks, :], hraw[:, ks, :], hhi[:, ks, :].bitcast(F32),
                                ALU.subtract).then_inc(*NL[n].step("l"))

            def ada_turn(i, first):
                for j in range(0 if first else LEAD, 16 + LEAD):
                    lo(i, j, 0)
                    if first and j < 16:
                        x_copy(j)
                    if first and j == 7:
                        dve.wait_ge(*PT_.upto("vectors"))
                        v.tensor_copy(small[:, :], ps[:, 3, 0:313]).then_inc(*PV_.step("vectors"))
                    if not first and j == 3:
                        norm_lo(0, i - 1)
                if first:
                    norm_mean(0, 4)
                    biases()
                    dve.wait_ge(*CA.upto("glr_hi"))
                    v.tensor_tensor(glo[:, :, :], wglr, ghi[:, :, :].bitcast(F32),
                                    ALU.subtract).then_inc(*CV.step("glr_lo"))
                dve.wait_ge(*AT.upto("turn_b", i))
                mod(i)
                dve.wait_ge(*AV.upto("mod", i))
                norm_group(0, i)

            ada_turn(0, True)
            with dve.Fori(1, 4) as i:
                ada_turn(i, False)
            norm_lo(0, 3)

            def in_turn(i, lead):
                for j in range(LEAD, 16 + LEAD):
                    if j < 16:
                        lo(i, j, CH_IN)
                    else:
                        lead(j - 16)
                    if j in (9, 15 + LEAD):
                        u = 1 if j == 9 else 3
                        spent(i, CH_IN, 4 * u + 4)
                        dve.wait_ge(*WV.upto(f"u{u - 1}", i))
                        v.tensor_copy(proj[:, bass.ds(i * 8 + 2 * u, 2), :], ps[:, 2:4, 0:TOK]).then_inc(WV.sem, 1)

            with dve.Fori(0, 2) as i:
                in_turn(i, lambda j: lo(i, 16 + j, CH_IN))
            in_turn(2, lambda j: lo(0, j, CH_IN2, 8, 768))

            pg = proj[:, :, :].rearrange("p (g n) c -> p g n c", n=8)
            dve.wait_ge(*WV.upto("u3", 2))

            def two_pairs(i, end):
                for par in range(2):
                    p = i * 2 + par

                    def los(first, last):
                        for j in range(first, last):
                            lo(p, j, CH_IN2, 8, 768)

                    qk = pg[:, 0:2, bass.ds(p, 1), :].rearrange("p g a c -> p g (a c)")
                    v.tensor_tensor(sqqk, qk, qk, ALU.mult).then_inc(*TV.step("squares"))
                    los(2, 3)
                    dve.wait_ge(*TT.upto("sums", p))
                    v.tensor_scalar(rsqk, ps[:, 4:6, 0:TOK], 1 / HD, EPS, ALU.mult, ALU.add).then_inc(*TV.step("ms"))
                    dve.wait_ge(*TA.upto("rs", p))
                    for g, name in enumerate("qk"):
                        v.scalar_tensor_tensor(
                            out=qkst[:, g, :], in0=proj[:, bass.ds(p + 8 * g, 1), :].rearrange("p a c -> p (a c)"),
                            scalar=small[:, QG + g:QG + g + 1], in1=rsqk[:, g, :], op0=ALU.mult,
                            op1=ALU.mult).then_inc(*TV.step(name))
                    dve.wait_ge(*TV.upto("k", p))
                    for g, dst in enumerate((qS, kS)):
                        last = v.tensor_copy(dst[:, bass.ds(p, 1), :].rearrange("p a c -> p (a c)"),
                                             qkst[:, g, SEQ:TOK])
                    last.then_inc(*TV.step("samples"))
                    los(3, 4)
                    dve.wait_ge(*TT.upto("kv_rows", p))
                    for g, (dst, name) in enumerate(((krows, "krows"), (vrows, "vrows"))):
                        dve.wait_ge(kv_stored, p + 1)
                        v.tensor_copy(dst[:, 0:2, :], ps[:, 6 + g, 0:256].rearrange("p (t c) -> p t c", t=2))
                        v.tensor_copy(dst[0:NS, 2, :], ps[0:NS, 6 + g, 256:384]).then_inc(*TV.step(name))
                    los(4, 5)
                    dve.wait_ge(*TT.upto("scores", p))
                    dve.wait_ge(biasp_in[par], i * 16 + 16)
                    for e in range(2):
                        v.scalar_tensor_tensor(out=prob[:, e, 0:P], in0=ps[:, 4 + e, 0:P], scalar=HD ** -0.5,
                                               in1=bias_p[:, par, e, P:SEQ], op0=ALU.mult, op1=ALU.add)
                        last = v.scalar_tensor_tensor(out=prob[:, e, P:3 * P], in0=ps[:, 4 + e, P:3 * P],
                                                      scalar=HD ** -0.5, in1=bias_p[:, par, e, :], op0=ALU.mult,
                                                      op1=ALU.add)
                    last.then_inc(*TV.step("biased"))
                    dve.wait_ge(*TV.upto("biased", p))
                    for e in range(2):
                        for q in range(2):
                            c = 2 * e + q
                            last = v.tensor_reduce(out=stat[:, c:c + 1], in_=prob[:, e, P * q:P * q + P * (q + 1)],
                                                   axis=AX_X, op=ALU.max, negate=True)
                    last.then_inc(*TV.step("max"))
                    los(5, 6)
                    dve.wait_ge(*TA.upto("exp", p))
                    v.reciprocal(stat[:, 8:12], stat[:, 4:8]).then_inc(*TV.step("recip"))
                    dve.wait_ge(*TV.upto("recip", p))
                    for e in range(2):
                        for q in range(2):
                            c = 2 * e + q
                            part = prob[:, e, P * q:P * q + P * (q + 1)]
                            last = v.tensor_scalar(part, part, stat[:, 8 + c:9 + c], None, ALU.mult)
                    last.then_inc(*TV.step("norm"))
                    los(6, end if par else 8 + LEAD)
                    dve.wait_ge(*TT.upto("out", p))
                    dve.sem_inc(copy_turns, 1)
                    for e in range(2):
                        h = slice(HD * e, HD * e + HD)
                        last = v.tensor_copy(proj[h, bass.ds(p, 1), 0:SEQ].rearrange("p a c -> p (a c)"),
                                             ps[h, 4 + e, 0:SEQ])
                    last.then_inc(*TV.step("out"))

            with dve.Fori(0, PAIRS // 2 - 1) as i:
                two_pairs(i, 8 + LEAD)
            two_pairs(PAIRS // 2 - 1, 8)

            dve.wait_ge(*PV_.upto("bias_s"))
            dve.wait_ge(*TT.upto("kv_rows", PAIRS - 1))
            v.memset(qd, 0.0).then_inc(*FZ.step("zero_qd"))
            dve.wait_ge(*FZ.upto("zero_qd"))
            def queries(g):
                dve.wait_ge(*ST.upto("s15", g - 1))
                for e in range(2):
                    h = slice(HD * e, HD * e + HD)
                    for b in range(2):
                        src = qS[h, :, bass.ds(g * 8 + TS * b, TS)].rearrange("p (h j) t -> p h j t", h=2)
                        last = v.tensor_copy(qd_blocks(qd, h, 256 * b + TS * e), src)
                last.then_inc(*SQ.step("qd"))

            def key_copy(g, n):
                dve.wait_ge(*ST.upto(f"k{n}", g))
                if n >= 2:
                    dve.wait_ge(*ST.upto(f"s{n - 2}", g))
                dve.wait_ge(*SK.upto(f"k{n - 1}", g))
                v.tensor_copy(kcT[:, 1, 0:512], ps[:, 2, :])
                v.tensor_copy(kcT[:, 1, CK:CK + NS], kS[:, 4 * (n // 4 % 2) + n % 4, :])
                v.tensor_copy(kcT[:, 1, 512:CK], ps[:, 3, 0:P]).then_inc(SK.sem, 1)

            def maxima(g):
                dve.wait_ge(*ST.upto("s15", g))
                dve.wait_ge(*SO.upto("probT", g - 1))
                sd = HD ** -0.5
                for out, src, bias in ((sc[:, 0:512], ps[:, 4, :], bias_s[:, 0:512]),
                                       (sc[:, 512:CK], ps[:, 5, 0:P], bias_s[:, 512:CK]),
                                       (sc[:, CK:CK + NS], ps[:, 5, P:160], bias_s[:, bass.ds(g * NS + CK, NS)])):
                    last = v.scalar_tensor_tensor(out=out, in0=src, scalar=sd, in1=bias, op0=ALU.mult, op1=ALU.add)
                last.then_inc(*SV.step("biased"))
                dve.wait_ge(*SV.upto("biased", g))
                v.tensor_reduce(out=stat[:, 0:1], in_=sc, axis=AX_X, op=ALU.max,
                                negate=True).then_inc(*SV.step("max"))

            def norm_scores(g):
                dve.wait_ge(*SA.upto("exp", g))
                v.reciprocal(stat[:, 2:3], stat[:, 1:2]).then_inc(*SV.step("recip"))
                dve.wait_ge(*SV.upto("recip", g))
                v.tensor_scalar(sc, sc, stat[:, 2:3], None, ALU.mult).then_inc(*SV.step("norm"))

            def output(g):
                dve.wait_ge(*SO.upto("oT", g))
                for e in range(2):
                    h = slice(HD * e, HD * e + HD)
                    for u in range(4):
                        b = u // 2
                        last = v.tensor_copy(
                            proj[h, 4 * (u % 2):4 * (u % 2) + 4, bass.ds(g * 8 + (SEQ + TS * b), TS)],
                            own_heads(ps, h, 32 * u + TS * e))
                last.then_inc(*SV.step("out"))

            queries(0)
            key_copy(0, 1)
            key_copy(0, 3)
            with dve.Fori(0, NB // 2 - 1) as g:
                for n in range(5, 16, 2):
                    key_copy(g, n)
                maxima(g)
                queries(g + 1)
                key_copy(g + 1, 1)
                norm_scores(g)
                key_copy(g + 1, 3)
                output(g)
            for n in range(5, 16, 2):
                key_copy(NB // 2 - 1, n)
            maxima(NB // 2 - 1)
            norm_scores(NB // 2 - 1)
            output(NB // 2 - 1)

            for n in range(2):
                k = slice(4 * n, 4 * n + 4)
                dve.wait_ge(*OT.upto(f"sums{n}"))
                v.tensor_scalar(proj[:, 8 + 4 * n:12 + 4 * n, :], ps[:, k, 0:TOK], 1 / HD, EPS, ALU.mult,
                                ALU.add).then_inc(*OV.step(f"ms{n}"))
            for n in range(2):
                k = slice(4 * n, 4 * n + 4)
                dve.wait_ge(*OA.upto(f"rs{n}"))
                v.scalar_tensor_tensor(out=proj[:, k, :], in0=proj[:, k, :], scalar=small[:, AO:AO + 1],
                                       in1=proj[:, 8 + 4 * n:12 + 4 * n, :], op0=ALU.mult,
                                       op1=ALU.mult).then_inc(*OV.step(f"done{n}"))
            for n in range(2):
                k = slice(4 * n, 4 * n + 4)
                dve.wait_ge(*OA.upto(f"hi{n}"))
                v.tensor_tensor(hlo[:, k, :], proj[:, k, :], hhi[:, k, :].bitcast(F32),
                                ALU.subtract).then_inc(*OV.step(f"lo{n}"))

            dve.wait_ge(*OV.upto("lo1"))
            kept = keep_g[:, SEQ:TOK].rearrange("p (b t) -> p b t", t=TS)
            v.memset(cumz[:, 0:1], 0.0)
            v.memset(keep_g[:, 0:SEQ], 1.0)
            v.memset(kept[:, :, 1:TS], 1.0)
            v.memset(kept[:, :, 0:1], 0.0).then_inc(*FZ.step("keep"))
            dve.wait_ge(*FZ.upto("keep"))
            dve.wait_ge(wg2_in, 16)
            with dve.Fori(0, H_B) as h:
                def los(first, end):
                    for j in range(first, end):
                        lo(h, j, CH_ADA2, 24)

                def file(g):
                    tiles = modT[:, bass.ds(h * 16 + (2 * KD + 4 * g), 4), :]
                    src = ps[:, 7, 0:72].rearrange("p (n c) -> p n c", n=4)
                    bias = small[:, bass.ds(h * 16 + (BA + 2 * KD + 4 * g), 4)].rearrange("p (n a) -> p n a", a=1)
                    dve.wait_ge(*RT.upto(f"turn{g}", h))
                    v.tensor_tensor(tiles, src[:, :, 0:NC9], bias.to_broadcast([P, 4, NC9]),
                                    ALU.add).then_inc(*RV.step(f"base{g}"))
                    dve.wait_ge(*RV.upto(f"base{g}", h))
                    v.tensor_tensor(tiles, src[:, :, NC9:2 * NC9], tiles, ALU.add).then_inc(*RV.step(f"mod{g}"))

                cum = cumz[:, 1:1 + TOK]
                qb = proj[:, bass.ds(h + 24, 1), :].rearrange("p a c -> p (a c)")
                kb = proj[:, bass.ds(h + 28, 1), :].rearrange("p a c -> p (a c)")
                dve.wait_ge(*RT.upto("z", h - 1))
                v.tensor_copy(wgs, wg2[:, bass.ds(h * P, P)]).then_inc(*RV.step("wgs"))
                dve.wait_ge(*RT.upto("z", h))
                v.tensor_scalar(zb, ps[:, 0, 0:TOK], small[:, bass.ds(h + BG, 1)], None,
                                ALU.add).then_inc(*RV.step("z"))
                dve.wait_ge(*RA.upto("ln", h))
                v.scalar_tensor_tensor(out=ex, in0=zb, scalar=0.0, in1=ex, op0=ALU.min,
                                       op1=ALU.subtract).then_inc(*RV.step("la"))
                dve.wait_ge(*RV.upto("la", h))
                v.tensor_tensor_scan(cum, keep_g, ex, 0.0, ALU.mult, ALU.add).then_inc(*RV.step("cum"))
                dve.wait_ge(*RV.upto("cum", h))
                mid = cum[:, 15:SEQ:32]
                v.tensor_scalar(rb[:, 0:8], mid, 1 / TAU, None, ALU.mult)
                v.tensor_scalar(rb[:, 8:9], cum[:, SEQ - 1:SEQ], 1 / TAU, None, ALU.mult).then_inc(*RV.step("rb"))
                v.tensor_tensor(qp.rearrange("p (n c) -> p n c", c=32),
                                cum[:, 0:SEQ].rearrange("p (n c) -> p n c", c=32),
                                mid.rearrange("p (n a) -> p n a", a=1).to_broadcast([P, 8, 32]),
                                ALU.subtract).then_inc(*RV.step("dq"))
                cs = cum[:, SEQ:TOK].rearrange("p (b t) -> p b t", t=TS)
                v.tensor_tensor(kd[:, SEQ:TOK].rearrange("p (b t) -> p b t", t=TS),
                                cs[:, :, TS - 1:TS].to_broadcast([P, NB, TS]), cs,
                                ALU.subtract).then_inc(*RV.step("dd"))
                sd = DK ** -0.5
                dve.wait_ge(*RA.upto("dec", h))
                v.scalar_tensor_tensor(out=qp, in0=qb[:, 0:SEQ], scalar=sd, in1=qp, op0=ALU.mult,
                                       op1=ALU.mult).then_inc(*RV.step("qp"))
                v.scalar_tensor_tensor(out=qe, in0=qb[:, SEQ:TOK], scalar=sd, in1=qe, op0=ALU.mult,
                                       op1=ALU.mult).then_inc(*RV.step("qe"))
                v.tensor_tensor(ke, kb[:, SEQ:TOK], ke, ALU.mult).then_inc(*RV.step("ke"))
                v.tensor_tensor(kd, kb, kd, ALU.mult).then_inc(*RV.step("kd"))
                v.memset(ps[:, 3, 0:384], 0.0).then_inc(*RV.step("zero_att"))
                dve.wait_ge(*RV.upto("zero_att", h))
                los(0, 2)
                for c in range(8):
                    dve.wait_ge(*RA.upto(f"ki{c}", h))
                    n = 32 * (c + 1)
                    v.tensor_tensor(ki[:, c % 2, 0:n], kb[:, 0:n], ki[:, c % 2, 0:n],
                                    ALU.mult).then_inc(*RV.step(f"ki{c}"))
                    if c == 1:
                        los(2, 4)
                    if c == 3:
                        file(0)
                dve.wait_ge(*RT.upto("att7", h))
                v.tensor_tensor(attT, ps[:, 3, 0:384], causal, ALU.mult).then_inc(*RV.step("att"))
                v.tensor_tensor(attS, ps[0:NS, 3, 384:384 + NS], causal_s, ALU.mult).then_inc(*RV.step("att_s"))
                los(4, 5)
                dve.wait_ge(*RT.upto("kdrows", h))
                v.tensor_copy(kdr[:, 0:2, :].rearrange("p t c -> p (t c)"), ps[:, 6, 0:256])
                v.tensor_copy(kdr[0:NS, 2, :], ps[0:NS, 6, 256:384]).then_inc(*RV.step("kdr"))
                dve.wait_ge(*RV.upto("kdr", h))
                v.tensor_tensor(kdm.rearrange("p (b c) -> p b c", b=NB),
                                kdr[0:NS, 2:3, :].to_broadcast([NS, NB, P]),
                                own_batch.rearrange("p (b a) -> p b a", a=1).to_broadcast([NS, NB, P]),
                                ALU.mult).then_inc(*RV.step("kdm"))
                los(5, 10)
                dve.wait_ge(*RT.upto("states", h))

                def new_state(b):
                    return v.scalar_tensor_tensor(out=s0[:, b, :], in0=s0[:, b, :], scalar=dec[:, b:b + 1],
                                                  in1=states(b), op0=ALU.mult, op1=ALU.add)

                new_state(7).then_inc(*RV.step("last_state"))
                file(1)
                los(10, 12)
                for b in range(6):
                    new_state(b)
                dve.wait_ge(*RA.upto("stp", h))
                new_state(6).then_inc(*RV.step("new_state"))
                los(12, 18)
                dve.wait_ge(*RT.upto("sum", h))
                v.tensor_scalar(rso[:, 0:SEQ], ps[:, 3, 0:SEQ], 1 / DV, EPS, ALU.mult, ALU.add)
                v.tensor_scalar(rso[:, SEQ:TOK], ps[:, 4, TOK:TOK + NS], 1 / DV, EPS, ALU.mult,
                                ALU.add).then_inc(*RV.step("ms"))
                dve.wait_ge(*RA.upto("rs", h))
                for j in range(2):
                    r = proj[:, bass.ds(h * 2 + 40 + j, 1), :].rearrange("p a c -> p (a c)")
                    tmp = sqo[:, j, :]
                    v.scalar_tensor_tensor(out=tmp, in0=ps[:, 4 + j, 0:TOK], scalar=small[:, GO + j:GO + j + 1],
                                           in1=rso, op0=ALU.mult, op1=ALU.mult).then_inc(*RV.step(f"g{j}"))
                    dve.wait_ge(*RV.upto(f"g{j}", h))
                    v.tensor_tensor(r, tmp, r, ALU.mult).then_inc(*RV.step(f"o{j}"))
                file(2)
                los(18, 24)
                file(3)
            dve.wait_ge(*OA.upto("gla_hi"))
            v.tensor_tensor(hlo[:, 8:16, :], proj[:, 40:48, :], hhi[:, 8:16, :].bitcast(F32),
                            ALU.subtract).then_inc(*OV.step("gla_lo"))

            def gated(gate, tile, psum, out, steps, n, i):
                tmp = tmp_s[:, 64 * (n % 2):64 * (n % 2) + 64]
                ts = tmp.rearrange("p (n b t) -> p n b t", n=2, b=NB)
                gs = modT[:, bass.ds(tile + gate, 2), 1:NC9].rearrange("p n (b a) -> p n b a", a=1)
                v.tensor_tensor(ts, psum[:, :, SEQ:TOK].rearrange("p n (b t) -> p n b t", t=TS),
                                gs.to_broadcast([P, 2, NB, TS]), ALU.mult).then_inc(*steps.step(f"s{n}"))
                for m in range(2):
                    v.scalar_tensor_tensor(
                        out=out(m)[:, 0:SEQ], in0=psum[:, m, 0:SEQ],
                        scalar=modT[:, bass.ds(tile + (gate + m), 1), 0:1].rearrange("p a b -> p (a b)"),
                        in1=xT[:, bass.ds(tile + m, 1), 0:SEQ].rearrange("p a c -> p (a c)"),
                        op0=ALU.mult, op1=ALU.add)
                dve.wait_ge(*steps.upto(f"s{n}", i))
                for m in range(2):
                    last = v.tensor_tensor(out(m)[:, SEQ:TOK], tmp[:, NS * m:NS * m + NS],
                                           xT[:, bass.ds(tile + m, 1), SEQ:TOK].rearrange("p a c -> p (a c)"), ALU.add)
                last.then_inc(*steps.step(f"u{n}"))

            for j in range(LEAD):
                lo(0, j, CH_OUT)
            with dve.Fori(0, 2) as i:
                for j in range(LEAD, 16 + LEAD):
                    lo(i, j, CH_OUT)
                    if j % 4 == 1:
                        u = (j - 5) // 4
                        spent(i, CH_OUT, 4 * u + 4)
                        dve.wait_ge(*UV.upto(f"u{(u + 3) % 4}", i if u else i - 1))
                        t = i * 8 + 2 * u
                        gated(2 * KD, t, ps[:, 2 * (u % 2):2 * (u % 2) + 2, :],
                              lambda m, t=t: xT[:, bass.ds(t + m, 1), :].rearrange("p a c -> p (a c)"), UV, u, i)
            norm_mean(1, 4)
            for j in range(LEAD, 4):
                lo(0, j, CH_UP)
            norm_group(1, 0)
            for j in range(4):
                if j < 3:
                    norm_group(1, j + 1)
                norm_lo(1, j)

            dve.wait_ge(*UV.upto("u3", 1))
            v.memset(gpad[:, :, 0:2], 0.0).then_inc(*FZ.step("zero"))
            dve.wait_ge(*FZ.upto("zero"))
            def up_turn(i, split):
                def los(first, end):
                    for j in range(first, end):
                        lo(i, j, CH_UP)

                w = lambda j, m: small[:, bass.ds(i * 4 + (CW + KF * j + m), 1)]

                def conv(n):
                    if n == 0:
                        dve.wait_ge(*FV.upto("hist", i))
                    dve.wait_ge(*FA.upto(f"g{n}", i))
                    if n:
                        dve.wait_ge(*FV.upto("act0", i))
                    for j, name in ((0, "a"), (1, "b"), (2, "conv")):
                        for m in range(2):
                            g = gpad[:, 2 * n + m, j:j + GW - 2]
                            if j == 0:
                                last = v.tensor_scalar(cv[:, m, :], g, w(0, 2 * n + m), w(3, 2 * n + m), ALU.mult,
                                                       ALU.add)
                            else:
                                last = v.scalar_tensor_tensor(out=cv[:, m, :], in0=g, scalar=w(j, 2 * n + m),
                                                              in1=cv[:, m, :], op0=ALU.mult, op1=ALU.add)
                        last.then_inc(*FV.step(f"{name}{n}"))
                        dve.wait_ge(*FV.upto(f"{name}{n}", i))

                def gate(n):
                    spent(i, CH_UP, 8 * n + 8)
                    dve.wait_ge(*FA.upto(f"silu{n}", i))
                    dst = actT[:, bass.ds(i * 4 + 2 * n, 2), :]
                    v.tensor_tensor(dst[:, :, 0:SEQ], ps[:, 2:4, 0:SEQ], cv[:, :, 0:SEQ], ALU.mult)
                    v.tensor_tensor(dst[:, :, SEQ:TOK].rearrange("p n (b t) -> p n b t", t=TS),
                                    ps[:, 2:4, SEQ:TOK].rearrange("p n (b t) -> p n b t", t=TS),
                                    samples_of(cv, 2 + SEQ), ALU.mult).then_inc(*FV.step(f"act{n}"))

                dve.wait_ge(*FT.upto("hist", i))
                v.tensor_copy(gpad[:, :, 2 + SEQ:GW].rearrange("p n (b t) -> p n b t", t=6)[:, :, :, 0:2],
                              ps[:, 4, 0:64].rearrange("p (n b r) -> p n b r", n=4, b=NB)).then_inc(*FV.step("hist"))
                los(split, 6)
                conv(0)
                los(6, 10)
                gate(0)
                los(10, 14)
                conv(1)
                dve.wait_ge(*FT.upto("rows", i - 1))
                v.tensor_copy(glast[:, :, 0:2], gpad[:, :, SEQ:SEQ + 2])
                v.tensor_copy(glast[:, :, 2:18].rearrange("p n (b r) -> p n b r", r=2),
                              gpad[:, :, 2 + SEQ:GW].rearrange("p n (b t) -> p n b t", t=6)[:, :, :, 4:6]
                              ).then_inc(*FV.step("last"))
                los(14, 18)
                gate(1)

            up_turn(0, 4)
            with dve.Fori(1, 11) as i:
                up_turn(i, LEAD)

            def act_parts(c, i):
                dve.wait_ge(act_hi, i * 12 + (c + 1))
                for k0, at, m in pieces(*KCH[c % 12]):
                    last = v.tensor_tensor(hlo[:, at:at + m, :], actT[:, k0:k0 + m, :],
                                           hhi[:, at:at + m, :].bitcast(F32), ALU.subtract)
                last.then_inc(act_lo, 1)

            def down_turn(i, end):
                def out(h):
                    dve.wait_ge(used, i * 24 + (CH_DOWN + BUFS + 21 + 3 * h))
                    dve.wait_ge(*DT.upto("t2", i - 1))
                    dve.wait_ge(*DV_.upto("u0" if h else "u1", i - 1 + h))
                    gated(5 * KD, i * 4 + 2 * h, ps[:, 2 * h:2 * h + 2, :], lambda m, h=h: yst[:, 2 * h + m, :],
                          DV_, h, i)

                for j in range(LEAD, end):
                    jj = j % 24
                    kg, h, kc = jj // 6, jj // 3 % 2, jj % 3
                    if j == 24:
                        out(0)
                    if h == 0:
                        act_parts(3 * kg + kc + 12 * (j // 24), i)
                    dve.wait_ge(hi_done, i * 24 + (CH_DOWN + j + 1))
                    n = 256 * KCH[3 * kg + kc][1]
                    v.tensor_tensor(wlo[:, jj % BUFS, 0:n], ring[:, (2 * kg + h) % SLOTS, CHUNK * kc:CHUNK * kc + n],
                                    whi[:, jj % BUFS, 0:n].bitcast(F32), ALU.subtract).then_inc(lo_done, 1)
                if end == 24:
                    out(0)
                out(1)

            dve.wait_ge(*FV.upto("act1", 10))
            dve.wait_ge(*FT.upto("rows", 10))
            for c in range(LEAD):
                act_parts(c, 0)
            with dve.Fori(0, 3) as i:
                down_turn(i, 24 + LEAD)
            down_turn(3, 24)


def qd_blocks(qd, h, lo):
    v = qd[h, lo:lo + 8]
    return bass.AP(v.tensor, v.offset, [list(v.ap[0]), [128, 2], [40, 4], [1, TS]])


def own_heads(ps, h, lo):
    v = ps[h, 6, lo:lo + 8]
    return bass.AP(v.tensor, v.offset, [list(v.ap[0]), [136, 4], [1, TS]])


def samples_of(cv, lo):
    v = cv[:, :, lo:lo + TS]
    part, blk = list(v.ap[0]), list(v.ap[1])
    return bass.AP(v.tensor, v.offset, [part, blk, [6, NB], [1, TS]])


_OUTS = [("y_p", (SEQ, D)), ("y_s", (NS, D)), ("new_k_p", (SEQ, 1024)), ("new_v_p", (SEQ, 1024)),
         ("new_gla_p", (H_B, DK, DV)), ("new_conv_p", (2, D_FF)), ("new_k_s", (NS, 1024)), ("new_v_s", (NS, 1024)),
         ("new_gla_s", (NB, H_B, DK, DV)), ("new_conv_s", (2 * NB, D_FF))]


def kernel(**inputs):
    import concourse.bacc as bacc
    from concourse.bass_utils import run_bass_kernel_spmd

    nc = bacc.Bacc("TRN2", target_bir_lowering=False, num_devices=1)
    tables = constants()
    arrays, a, o = {}, {}, {}
    for name, x in {**inputs, "tables": tables}.items():
        x = np.ascontiguousarray(x)
        arrays[f"in_{name}"] = x
        a[name] = nc.dram_tensor(f"in_{name}", x.shape, mybir.dt.from_np(x.dtype), kind="ExternalInput").ap()
    for name, shape in _OUTS:
        o[name] = nc.dram_tensor(f"out_{name}", shape, F32, kind="ExternalOutput").ap()
    bias_rows = nc.dram_tensor("bias_rows", [H_A, 512], F32)
    bias_full = nc.dram_tensor("bias_full", [H_A, P, SEQ], F32)
    build(nc, a, o, bias_rows, bias_full)
    r = run_bass_kernel_spmd(nc, [arrays], core_ids=[0]).results[0]
    g = {name: r[f"out_{name}"] for name, _ in _OUTS}
    return (g["y_p"].reshape(1, SEQ, D), g["y_s"].reshape(NB, TS, D),
            g["new_k_p"].reshape(1, 1, SEQ, H_A, HD), g["new_v_p"].reshape(1, 1, SEQ, H_A, HD),
            g["new_gla_p"].reshape(1, 1, H_B, DK, DV), g["new_conv_p"].reshape(1, 1, 2, D_FF),
            g["new_k_s"].reshape(1, NB, TS, H_A, HD), g["new_v_s"].reshape(1, NB, TS, H_A, HD),
            g["new_gla_s"].reshape(1, NB, H_B, DK, DV), g["new_conv_s"].reshape(1, NB, 2, D_FF))
```
